# Optimizing a Trainium2 kernel written in Bass

```python
import math
import jax, jax.numpy as jnp
from jax import lax
import numpy as np

D_MODEL = 2048
BATCH = 1
SEQ = 256
DEPTH = 1

N_Q_HEADS = 32
N_KV_HEADS = 4
GROUP = N_Q_HEADS // N_KV_HEADS
HEAD_DIM = 64
ATTN_WIDTH = N_Q_HEADS * HEAD_DIM
KV_WIDTH = N_KV_HEADS * HEAD_DIM
WINDOW = 128
BLOCK = 128
NEG_INF = -1e30
N_BUCKETS = 32
MAX_DISTANCE = 128
LRU_WIDTH = D_MODEL
LRU_BLOCKS = 16
LRU_BLOCK_W = LRU_WIDTH // LRU_BLOCKS
CONV_WIDTH = 4
LRU_C = 8.0
D_FF = 4 * D_MODEL
EPS = 1e-6
IN_SPLITS = (LRU_WIDTH, LRU_WIDTH, ATTN_WIDTH, KV_WIDTH, KV_WIDTH, D_MODEL, D_MODEL)
IN_WIDTH = sum(IN_SPLITS)


def _rms_norm(x, g):
    xf = x.astype(jnp.float32)
    y = xf * lax.rsqrt(jnp.mean(xf * xf, axis=-1, keepdims=True) + EPS)
    return (y * g.astype(jnp.float32)).astype(x.dtype)

def _modulate(h, shift, scale):
    return h * (1.0 + scale[:, None, :]) + shift[:, None, :]

def _causal_depthwise_conv(x, w, b):
    s = x.shape[1]
    xp = jnp.pad(x, ((0, 0), (CONV_WIDTH - 1, 0), (0, 0)))
    y = b
    for k in range(CONV_WIDTH):
        y = y + xp[:, k:k + s] * w[k]
    return y

def _rg_lru(x, wa, ba, wx, bx, lam):
    b_, s, w = x.shape
    xb = x.reshape(b_, s, LRU_BLOCKS, LRU_BLOCK_W)
    r = jax.nn.sigmoid(jnp.einsum("bshi,hij->bshj", xb, wa).reshape(b_, s, w) + ba)
    i = jax.nn.sigmoid(jnp.einsum("bshi,hij->bshj", xb, wx).reshape(b_, s, w) + bx)
    log_a = -LRU_C * r.astype(jnp.float32) * jax.nn.softplus(-lam.astype(jnp.float32))
    a = jnp.exp(log_a)
    mult = jnp.sqrt(-jnp.expm1(2.0 * log_a))
    mult = jnp.where(jnp.arange(s)[None, :, None] == 0, 1.0, mult)
    u = mult * (i * x).astype(jnp.float32)

    def step(h, au):
        a_t, u_t = au
        h = a_t * h + u_t
        return h, h

    h0 = jnp.zeros((b_, w), jnp.float32)
    _, hs = lax.scan(step, h0, (jnp.swapaxes(a, 0, 1), jnp.swapaxes(u, 0, 1)))
    return jnp.swapaxes(hs, 0, 1).astype(x.dtype)

def _t5_causal_bucket(rel):
    max_exact = N_BUCKETS // 2
    relf = jnp.maximum(rel, 1).astype(jnp.float32)
    large = max_exact + (jnp.log(relf / max_exact) / math.log(MAX_DISTANCE / max_exact)
                         * (N_BUCKETS - max_exact)).astype(jnp.int32)
    large = jnp.minimum(large, N_BUCKETS - 1)
    return jnp.where(rel < max_exact, rel, large)

def _band_bias_and_mask(rel_bias, n_blocks):
    qi = jnp.arange(BLOCK)[:, None]
    ki = jnp.arange(2 * BLOCK)[None, :]
    rel = qi + BLOCK - ki
    bucket = _t5_causal_bucket(jnp.maximum(rel, 0))
    bias = jnp.transpose(rel_bias[bucket], (2, 0, 1)).astype(jnp.float32)
    bias = bias.reshape(N_KV_HEADS, GROUP, BLOCK, 2 * BLOCK)
    kpos = jnp.arange(n_blocks)[:, None, None] * BLOCK - BLOCK + ki[None]
    valid = (kpos >= 0) & (rel[None] >= 0) & (rel[None] < WINDOW)
    return bias, valid

def _swa_sink_attention(q, k, v, sinks, rel_bias):
    b_, s, _ = q.shape
    n = s // BLOCK
    bias, valid = _band_bias_and_mask(rel_bias, n)
    q = q.reshape(b_, n, BLOCK, N_KV_HEADS, GROUP, HEAD_DIM)

    def band(t):
        t = t.reshape(b_, s, N_KV_HEADS, HEAD_DIM)
        tp = jnp.pad(t, ((0, 0), (BLOCK, 0), (0, 0), (0, 0)))
        tp = tp.reshape(b_, n + 1, BLOCK, N_KV_HEADS, HEAD_DIM)
        return jnp.concatenate([tp[:, :-1], tp[:, 1:]], axis=2)

    kb, vb = band(k), band(v)
    logits = jnp.einsum("bnqkgd,bnskd->bnkgqs", q, kb,
                        preferred_element_type=jnp.float32) * (HEAD_DIM ** -0.5)
    logits = jnp.where(valid[None, :, None, None], logits + bias[None, None], NEG_INF)
    sink = sinks.astype(jnp.float32).reshape(N_KV_HEADS, GROUP)[None, None, :, :, None, None]
    m = jnp.maximum(jnp.max(logits, axis=-1, keepdims=True), sink)
    e = jnp.exp(logits - m)
    p = e / (jnp.sum(e, axis=-1, keepdims=True) + jnp.exp(sink - m))
    o = jnp.einsum("bnkgqs,bnskd->bnqkgd", p.astype(vb.dtype), vb)
    return o.reshape(b_, s, ATTN_WIDTH)

def first_inputs(seed: int = 0) -> dict:
    key = jax.random.key(seed)
    ks = jax.random.split(key, 24)
    f32 = jnp.float32
    L, D = DEPTH, D_MODEL

    def nrm(k, shape, scale):
        return jax.random.normal(k, shape, f32) * scale

    a_c = jax.random.uniform(ks[12], (L, LRU_WIDTH), f32, 0.9, 0.999)
    a0 = a_c ** (1.0 / LRU_C)
    lam = jnp.log(a0) - jnp.log1p(-a0)
    return {
        "x": nrm(ks[0], (BATCH, SEQ, D), 1.0),
        "c": nrm(ks[1], (BATCH, D), 1.0),
        "w_ada": nrm(ks[2], (L, D, 6 * D), 0.5 * D ** -0.5),
        "b_ada": nrm(ks[3], (L, 6 * D), 0.02),
        "norm1_g": 1.0 + nrm(ks[4], (L, D), 0.02),
        "w_in": nrm(ks[5], (L, D, IN_WIDTH), D ** -0.5),
        "conv_w": nrm(ks[6], (L, CONV_WIDTH, LRU_WIDTH), CONV_WIDTH ** -0.5),
        "conv_b": nrm(ks[7], (L, LRU_WIDTH), 0.02),
        "lru_wa": nrm(ks[8], (L, LRU_BLOCKS, LRU_BLOCK_W, LRU_BLOCK_W), LRU_BLOCK_W ** -0.5),
        "lru_ba": nrm(ks[9], (L, LRU_WIDTH), 0.02),
        "lru_wx": nrm(ks[10], (L, LRU_BLOCKS, LRU_BLOCK_W, LRU_BLOCK_W), LRU_BLOCK_W ** -0.5),
        "lru_bx": nrm(ks[11], (L, LRU_WIDTH), 0.02),
        "lru_lambda": lam,
        "w_lru_out": nrm(ks[13], (L, LRU_WIDTH, D), LRU_WIDTH ** -0.5),
        "w_attn_out": nrm(ks[14], (L, ATTN_WIDTH, D), ATTN_WIDTH ** -0.5),
        "attn_sinks": nrm(ks[15], (L, N_Q_HEADS), 1.0),
        "rel_bias": nrm(ks[16], (N_BUCKETS, N_Q_HEADS), 0.5),
        "w_out": nrm(ks[17], (L, D, D), D ** -0.5),
        "norm2_g": 1.0 + nrm(ks[18], (L, D), 0.02),
        "w_ff1": nrm(ks[19], (L, D, D_FF), D ** -0.5),
        "w_ff2": nrm(ks[20], (L, D_FF, D), D_FF ** -0.5),
        "final_g": 1.0 + nrm(ks[21], (D,), 0.02),
    }

def first_block(x, c, w_ada, b_ada, norm1_g, w_in, conv_w, conv_b, lru_wa, lru_ba, lru_wx,
              lru_bx, lru_lambda, w_lru_out, w_attn_out, attn_sinks, rel_bias, w_out,
              norm2_g, w_ff1, w_ff2, final_g):
    split_idx = list(np.cumsum(IN_SPLITS)[:-1])
    c_act = jax.nn.silu(c)
    for l in range(DEPTH):
        mod = jnp.dot(c_act, w_ada[l]) + b_ada[l]
        shift1, scale1, gate1, shift2, scale2, gate2 = jnp.split(mod, 6, axis=-1)

        h = _modulate(_rms_norm(x, norm1_g[l]), shift1, scale1)
        proj = jnp.einsum("bsd,de->bse", h, w_in[l])
        lru_x, lru_gate, q, k, v, g_a, g_b = jnp.split(proj, split_idx, axis=-1)

        xc = _causal_depthwise_conv(lru_x, conv_w[l], conv_b[l])
        rec = _rg_lru(xc, lru_wa[l], lru_ba[l], lru_wx[l], lru_bx[l], lru_lambda[l])
        y_a = jnp.einsum("bsw,wd->bsd", rec * jax.nn.gelu(lru_gate, approximate=True),
                         w_lru_out[l])

        att = _swa_sink_attention(q, k, v, attn_sinks[l], rel_bias)
        y_b = jnp.einsum("bsw,wd->bsd", att, w_attn_out[l])

        merged = jax.nn.sigmoid(g_a) * y_a + jax.nn.sigmoid(g_b) * y_b
        x = x + gate1[:, None, :] * jnp.einsum("bsd,de->bse", merged, w_out[l])

        h2 = _modulate(_rms_norm(x, norm2_g[l]), shift2, scale2)
        ff = jnp.square(jax.nn.relu(jnp.einsum("bsd,df->bsf", h2, w_ff1[l])))
        x = x + gate2[:, None, :] * jnp.einsum("bsf,fd->bsd", ff, w_ff2[l])

    return _rms_norm(x, final_g)


DEPTH_2 = 2

HEAD_DIM_2 = 128
H_FOX = 6
H_DSA = 6
H_MEM = 4
D_FOX = H_FOX * HEAD_DIM_2
D_DSA = H_DSA * HEAD_DIM_2
D_MEMG = H_MEM * HEAD_DIM_2
D_MIX = D_FOX + D_DSA + D_MEMG
IDX_HEADS = 16
IDX_DIM = 64
INDEX_TOPK = 256
N_MEM = 256
Q_BLOCK = 128
ROPE_THETA = 10000.0
LN_EPS = 1e-5
ALPHA = (2 * DEPTH_2) ** 0.25
BETA = (8 * DEPTH_2) ** -0.25
NEG = -1e30

SPLITS = (
    D_FOX, D_FOX, D_FOX, D_FOX, H_FOX,
    D_DSA, D_DSA, D_DSA, D_DSA,
    IDX_HEADS * IDX_DIM, IDX_DIM, IDX_HEADS,
    D_MEMG, D_MEMG,
)
N_IN = sum(SPLITS)


def rope(x, pos):
    d = x.shape[-1]
    half = d // 2
    inv_freq = ROPE_THETA ** (-jnp.arange(half, dtype=jnp.float32) / half)
    ang = pos.astype(jnp.float32)[:, None] * inv_freq[None, :]
    cos = jnp.cos(ang)[None, :, None, :].astype(x.dtype)
    sin = jnp.sin(ang)[None, :, None, :].astype(x.dtype)
    x1, x2 = x[..., :half], x[..., half:]
    return jnp.concatenate([x1 * cos - x2 * sin, x2 * cos + x1 * sin], axis=-1)

def to_blocks(a):
    b, s = a.shape[0], a.shape[1]
    return jnp.moveaxis(a.reshape(b, s // Q_BLOCK, Q_BLOCK, *a.shape[2:]), 1, 0)

def from_blocks(a):
    a = jnp.moveaxis(a, 0, 1)
    return a.reshape(a.shape[0], a.shape[1] * a.shape[2], *a.shape[3:])

def fox_attention(q, k, v, cum_logf):
    b, s, h, d = q.shape
    scale = d ** -0.5
    key_pos = jnp.arange(s)
    c_keys = jnp.transpose(cum_logf, (0, 2, 1))
    q_pos = key_pos.reshape(s // Q_BLOCK, Q_BLOCK)

    def one_block(args):
        qb, cb, tb = args
        sc = jnp.einsum('bqhd,bkhd->bhqk', qb, k).astype(jnp.float32) * scale
        sc = sc + (jnp.transpose(cb, (0, 2, 1))[:, :, :, None] - c_keys[:, :, None, :])
        causal = tb[:, None] >= key_pos[None, :]
        sc = jnp.where(causal[None, None], sc, NEG)
        p = jax.nn.softmax(sc, axis=-1).astype(v.dtype)
        return jnp.einsum('bhqk,bkhd->bqhd', p, v)

    out = lax.map(one_block, (to_blocks(q), to_blocks(cum_logf), q_pos))
    return from_blocks(out)

def dsa_attention(q, k, v, q_idx, k_idx, w_idx):
    b, s, h, d = q.shape
    topk = min(INDEX_TOPK, s // 4)
    scale = d ** -0.5
    idx_scale = IDX_DIM ** -0.5
    key_pos = jnp.arange(s)
    q_pos = key_pos.reshape(s // Q_BLOCK, Q_BLOCK)

    def one_block(args):
        qb, qib, wb, tb = args
        rel = jax.nn.relu(jnp.einsum('bqhi,bki->bqhk', qib, k_idx).astype(jnp.float32) * idx_scale)
        score = jnp.einsum('bqhk,bqh->bqk', rel, wb.astype(jnp.float32))
        causal = tb[:, None] >= key_pos[None, :]
        score = jnp.where(causal[None], score, NEG)
        _, sel = lax.top_k(score, topk)
        valid = sel <= tb[None, :, None]
        kg = jax.vmap(lambda kk, ii: kk[ii])(k, sel)
        vg = jax.vmap(lambda vv, ii: vv[ii])(v, sel)
        sc = jnp.einsum('bqhd,bqkhd->bhqk', qb, kg).astype(jnp.float32) * scale
        sc = jnp.where(jnp.transpose(valid, (0, 1, 2))[:, None], sc, NEG)
        p = jax.nn.softmax(sc, axis=-1).astype(vg.dtype)
        return jnp.einsum('bhqk,bqkhd->bqhd', p, vg)

    out = lax.map(one_block, (to_blocks(q), to_blocks(q_idx), to_blocks(w_idx), q_pos))
    return from_blocks(out)

def memory_attention(q, k_mem, v_mem):
    scale = q.shape[-1] ** -0.5
    sc = jnp.einsum('bshd,bmhd->bhsm', q, k_mem).astype(jnp.float32) * scale
    p = jax.nn.softmax(sc, axis=-1).astype(v_mem.dtype)
    return jnp.einsum('bhsm,bmhd->bshd', p, v_mem)

def layer_norm(z, g, b):
    zf = z.astype(jnp.float32)
    mu = jnp.mean(zf, axis=-1, keepdims=True)
    var = jnp.mean(jnp.square(zf - mu), axis=-1, keepdims=True)
    out = (zf - mu) * lax.rsqrt(var + LN_EPS) * g.astype(jnp.float32) + b.astype(jnp.float32)
    return out.astype(z.dtype)

def hybrid_layer(x, mem, w_in, b_forget, w_mem_kv, w_out, ln_gain, ln_bias):
    b, s, _ = x.shape
    pos = jnp.arange(s)
    h = jnp.einsum('bsd,dn->bsn', x, w_in)
    offsets = np.cumsum(SPLITS)[:-1].tolist()
    (fq, fk, fv, fg, f_logit,
     dq, dk, dv, dg,
     iq, ik, iw,
     mq, mg) = jnp.split(h, offsets, axis=-1)

    heads = lambda t, nh: t.reshape(b, s, nh, HEAD_DIM_2)

    log_f = jax.nn.log_sigmoid(f_logit.astype(jnp.float32) + b_forget.astype(jnp.float32))
    cum_logf = jnp.cumsum(log_f, axis=1)
    y_fox = fox_attention(heads(fq, H_FOX), heads(fk, H_FOX), heads(fv, H_FOX), cum_logf)
    y_fox = y_fox.reshape(b, s, D_FOX) * jax.nn.silu(fg)

    q_idx = rope(iq.reshape(b, s, IDX_HEADS, IDX_DIM), pos)
    k_idx = rope(ik.reshape(b, s, 1, IDX_DIM), pos)[:, :, 0, :]
    w_idx = iw * (IDX_HEADS ** -0.5)
    y_dsa = dsa_attention(rope(heads(dq, H_DSA), pos), rope(heads(dk, H_DSA), pos), heads(dv, H_DSA),
                          q_idx, k_idx, w_idx)
    y_dsa = y_dsa.reshape(b, s, D_DSA) * jax.nn.silu(dg)

    kv = jnp.einsum('bmd,dn->bmn', mem, w_mem_kv)
    k_mem, v_mem = jnp.split(kv, 2, axis=-1)
    m = mem.shape[1]
    y_mem = memory_attention(heads(mq, H_MEM), k_mem.reshape(b, m, H_MEM, HEAD_DIM_2),
                             v_mem.reshape(b, m, H_MEM, HEAD_DIM_2))
    y_mem = y_mem.reshape(b, s, D_MEMG) * jax.nn.silu(mg)

    y = jnp.concatenate([y_fox, y_dsa, y_mem], axis=-1)
    y = jnp.einsum('bsn,nd->bsd', y, w_out)
    return layer_norm(ALPHA * x + y, ln_gain, ln_bias)

def second_inputs(seed: int = 0) -> dict:
    key = jax.random.key(seed)
    ks = jax.random.split(key, 8)
    x = jax.random.normal(ks[0], (BATCH, SEQ, D_MODEL), jnp.float32)
    mem = jax.random.normal(ks[1], (BATCH, N_MEM, D_MODEL), jnp.float32)
    w_in = jax.random.normal(ks[2], (DEPTH_2, D_MODEL, N_IN), jnp.float32) * D_MODEL ** -0.5
    b_forget = 3.0 + 0.5 * jax.random.normal(ks[3], (DEPTH_2, H_FOX), jnp.float32)
    w_mem_kv = jax.random.normal(ks[4], (DEPTH_2, D_MODEL, 2 * D_MEMG), jnp.float32) * D_MODEL ** -0.5
    w_out = jax.random.normal(ks[5], (DEPTH_2, D_MIX, D_MODEL), jnp.float32) * (D_MIX ** -0.5) * BETA
    ln_gain = 1.0 + 0.05 * jax.random.normal(ks[6], (DEPTH_2, D_MODEL), jnp.float32)
    ln_bias = 0.02 * jax.random.normal(ks[7], (DEPTH_2, D_MODEL), jnp.float32)
    return {"x": x, "mem": mem, "w_in": w_in, "b_forget": b_forget, "w_mem_kv": w_mem_kv,
            "w_out": w_out, "ln_gain": ln_gain, "ln_bias": ln_bias}

def second_block(x, mem, w_in, b_forget, w_mem_kv, w_out, ln_gain, ln_bias):
    h = x
    for l in range(DEPTH_2):
        h = hybrid_layer(h, mem, w_in[l], b_forget[l], w_mem_kv[l], w_out[l], ln_gain[l], ln_bias[l])
    return h


def setup_inputs(seed=0):
    out = dict(first_inputs(seed))
    for name, value in second_inputs(seed + 1).items():
        if name != "x":
            out[name + "_2"] = value
    return out


def reference(
    x, c, w_ada, b_ada, norm1_g, w_in, conv_w, conv_b, lru_wa, lru_ba, lru_wx, lru_bx,
    lru_lambda, w_lru_out, w_attn_out, attn_sinks, rel_bias, w_out, norm2_g, w_ff1, w_ff2,
    final_g, mem_2, w_in_2, b_forget_2, w_mem_kv_2, w_out_2, ln_gain_2, ln_bias_2,
):
    x = first_block(
        x, c, w_ada, b_ada, norm1_g, w_in, conv_w, conv_b, lru_wa, lru_ba, lru_wx, lru_bx,
        lru_lambda, w_lru_out, w_attn_out, attn_sinks, rel_bias, w_out, norm2_g, w_ff1, w_ff2,
        final_g,
    )
    return second_block(
        x, mem_2, w_in_2, b_forget_2, w_mem_kv_2, w_out_2, ln_gain_2, ln_bias_2,
    )


_drawn_inputs = setup_inputs


def setup_inputs(seed=0):
    import zlib

    import numpy as np

    out = dict(_drawn_inputs(seed))
    spreads = {}
    factors = {'norm1_g': 8.0,
     'conv_b': 5.41,
     'lru_wa': 2.68,
     'lru_ba': 8.0,
     'lru_bx': 8.0,
     'attn_sinks': 8.0,
     'rel_bias': 3.42,
     'norm2_g': 5.761,
     'final_g': 2.689,
     'mem_2': 3.666,
     'b_forget_2': 40.752,
     'w_mem_kv_2': 3.523}
    for name, (base, spread) in spreads.items():
        noise = np.random.default_rng([zlib.crc32(name.encode()), seed]).standard_normal(out[name].shape)
        drawn = base * np.exp(spread * noise) if base else spread * noise
        out[name] = __import__('jax').numpy.asarray(drawn.astype(out[name].dtype))
    for name, factor in factors.items():
        out[name] = (out[name] * factor).astype(out[name].dtype)
    return out
```

```python
from collections import deque
from contextlib import ExitStack

import numpy as np

import concourse.bass as bass
from concourse import mybir

F32 = mybir.dt.float32
F32R = mybir.dt.float32r
ALU = mybir.AluOpType
ACT = mybir.ActivationFunctionType
AX = mybir.AxisListType

D = 2048
S = 256
NB = D // 128
EPS = 1e-6
LN_EPS = 1e-5
ALPHA = 4 ** 0.25
NEG = -1e30
TAKEN = -3e38
SC1 = 64 ** -0.5
SC2 = 128 ** -0.5

V_N1, V_CW, V_CB, V_BA, V_BX, V_LAM, V_N2, V_FG = 0, 16, 80, 96, 112, 128, 144, 160
V_LNG, V_LNB, V_C, V_ADA, V_SINK, V_BF = 176, 208, 240, 256, 352, 384
V_END = 396
C_ONE, C_ID, C_P64, C_P128, C_U = 0, 128, 256, 384, 512
C_COS128, C_SIN128, C_COS64, C_SIN64, C_END = 768, 1024, 1280, 1536, 1792

CH = 1024
NRAW = 5
NSP = 4
AHEAD = NSP - 1
SPAN = 2


def build(nc, d_x, d_mem, d_vec, d_cst, d_hot, d_relb, d_ada, d_lru, d_w, d_s2, d_out):
    ctx = ExitStack()
    with ctx:
        cur = [16512]

        def place(nbytes):
            at = cur[0]
            cur[0] += nbytes
            return at

        def at(name, shape, off, dt=F32):
            return nc.alloc_sbuf_tensor_at(name, shape, dt, offset=off)

        o_raw = place(NRAW * CH * 4)
        o_hi = place(NSP * CH * 4)
        o_lo = place(NSP * CH * 4)
        raw = [at(f"raw{i}", [128, CH], o_raw + i * CH * 4) for i in range(NRAW)]
        whi = at("whi", [128, NSP, CH], o_hi, F32R)
        wlo = at("wlo", [128, NSP, CH], o_lo, F32R)
        RES = at("RES", [128, NB, S], place(NB * S * 4))
        o_h = place(2 * NB * S * 4)
        Hhi = at("Hhi", [128, NB, S], o_h, F32R)
        Hlo = at("Hlo", [128, NB, S], o_h + 16384, F32R)
        o_a = place(4 * 16384)
        o_acc = place(4096)
        o_kv = place(8192)
        KM = at("KM", [128, 4, S], o_kv)
        VM = at("VM", [128, 2, 512], o_kv + 4096)
        cst = at("cst", [128, C_END], place(C_END * 4))
        vec = at("vec", [128, V_END], place(1600))
        mod = at("mod", [128, 96], place(384))
        A1v = at("A1v", [128, NB], place(64))
        A2v = at("A2v", [128, NB], place(64))
        o_lp = place(3 * 2048)
        o_pt = place(2 * 2048)
        o_bt = place(2 * 2048)
        o_tg = place(4 * 2048)
        o_sm = place(384)
        assert cur[0] <= 229344, cur[0]
        LP = at("LP", [128, 3, 2, S], o_lp)
        PT = at("PT", [128, 2, 4, 128], o_pt)
        BT = at("BT", [128, 2, 2, S], o_bt)
        TG = at("TG", [128, 4, 512], o_tg)
        SM = at("SM", [128, 4, 6, 2], o_sm)
        MX8 = at("MX8", [128, 8], o_sm + 192)
        ones = cst[:, C_ONE:C_ONE + 128]
        ident = cst[:, C_ID:C_ID + 128]
        U = cst[:, C_U:C_U + 256]

        acc = at("acc", [128, CH], o_acc)
        AT = at("AT", [128, NB, S], o_a)
        XC = at("XC", [128, NB, S], o_a + 16384)
        AA = at("AA", [128, NB, S], o_a + 32768)
        MM = at("MM", [128, NB, S], o_a + 49152)
        Zh = at("Zh", [128, NB, S], o_a + 16384, F32R)
        Zl = at("Zl", [128, NB, S], o_a + 32768, F32R)
        KT = at("KT", [128, 2, S], o_kv)
        VT = at("VT", [128, 2, 256], o_kv + 2048)
        Mh0 = at("Mh0", [128, NB, S], o_a + 16384, F32R)
        Ml0 = at("Ml0", [128, NB, S], o_a + 49152, F32R)
        Fh = [at(f"Fh{i}", [128, 8, S], o_a + 32768 * i, F32R) for i in range(2)]
        Fl = [at(f"Fl{i}", [128, 8, S], o_a + 32768 * i + 8192, F32R) for i in range(2)]
        DQ = at("DQ", [128, 6, S], o_a)
        DK = at("DK", [128, 6, S], o_a + 6144)
        DV = at("DV", [128, 2, 768], o_a + 12288)
        FQ = at("FQ", [128, 6, S], o_a + 18432)
        FK = at("FK", [128, 6, S], o_a + 24576)
        FV = at("FV", [128, 2, 768], o_a + 30720)
        MQ = at("MQ", [128, 4, S], o_a + 36864)
        IQ = at("IQ", [128, 8, S], o_a + 40960)
        Y = at("Y", [128, NB, S], o_a + 49152)
        Yh = at("Yh", [128, NB, S], o_a + 49152, F32R)
        Yl = at("Yl", [128, NB, S], o_a, F32R)
        Mh1 = at("Mh1", [128, NB, S], o_a + 16384, F32R)
        Ml1 = at("Ml1", [128, NB, S], o_a + 32768, F32R)
        IK = at("IK", [128, S], o_acc)
        SC = at("SC", [128, 384], o_acc + 1024)
        TK = at("TK", [128, 2, 22], o_acc + 2560)
        LF = at("LF", [128, 2, 6], o_acc + 2752)
        CQ = at("CQ", [128, 2, 6], o_acc + 2816)
        SMALL = at("SMALL", [128, 6, 16], o_acc + 2880)
        hot = at("hot", [32, 384], o_tg)
        relb = at("relb", [32, 32], o_tg + 1536)
        gsb = at("gsb", [32, 384], o_tg + 2048)
        LPS = at("LPS", [128, 8, 16], o_lp)
        CS = at("CS", [128, NB], o_sm + 256)
        SP4 = at("SP4", [128, NB], o_sm + 320)

        bank = [nc.alloc_psum_tensor(f"bank{i}", [128, 512], F32) for i in range(3)]
        pS2 = nc.alloc_psum_tensor("pS2", [128, 2, 512], F32)
        pS = pS2[:, 0, :]
        pT, pO, pM = (nc.alloc_psum_tensor(f"p{i}", [128, 512], F32) for i in "TOM")
        gdram = nc.dram_tensor("gtab", (32, 384), F32, kind="Internal").ap()

        prog = {e: [] for e in ("pe", "act", "dve", "pool", "sp")}
        sems = {e: ctx.enter_context(nc.semaphore(f"s_{e}")) for e in ("pe", "act", "dve", "pool")}
        names = {id(s): e for e, s in sems.items()}
        count = {}
        reached = {}

        def dma_sem(name):
            return ctx.enter_context(nc.semaphore(name))

        def signal(sem, by):
            count[id(sem)] = count.get(id(sem), 0) + by
            return sem, count[id(sem)]

        def wait(e, toks):
            for sem, v in toks:
                if reached.get((e, id(sem)), 0) < v:
                    reached[(e, id(sem))] = v
                    prog[e].append(lambda eng, sem=sem, v=v: eng.wait_ge(sem, v))

        def op(e, fn, *toks):
            wait(e, toks)
            sem = sems[e]
            tok = signal(sem, 1)
            prog[e].append(lambda eng: fn(eng).then_inc(sem, 1))
            if e == "pe":
                st["pe"] = tok
            return tok

        def quiet(e, fn, *toks):
            wait(e, toks)
            prog[e].append(fn)

        def dma(e, out, in_, sem, *toks):
            wait(e, toks)
            tok = signal(sem, 16)
            prog[e].append(lambda eng: eng.dma_start(out, in_).then_inc(sem, 16))
            return tok

        def tt(e, out, a, b, o, *toks):
            return op(e, lambda g: g.tensor_tensor(out, a, b, o), *toks)

        def ts(e, out, a, s1, o1, s2, o2, *toks):
            if o2 is None:
                return op(e, lambda g: g.tensor_scalar(out, a, s1, None, o1), *toks)
            return op(e, lambda g: g.tensor_scalar(out, a, s1, s2, o1, o2), *toks)

        def stt(out, a, s, b, o0, o1, *toks):
            return op("dve", lambda g: g.scalar_tensor_tensor(out=out, in0=a, scalar=s, in1=b, op0=o0, op1=o1), *toks)

        def act(out, in_, f, *toks, **kw):
            return op("act", lambda g: g.activation(out, in_, f, **kw), *toks)

        def over(ap, n):
            a = list(ap.ap)
            return bass.AP(tensor=ap.tensor, offset=ap.offset, ap=[list(a[0]), [0, n]] + [list(z) for z in a[1:]])

        def spread(ap, n):
            return bass.AP(tensor=ap.tensor, offset=ap.offset, ap=[list(ap.ap[0]), [0, n]])

        def mirrored(ap):
            a = [list(z) for z in ap.ap]
            step, n = a[-1]
            return bass.AP(tensor=ap.tensor, offset=ap.offset + step * (n - 1), ap=a[:-1] + [[-step, n]])

        def v32(ap):
            return ap.bitcast(F32)

        stream = []
        s_raw = [dma_sem(f"s_raw{i}") for i in range(NRAW)]
        raw_free = [[] for _ in range(NRAW)]
        sp_free = [[] for _ in range(NSP)]
        landed = {}
        st = {"dma": 0, "split": 0, "w": 0, "main": 0, "tick": 0, "pe": None}
        ready = {}
        acc_free = [None]
        modtok = {}

        released = set()

        def pump():
            while st["dma"] < len(stream) and (st["dma"] < NRAW or st["dma"] - NRAW in released):
                i = st["dma"]
                r = i % NRAW
                n = stream[i]["n"]
                landed[i] = dma("sp", raw[r][:, 0:n], stream[i]["src"], s_raw[r], *raw_free[r])
                st["dma"] += 1

        def release(i, toks):
            raw_free[i % NRAW] = toks
            released.add(i)
            pump()

        def push_split():
            i = st["split"]
            el = stream[i]
            r = i % NRAW
            assert i in landed
            kind = el["kind"]
            if kind == "w":
                s = el["slot"]
                n = el["n"]
                th = act(whi[:, s, 0:n], raw[r][:, 0:n], ACT.Copy, landed[i], *sp_free[s])
                tl = tt("dve", wlo[:, s, 0:n], raw[r][:, 0:n], v32(whi[:, s, 0:n]), ALU.subtract, landed[i], th, *sp_free[s])
                ready[i] = [th, tl]
                release(i, [th, tl])
            elif kind == "ada":
                g, kt = el["g"], el["kt"]
                cs = CS[:, kt:kt + 1]
                if kt == 0:
                    t = ts("dve", acc[:, :], raw[r][:, :], cs, ALU.mult, None, None, landed[i], t_cs,
                           *([acc_free[0]] if acc_free[0] else []))
                else:
                    t = stt(acc[:, :], raw[r][:, :], cs, acc[:, :], ALU.mult, ALU.add, landed[i], ada_last[0])
                ada_last[0] = t
                release(i, [t])
                if kt == NB - 1:
                    def fold(g=g, t=t):
                        for j in range(8):
                            o, w = pM[:, j:j + 1], acc[:, j * 128:(j + 1) * 128]
                            f = lambda e, o=o, w=w: e.matmul(o, w, ones[:, 0:1], start=True, stop=True)
                            if j < 7:
                                quiet("pe", f, t, t_cst, *free["M"])
                            else:
                                tp = op("pe", f, t)
                        tm = tt("dve", mod[:, 8 * g:8 * g + 8], pM[:, 0:8], vec[:, V_ADA + 8 * g:V_ADA + 8 * g + 8],
                                ALU.add, tp, t_vec)
                        free["M"] = [tm]
                        acc_free[0] = tp
                        modtok[g] = tm
                    fold()
            elif kind == "mem":
                q = el["q"]
                mh, ml = el["dst"]
                src = raw[r][:, :].rearrange("p (b s) -> p b s", b=4)
                wt = el["after"]()
                th = act(mh[:, 4 * q:4 * q + 4, :], src, ACT.Copy, landed[i], *wt)
                tl = tt("dve", ml[:, 4 * q:4 * q + 4, :], src, v32(mh[:, 4 * q:4 * q + 4, :]), ALU.subtract, landed[i], th, *wt)
                release(i, [th, tl])
                el["done"][q] = [th, tl]
            st["split"] += 1

        def ensure(i):
            while st["split"] <= i and st["split"] < len(stream):
                push_split()

        jobs = deque()
        flight = []
        later = []

        def advance():
            for j in list(flight):
                j["steps"][j["at"]]()
                j["at"] += 1
                if j["at"] == len(j["steps"]):
                    flight.remove(j)
            if jobs:
                j = {"steps": jobs.popleft(), "at": 0}
                j["steps"][0]()
                j["at"] = 1
                if j["at"] < len(j["steps"]):
                    flight.append(j)

        def tick():
            st["tick"] += 1
            due = [x for x in later if x[0] <= st["tick"]]
            for x in due:
                later.remove(x)
                x[1]()
            if st["tick"] % SPAN == 0:
                advance()

        def flush_later():
            while later:
                later.sort(key=lambda x: x[0])
                later.pop(0)[1]()

        def drain_jobs():
            while jobs or flight:
                advance()

        def defer(n, fn):
            later.append((st["tick"] + n, fn))

        free = {k: [] for k in ("S", "T", "O", "M", "TG0", "TG1", "TG2", "TG3", "BT0", "BT1", "PT0", "PT1",
                                "LP0", "LP1", "LP2", "SM0", "SM1", "SM2", "SM3")}
        main_free = [[] for _ in range(3)]

        steps = []

        def unit(src, u, nkc, xact, evac, mode="f", kt0=0, width=256, kc0=0):
            steps.append(("unit", dict(src=src, u=u, nkc=nkc, x=xact, evac=evac, mode=mode, kt0=kt0, width=width, kc0=kc0)))

        def call(fn):
            steps.append(("call", fn))

        def run_unit(s):
            b = st["main"] % 3
            st["main"] += 1
            ps = bank[b]
            x = s["x"]()
            wait("pe", main_free[b])
            first = True
            width = s["width"]
            last = None
            for c in range(s["nkc"]):
                i = s["ids"][c]
                el = stream[i]
                ensure(s["ahead"][c])
                wait("pe", ready[i])
                slot = el["slot"]
                mms = []
                for k in range(4):
                    kt = s["kt0"] + 4 * c + k
                    for t in x["toks"][kt]:
                        mms.append(("w", t))
                    w0 = k * width

                    def feat(col, o, kt=kt, w0=w0):
                        h, l = whi[:, slot, w0 + col:w0 + col + 128], wlo[:, slot, w0 + col:w0 + col + 128]
                        xh, xl = x["hi"][:, kt, :], x["lo"][:, kt, :]
                        mms.extend([("m", o, h, xh), ("m", o, h, xl), ("m", o, l, xh)])

                    def toks(col, n, stride, off, kt=kt, w0=w0):
                        h, l = whi[:, slot, w0 + col:w0 + col + n], wlo[:, slot, w0 + col:w0 + col + n]
                        for t in range(2):
                            o = ps[:, off + t * stride:off + t * stride + n]
                            xh = x["hi"][:, kt, t * 128:(t + 1) * 128]
                            xl = x["lo"][:, kt, t * 128:(t + 1) * 128]
                            mms.extend([("m", o, xh, h), ("m", o, xh, l), ("m", o, xl, h)])

                    if s["mode"] == "f":
                        feat(0, ps[:, 0:256])
                        feat(128, ps[:, 256:512])
                    elif s["mode"] == "t":
                        toks(0, 256, 256, 0)
                    else:
                        feat(0, ps[:, 0:256])
                        toks(128, 22, 32, 256)
                endm = max(j for j, m in enumerate(mms) if m[0] == "m")
                for j, m in enumerate(mms):
                    if m[0] == "w":
                        wait("pe", [m[1]])
                        continue
                    fn = lambda e, m=m, f=first, z=(c == s["nkc"] - 1 and j == endm): e.matmul(
                        m[1], m[2], m[3], start=f, stop=z, skip_group_check=True)
                    first = False
                    if j == endm:
                        last = op("pe", fn)
                    else:
                        quiet("pe", fn)
                sp_free[slot] = [last]
                if c < s["nkc"] - 1:
                    tick()
            main_free[b] = s["evac"](ps, last)
            tick()

        s_in = dma_sem("s_in")
        s_in2 = dma_sem("s_in2")
        s_hot = dma_sem("s_hot")
        s_g = dma_sem("s_g")
        t_vec = dma("pool", vec[:, :], d_vec, s_in)
        t_cst = dma("pool", cst[:, :], d_cst, s_in2)
        dma("pool", hot[:, :], d_hot, s_hot)
        t_hot = dma("pool", relb[:, :], d_relb, s_hot)
        s_x = dma_sem("s_x")
        t_x = dma("pool", RES[:, :, :], d_x, s_x)
        ada_last = [None]

        def v(c, n=1):
            return vec[:, c:c + n]

        t0 = act(LPS[:, 0, :], v(V_C, 16), ACT.Tanh, t_vec, scale=0.5)
        t0 = stt(LPS[:, 1, :], LPS[:, 0, :], 1.0, v(V_C, 16), ALU.add, ALU.mult, t0)
        t_cs = ts("dve", CS[:, :], LPS[:, 1, :], 0.5, ALU.mult, None, None, t0)

        def log1p_exp(tmp, z_abs, n, tz):
            e, d, s, q, p = (tmp(i) for i in range(5))
            t = act(e, z_abs, ACT.Exp, tz, scale=-1.0)
            t = ts("dve", d, e, 2.0, ALU.add, None, None, t)
            t = op("dve", lambda g: g.reciprocal(d, d), t)
            t = tt("dve", s, e, d, ALU.mult, t)
            t = tt("dve", q, s, s, ALU.mult, t)
            t = ts("dve", p, q, 1.0 / 17, ALU.mult, None, None, t)
            for k in (15, 13, 11, 9, 7, 5, 3):
                t = stt(p, p, 1.0 / k, q, ALU.add, ALU.mult, t)
            t = stt(p, p, 1.0, s, ALU.add, ALU.mult, t)
            return p, t

        t1 = stt(LPS[:, 2, :], v(V_LAM, 16), -1.0, v(V_LAM, 16), ALU.mult, ALU.max, t_vec)
        p, t1 = log1p_exp(lambda i: LPS[:, 3 + i, :], LPS[:, 2, :], 16, t1)
        t2 = ts("dve", LPS[:, 2, :], v(V_LAM, 16), -1.0, ALU.mult, 0.0, ALU.max, t1)
        t2 = stt(LPS[:, 3, :], p, 2.0, LPS[:, 2, :], ALU.mult, ALU.add, t2)
        t_sp = ts("dve", SP4[:, :], LPS[:, 3, :], -4.0, ALU.mult, None, None, t2)
        t_half = ts("dve", vec[:, V_BA:V_BA + 32], vec[:, V_BA:V_BA + 32], 0.5, ALU.mult, None, None, t_vec)

        tg = op("pe", lambda e: e.matmul(pT[0:32, 0:384], relb[:, :], hot[:, :], start=True, stop=True), t_hot)
        tg = op("dve", lambda e: e.tensor_copy(gsb[:, :], pT[0:32, 0:384]), tg)
        tga = op("pool", lambda e: e.memset(gsb[:, 0:128], NEG), tg)
        tgb = op("pool", lambda e: e.memset(gsb[:, 256:384], NEG), tg)
        free["T"] = [tg]
        t_g = dma("pool", gdram, gsb[:, :], s_g, tga, tgb)
        free["TG0"] = free["TG1"] = [t_g]

        def stat_sq(j, src, tok):
            k = j % 2
            tq = act(TG[:, k, :], src, ACT.Square, tok, *free[f"TG{k}"])

            def mm():
                stat_mm(j, TG[:, k, :], tq)
                free[f"TG{k}"] = [st["stat"]]
            return mm

        def stat_mm(j, src, tq):
            wt = free["S"] if j == 0 else []
            quiet("pe", lambda e: e.matmul(pS[:, 0:256], ones, src[:, 0:256], start=(j == 0), stop=False,
                                           skip_group_check=True), tq, t_cst, *wt)
            st["stat"] = op("pe", lambda e: e.matmul(pS[:, 0:256], ones, src[:, 256:512], start=False, stop=(j == 7),
                                                     skip_group_check=True), tq)

        def pair(t, j):
            return t[:, 2 * j:2 * j + 2, :].rearrange("p b s -> p (b s)")

        Rv, R2, R3, R4 = (BT[:, 0, 0, :], BT[:, 0, 1, :], BT[:, 1, 0, :], BT[:, 1, 1, :])

        def rstd(eps):
            w = free["BT0"] + free["BT1"]
            t = ts("dve", R2, pS[:, 0:256], 1.0 / D, ALU.mult, eps, ALU.add, st["stat"], *w)
            free["S"] = [t]
            t = op("dve", lambda g: g.reciprocal(R3, R2), t)
            t = act(R4, R3, ACT.Sqrt, t)
            t = tt("dve", R3, R4, R4, ALU.mult, t)
            t = tt("dve", R3, R3, R2, ALU.mult, t)
            t = ts("dve", R3, R3, -0.5, ALU.mult, 1.5, ALU.add, t)
            t = tt("dve", Rv, R4, R3, ALU.mult, t)
            free["BT0"] = free["BT1"] = []
            return t

        hact = {"hi": Hhi, "lo": Hlo, "toks": [[] for _ in range(NB)]}
        restok = [[] for _ in range(NB)]

        def tslot(b):
            k = 2 + (b // 2) % 2
            return TG[:, k, (b % 2) * 256:(b % 2) * 256 + 256], f"TG{k}{b % 2}"

        tfree = {}

        def emit_h(b, kind, tr, g, sh, last_read, tmod=()):
            wh = [last_read] if last_read else []
            hi, lo, r = Hhi[:, b, :], Hlo[:, b, :], RES[:, b, :]
            if kind == "rms":
                t = stt(r, r, g, Rv, ALU.mult, ALU.mult, tr, t_vec, *restok[b])
                restok[b] = [t]
                th = act(hi, r, ACT.Copy, t, *wh)
                tl = tt("dve", lo, r, v32(hi), ALU.subtract, th, t, *wh)
                hact["toks"][b] = [th, tl]
                restok[b] = [t]
                return [t, th, tl]
            sl, key = tslot(b)
            w = tfree.get(key, free["TG2"] + free["TG3"])
            t = stt(sl, r, g, Rv, ALU.mult, ALU.mult, tr, t_vec, *tmod, *w, *restok[b])
            out = []
            if kind in ("ln", "out"):
                tx = act(r, sl, ACT.Identity, t, bias=sh)
                restok[b] = [tx]
                out.append(tx)
            if kind == "out":
                tfree[key] = [tx]
                return out
            th = act(hi, sl, ACT.Identity, t, *wh, bias=sh)
            tl = stt(lo, sl, sh, v32(hi), ALU.add, ALU.subtract, t, th, *wh)
            tfree[key] = [th, tl]
            hact["toks"][b] = [th, tl]
            return out + [t, th, tl]

        PERM = []
        for b in range(16):
            PERM.append((b, 8 + b) if b < 8 else (8 + b, 16 + b))

        w_in, w_lo, w_ao, w_o, w_f1, w_f2 = (d_w[k] for k in ("in", "lru_out", "attn_out", "out", "ff1", "ff2"))

        def x_first():
            for j in range(8):
                stat_sq(j, pair(RES, j), t_x)()
        call(x_first)

        def norm1():
            tr = rstd(EPS)
            t = stt(A1v[:, :], mod[:, 16:32], 1.0, v(V_N1, 16), ALU.add, ALU.mult, modtok[2], modtok[3], t_vec)
            for b in range(NB):
                restok[b] = [t_x]
                emit_h(b, "mod", tr, A1v[:, b:b + 1], mod[:, b:b + 1], None, tmod=[t, modtok[0], modtok[1]])
            for k in (2, 3):
                free[f"TG{k}"] = tfree[f"TG{k}0"] + tfree[f"TG{k}1"]
            tfree.clear()
            st["norm_done"] = hact["toks"][NB - 1]
        call(norm1)

        xctok = [[] for _ in range(NB)]

        def evac_lrux(j):
            def f(ps, tp):
                out = []
                for i in range(2):
                    b = 2 * j + i
                    o = XC[:, b, :]
                    p_ = ps[:, i * 256:(i + 1) * 256]
                    t = ts("dve", o, p_, v(V_CW + 48 + b), ALU.mult, v(V_CB + b), ALU.add, tp, t_vec)
                    for k in (2, 1, 0):
                        s = 3 - k
                        t = stt(o[:, s:S], p_[:, 0:S - s], v(V_CW + 16 * k + b), o[:, s:S], ALU.mult, ALU.add, t)
                    xctok[b] = [t]
                    out.append(t)
                return [out[-1]]
            return f

        def X():
            return hact
        for j in range(8):
            unit(w_in, j, 4, X, evac_lrux(j))

        qtok = [[] for _ in range(NB)]

        def evac_q(j):
            def f(ps, tp):
                src = mirrored(ps[:, :].rearrange("p (a q) -> p a q", q=128))
                t = act(pair(AT, j).rearrange("p (a q) -> p a q", q=128), src, ACT.Copy, tp)
                qtok[2 * j] = qtok[2 * j + 1] = [t]
                return [t]
            return f

        def evac_copy(dst, tokl, j, e="act"):
            def f(ps, tp):
                t = act(pair(dst, j), ps[:, :], ACT.Copy, tp)
                tokl[2 * j] = [t]
                tokl[2 * j + 1] = [t]
                return [t]
            return f
        LW = [at(f"LW{c}", [128, CH], o_lp + 4096 * c if c < 3 else o_kv + 4096) for c in range(4)]
        s_lw = dma_sem("s_lw")
        lwtok = []

        def lru_weights():
            for c in range(4):
                t = dma("pool", LW[c][:, :], d_lru[c], s_lw, *st["norm_done"])
            lwtok.append(t)
        call(lru_weights)
        mmtok = [[] for _ in range(NB)]
        aatok = [[] for _ in range(NB)]

        def lru_gates(j):
            def f():
                w = LW[j // 2][:, :].rearrange("p (b g m) -> p b g m", b=4, g=2)
                tps = []
                for g, bk, key in ((0, pS, "S"), (1, pT, "T")):
                    for h in range(2):
                        b = 2 * j + h
                        fn = lambda e, g=g, h=h, b=b, bk=bk: e.matmul(
                            bk[:, h * 256:(h + 1) * 256], w[:, b % 4, g, :], XC[:, b, :], start=(h == 0), stop=True,
                            skip_group_check=True)
                        if h == 0:
                            quiet("pe", fn, lwtok[0], *free[key], *xctok[b])
                        else:
                            tps.append(op("pe", fn, *xctok[b]))
                if j == 7:
                    for k in ("LP0", "LP1", "LP2", "PT0", "PT1", "BT0", "BT1"):
                        free[k] = [tps[1]]
                tg_ = []
                for g, bk in ((0, pS), (1, pT)):
                    for h in range(2):
                        b = 2 * j + h
                        t = act(TG[:, g, h * 256:(h + 1) * 256], bk[:, h * 256:(h + 1) * 256], ACT.Tanh, tps[g], t_half,
                                *free[f"TG{g}"], bias=v(V_BA + 16 * g + b), scale=0.5)
                    tg_.append(t)
                free["S"], free["T"] = [tg_[0]], [tg_[1]]
                for h in range(2):
                    b = 2 * j + h
                    tL = ts("dve", TG[:, 2, h * 256:(h + 1) * 256], TG[:, 0, h * 256:(h + 1) * 256], 1.0, ALU.add,
                            SP4[:, b:b + 1], ALU.mult, tg_[0], t_sp, *free["TG2"])
                tu = stt(pair(XC, j), TG[:, 1, :], 1.0, pair(XC, j), ALU.add, ALU.mult, tg_[1], tps[1])
                free["TG1"] = [tu]
                ta = act(pair(AA, j), TG[:, 2, :], ACT.Exp, tL)
                tt_ = act(TG[:, 0, :], TG[:, 2, :], ACT.Tanh, tL)
                free["TG2"] = [tt_]
                td = ts("dve", TG[:, 3, :], TG[:, 0, :], -1.0, ALU.mult, 1.0, ALU.add, tt_, *free["TG3"])
                td = op("dve", lambda e: e.reciprocal(TG[:, 3, :], TG[:, 3, :]), td)
                tm = stt(pair(MM, j), TG[:, 0, :], -2.0, TG[:, 3, :], ALU.mult, ALU.mult, td, tt_)
                free["TG0"] = [tm]
                free["TG3"] = [tm]
                for h in range(2):
                    xctok[2 * j + h] = [tu]
                    aatok[2 * j + h] = [ta]
                    mmtok[2 * j + h] = [tm]
            return f

        def lru_scan():
            for q in range(4):
                sl = MM[:, 4 * q:4 * q + 4, :]
                t = act(sl, sl, ACT.Sqrt, *mmtok[4 * q + 3], scale=0.25)
                t2_ = op("dve", lambda e, q=q: e.memset(MM[:, 4 * q:4 * q + 4, 0:1], 0.5), t)
                t3 = tt("dve", XC[:, 4 * q:4 * q + 4, :], XC[:, 4 * q:4 * q + 4, :], sl, ALU.mult, t2_, t,
                        *xctok[4 * q + 3])
                for b in range(4 * q, 4 * q + 4):
                    mmtok[b] = [op("dve", lambda e, b=b: e.tensor_tensor_scan(
                        MM[:, b, :], AA[:, b, :], XC[:, b, :], 0.0, ALU.mult, ALU.add), t3, *aatok[b])]

        ktok = [[], []]
        for j in range(8):
            unit(w_in, 8 + j, 4, X, evac_q(j))
            if j < 7:
                call(lambda j=j: defer(1, lru_gates(j)))
            if j == 6:
                call(lambda: defer(2, lru_gates(7)))
        unit(w_in, 16, 4, X, evac_copy(KT, ktok, 0))
        call(lambda: defer(1, lru_scan))
        vtok = [[]]

        def evac_tok(dst, c0, tokl, n=256):
            def f(ps, tp):
                t = act(dst[:, :, c0:c0 + n], ps[:, :].rearrange("p (t c) -> p t c", t=2), ACT.Copy, tp)
                tokl[0] = [t]
                return [t]
            return f
        unit(w_in, 17, 4, X, evac_tok(VT, 0, vtok), mode="t")

        s_bt = [dma_sem("s_bt0"), dma_sem("s_bt1")]
        jn = [0]

        def attn_steps(heads, nk, scale, bias, out, sink=None, pre=None, outtok=None, d64=False):
            n = jn[0]
            jn[0] += 1
            nkt = nk // 128
            L = LP[:, n % 3, :, 0:nk]
            lp, pt, sm = f"LP{n % 3}", f"PT{n % 2}", f"SM{n % 4}"
            mx, nm, rs, es, rd = (SM[:, n % 4, i, :] for i in range(5))
            Tv = pT[:, 0:2 * nkt * 128].rearrange("p (a q) -> p a q", q=128)
            Pv = PT[:, n % 2, 0:2 * nkt, :]
            s = {}

            def s0():
                bi, bt = (None, []) if bias is None else bias()
                for i, (q, k, _, tk) in enumerate(heads()):
                    fn = lambda e, q=q, k=k, i=i: e.matmul(pS2[:, i, 0:nk], q, k, start=True, stop=True,
                                                           skip_group_check=True)
                    tp = op("pe", fn, *tk, *free["S"])
                sv = pS2[:, :, 0:nk]
                if bi is None:
                    t = ts("dve", L, sv, scale, ALU.mult, None, None, tp, *free[lp])
                else:
                    t = stt(L, sv, scale, bi, ALU.mult, ALU.add, tp, *bt, *free[lp])
                s["bias_read"] = t
                free["S"] = [t]
                if pre:
                    pre(t)
                if sink is None:
                    t = op("dve", lambda e: e.tensor_reduce(nm, L, AX.X, ALU.max, negate=True), t, *free[sm])
                else:
                    t = op("dve", lambda e: e.tensor_reduce(mx, L, AX.X, ALU.max), t, *free[sm])
                    t = tt("dve", mx, mx, sink, ALU.max, t, t_vec)
                    t = ts("dve", nm, mx, -1.0, ALU.mult, None, None, t)
                    s["es"] = tt("dve", es, sink, nm, ALU.add, t)
                for i in range(2):
                    te = op("act", lambda e, i=i: e.activation(L[:, i, :], L[:, i, :], ACT.Exp, bias=nm[:, i:i + 1],
                                                               accum_out=rs[:, i:i + 1]), t)
                if sink is not None:
                    te = act(es, es, ACT.Exp, s["es"])
                s["e"] = te

            def s1():
                t = s["e"]
                if sink is not None:
                    t = tt("dve", rs, rs, es, ALU.add, t)
                t = op("dve", lambda e: e.reciprocal(rd, rs), t)
                for i in range(2):
                    t2_ = ts("dve", L[:, i, :], L[:, i, :], rd[:, i:i + 1], ALU.mult, None, None, t)
                free[sm] = [t2_]
                s["p"] = t2_

            def s2():
                for i in range(2):
                    for k in range(nkt):
                        a = i * nkt + k
                        fn = lambda e, i=i, k=k, a=a: e.transpose(Tv[:, a, :], L[:, i, k * 128:(k + 1) * 128], ident)
                        tp = op("pe", fn, s["p"], t_cst, *free["T"])
                free[lp] = [tp]
                t = act(Pv, Tv, ACT.Copy, tp, *free[pt])
                free["T"] = [t]
                s["pt"] = t

            def s3():
                hs = heads()
                for i in range(2):
                    o = pO[i * 64:(i + 1) * 64, 0:128] if d64 else pO[:, i * 128:(i + 1) * 128]
                    for k in range(nkt):
                        fn = lambda e, i=i, k=k, o=o, w=hs[i][2][k]: e.matmul(
                            o, w, Pv[:, i * nkt + k, :], start=(k == 0), stop=(k == nkt - 1), skip_group_check=True)
                        tp = op("pe", fn, s["pt"], *hs[i][3], *free["O"])
                free[pt] = [tp]
                src = mirrored(pO[:, 0:128]) if d64 else pO[:, 0:256].rearrange("p (a q) -> p a q", a=2)
                t = act(out, src, ACT.Copy, tp, *(s.get("war", [])))
                free["O"] = [t]
                outtok(t)
            return [s0, s1, s2, s3], s

        bt_at = {}
        ytok = [[] for _ in range(NB)]
        qk_done = {}

        def load_bt(b):
            def f():
                k = b % 2
                for i, h in enumerate(PERM[b]):
                    src = bass.AP(tensor=gdram.tensor, offset=h * 384, ap=[[1, 128], [1, 256]])
                    t = dma("pool", BT[:, k, i, :], src, s_bt[k], t_g, *free[f"BT{k}"])
                bt_at[b] = t
            return f

        def att_jobs():
            load_bt(0)()
            load_bt(1)()
            for b in range(NB):
                grp = b // 8
                for t in (0, 1):
                    nk = 128 * (t + 1)

                    def heads(b=b, t=t, nk=nk, grp=grp):
                        out = []
                        for i in range(2):
                            r = slice(64 * i, 64 * i + 64)
                            g = 2 * grp + i
                            out.append((AT[r, b, t * 128:(t + 1) * 128], KT[r, grp, 0:nk],
                                        [VT[:, k, g * 64:(g + 1) * 64] for k in range(t + 1)],
                                        [*qtok[b], *ktok[0], *vtok[0]]))
                        return out

                    def bias(b=b, t=t, nk=nk):
                        return BT[:, b % 2, :, 256 - nk:256], [bt_at[b]]

                    def pre(tok, b=b, t=t):
                        if t == 1:
                            free[f"BT{b % 2}"] = [tok]
                            if b + 2 < NB:
                                load_bt(b + 2)()

                    def done(tok, b=b):
                        ytok[b] = ytok[b] + [tok]
                    js, _ = attn_steps(heads, nk, SC1, bias, AT[:, b, t * 128:(t + 1) * 128],
                                       sink=v(V_SINK + 2 * b, 2), pre=pre, outtok=done, d64=True)
                    jobs.append(js)
        call(att_jobs)

        G0, G1 = 2 * 0.7978845608028654, 2 * 0.7978845608028654 * 0.044715
        ztok = [[] for _ in range(NB)]
        zact = {"hi": Zh, "lo": Zl, "toks": ztok}

        def split_out(hi, lo, src, t, key, *w):
            th = act(hi, src, ACT.Copy, t, *w)
            tl = tt("dve", lo, src, v32(hi), ALU.subtract, t, th, *w)
            free[key] = [th, tl]
            return [th, tl]

        def evac_gate(j):
            def f(ps, tp):
                g0, g1, g2 = TG[:, 0, :], TG[:, 1, :], TG[:, 2, :]
                t = act(g0, ps[:, :], ACT.Square, tp, *free["TG0"])
                t = ts("dve", g0, g0, 0.5 * G1, ALU.mult, 0.5 * G0, ALU.add, t)
                t = tt("dve", g0, g0, ps[:, :], ALU.mult, t)
                t = act(g1, g0, ACT.Tanh, t, *free["TG1"])
                free["TG0"] = [t]
                t = stt(g1, g1, 1.0, ps[:, :], ALU.add, ALU.mult, t)
                fr = [t]
                t = stt(g2, g1, 0.5, pair(MM, j), ALU.mult, ALU.mult, t, *mmtok[2 * j + 1], *free["TG2"])
                free["TG1"] = [t]
                tk = split_out(pair(Zh, j), pair(Zl, j), g2, t, "TG2", *mmtok[15])
                ztok[2 * j] = ztok[2 * j + 1] = tk
                mmtok[2 * j] = mmtok[2 * j + 1] = [t]
                return fr
            return f
        for j in range(8):
            unit(w_in, 18 + j, 4, X, evac_gate(j))

        gtok = [[] for _ in range(NB)]

        def evac_sig(dst, j, war):
            def f(ps, tp):
                t = act(pair(dst, j), ps[:, :], ACT.Tanh, tp, *war(j), scale=0.5)
                gtok[2 * j] = gtok[2 * j + 1] = [t]
                return [t]
            return f

        def evac_ya(j):
            def f(ps, tp):
                t = stt(pair(MM, j), pair(MM, j), 1.0, ps[:, :], ALU.add, ALU.mult, tp, *gtok[2 * j])
                mmtok[2 * j] = mmtok[2 * j + 1] = [t]
                return [t]
            return f
        for j in range(8):
            unit(w_in, 26 + j, 4, X, evac_sig(MM, j, lambda j: mmtok[2 * j]))
        for j in range(8):
            unit(w_lo, j, 4, lambda: zact, evac_ya(j))
        TB = at("TB", [128, NB, S], o_a + 16384)
        for j in range(8):
            unit(w_in, 34 + j, 4, X, evac_sig(TB, j, lambda j: [st["ya_end"]]))
            if j == 0:
                steps.insert(len(steps) - 1, ("call", lambda: st.__setitem__("ya_end", st["pe"])))

        def att_split():
            flush_later()
            drain_jobs()
            for q in range(4):
                src = AT[:, 4 * q:4 * q + 4, :]
                w = [x for b in range(4 * q, 4 * q + 4) for x in ytok[b]]
                th = act(Hhi[:, 4 * q:4 * q + 4, :], src, ACT.Copy, st["pe"], *w)
                tl = tt("dve", Hlo[:, 4 * q:4 * q + 4, :], src, v32(Hhi[:, 4 * q:4 * q + 4, :]), ALU.subtract, th, st["pe"], *w)
                for b in range(4 * q, 4 * q + 4):
                    hact["toks"][b] = [th, tl]
                st["att_read"] = [th, tl]
        call(att_split)
        Gh = at("Gh", [128, NB, S], o_a, F32R)
        Gl = at("Gl", [128, NB, S], o_a + 32768, F32R)
        mgtok = [[] for _ in range(NB)]
        mact = {"hi": Gh, "lo": Gl, "toks": mgtok}

        def evac_yb(j):
            def f(ps, tp):
                g0, g1 = TG[:, 0, :], TG[:, 1, :]
                t = stt(g0, pair(TB, j), 1.0, ps[:, :], ALU.add, ALU.mult, tp, *gtok[2 * j], *free["TG0"])
                fr = [t]
                t = tt("dve", g1, g0, pair(MM, j), ALU.add, t, *mmtok[2 * j], *free["TG1"])
                free["TG0"] = [t]
                th = act(pair(Gh, j), g1, ACT.Copy, t, *st["att_read"], scale=0.5)
                tl = stt(pair(Gl, j), g1, 0.5, v32(pair(Gh, j)), ALU.mult, ALU.subtract, t, th, st["ya_end"])
                free["TG1"] = [th, tl]
                mgtok[2 * j] = mgtok[2 * j + 1] = [th, tl]
                st["mm_read"] = t
                return fr
            return f
        for j in range(8):
            unit(w_ao, j, 4, X, evac_yb(j))

        def evac_res(j, gcol, stat, gg):
            def f(ps, tp):
                for i in range(2):
                    b = 2 * j + i
                    t = stt(RES[:, b, :], ps[:, i * 256:(i + 1) * 256], mod[:, gcol + b:gcol + b + 1], RES[:, b, :],
                            ALU.mult, ALU.add, tp, modtok[gg[0]], modtok[gg[1]], *restok[b])
                    restok[b] = [t]
                if stat:
                    mm = stat_sq(j, pair(RES, j), t)
                    if j < 7:
                        defer(1, mm)
                    else:
                        flush_later()
                        mm()
                return [t]
            return f
        for j in range(8):
            unit(w_o, j, 4, lambda: mact, evac_res(j, 32, True, (4, 5)))

        memtok0 = [None] * 4
        mem0 = {"hi": Mh0, "lo": Ml0}

        def mem_act(m, tk):
            return lambda: {**m, "toks": [tk[k // 4] for k in range(NB)]}
        w_kv, w_2, w_o2 = d_w["kv"], d_w["in2"], d_w["out2"]

        def mem_load(m, tk, after):
            steps.append(("mem", dict(dst=(m["hi"], m["lo"]), done=tk, after=after)))
        mem_load(mem0, memtok0, lambda: [st["mm_read"]])
        kvtok = {"k": [[] for _ in range(4)], "v": [[], []]}
        
        def kv_war():
            return [st["kv_end"]]

        def evac_km(j):
            def f(ps, tp):
                t = act(pair(KM, j), ps[:, :], ACT.Copy, tp, *kv_war())
                kvtok["k"][2 * j] = kvtok["k"][2 * j + 1] = [t]
                return [t]
            return f

        def evac_vm(j):
            def f(ps, tp):
                t = act(VM[:, :, j * 256:(j + 1) * 256], ps[:, :].rearrange("p (t c) -> p t c", t=2), ACT.Copy, tp,
                        *kv_war())
                kvtok["v"][j] = [t]
                return [t]
            return f

        def kv_unit(layer, j, m, tk):
            unit(w_kv, 4 * layer + j, 4, mem_act(m, tk), evac_km(j) if j < 2 else evac_vm(j - 2), mode="f" if j < 2 else "t")

        def norm2():
            last = st["pe"]

            def head():
                tr = rstd(EPS)
                t = stt(A2v[:, :], mod[:, 64:80], 1.0, v(V_N2, 16), ALU.add, ALU.mult, modtok[8], modtok[9], t_vec)
                for q in range(5):
                    def blocks(q=q):
                        for b in range(q * 4, min(NB, q * 4 + 4)):
                            emit_h(b, "mod", tr, A2v[:, b:b + 1], mod[:, 48 + b:49 + b], last,
                                   tmod=[t, modtok[6], modtok[7]])
                        if q == 4:
                            close_t()
                    defer(1 + q, blocks)
            defer(1, head)
        call(norm2)

        def close_t():
            for k in (2, 3):
                free[f"TG{k}"] = tfree.pop(f"TG{k}0", []) + tfree.pop(f"TG{k}1", [])
        call(lambda: st.__setitem__("kv_end", st["pe"]))
        kv_unit(0, 0, mem0, memtok0)
        kv_unit(0, 1, mem0, memtok0)
        call(flush_later)

        ftok = [[[] for _ in range(8)] for _ in range(2)]
        fread = [[], []]

        def evac_ff1(f_, j):
            def f(ps, tp):
                k = f_ % 2
                a, b_ = TG[:, 2 * (j % 2), :], TG[:, 2 * (j % 2) + 1, :]
                ka, kb = f"TG{2 * (j % 2)}", f"TG{2 * (j % 2) + 1}"
                t = ts("dve", a, ps[:, :], 0.0, ALU.max, None, None, tp, *free[ka])
                fr = [t]
                t = act(b_, a, ACT.Square, t, *free[kb])
                free[ka] = [t]
                tk = split_out(pair(Fh[k], j), pair(Fl[k], j), b_, t, kb, *fread[k])
                ftok[k][2 * j] = ftok[k][2 * j + 1] = tk
                return fr
            return f

        def ff1(f_):
            if f_ < 2:
                call(lambda: fread.__setitem__(f_, [st["ffw"]]))
            for j in range(4):
                unit(w_f1, 4 * f_ + j, 4, X, evac_ff1(f_, j))

        def ff2(f_):
            k = f_ % 2
            for j in range(8):
                unit(w_f2, j, 2, lambda k=k: {"hi": Fh[k], "lo": Fl[k], "toks": ftok[k]},
                     evac_res(j, 80, f_ == 7, (10, 11)), kc0=2 * f_)
            call(lambda k=k: fread.__setitem__(k, [st["pe"]]))
        call(lambda: st.__setitem__("ffw", st["pe"]))
        ff1(0)
        for f_ in range(1, 8):
            ff1(f_)
            ff2(f_ - 1)
        ff2(7)

        def norm3():
            last = st["pe"]

            def head():
                tr = rstd(EPS)
                for q in range(4):
                    def blocks(q=q):
                        for b in range(q * 4, q * 4 + 4):
                            emit_h(b, "rms", tr, v(V_FG + b), None, last)
                    defer(1 + q, blocks)
            defer(1, head)
        call(norm3)
        kv_unit(0, 2, mem0, memtok0)
        kv_unit(0, 3, mem0, memtok0)
        call(flush_later)

        memtok1 = [None] * 4
        mem1 = {"hi": Mh1, "lo": Ml1}

        def layer(l):
            tk = {n: [[] for _ in range(8)] for n in ("DQ", "DK", "FQ", "FK", "MQ", "IQ")}
            tk1 = {n: [[]] for n in ("DV", "FV")}
            s_ = {}
            a_war = lambda: [st["a_end"]]
            call(lambda: st.__setitem__("a_end", st["pe"]))

            def evac_rope(dst, j, cc, name):
                def f(ps, tp):
                    g0, g1, g2 = TG[:, 0, :], TG[:, 1, :], TG[:, 2, :]
                    t = act(g0, ps[:, :], ACT.Copy, tp, *free["TG0"])

                    def rest(t=t):
                        pm = cst[:, cc[0]:cc[0] + 128]
                        tq = op("pe", lambda e: e.matmul(pM[:, :], pm, g0, start=True, stop=True), t, *free["M"])
                        v3 = lambda a: a.rearrange("p (b s) -> p b s", b=2)
                        t1_ = tt("dve", v3(g1), v3(g0), over(cst[:, cc[1]:cc[1] + 256], 2), ALU.mult, t, *free["TG1"])
                        t2_ = tt("dve", v3(g2), v3(pM[:, :]), over(cst[:, cc[2]:cc[2] + 256], 2), ALU.mult, tq,
                                 *free["TG2"])
                        free["M"] = [t2_]
                        free["TG0"] = [tq, t1_]
                        t3 = tt("dve", pair(dst, j), g1, g2, ALU.add, t1_, t2_, *a_war())
                        free["TG1"] = free["TG2"] = [t3]
                        tk[name][2 * j] = tk[name][2 * j + 1] = [t3]
                    defer(1, rest)
                    return [t]
                return f
            R64 = (C_P64, C_COS64, C_SIN64)
            R128 = (C_P128, C_COS128, C_SIN128)

            def evac_plain(dst, j, name):
                def f(ps, tp):
                    t = act(pair(dst, j), ps[:, :], ACT.Copy, tp, *a_war())
                    tk[name][2 * j] = tk[name][2 * j + 1] = [t]
                    return [t]
                return f

            def evac_v(dst, j, name):
                def f(ps, tp):
                    t = act(dst[:, :, j * 256:(j + 1) * 256], ps[:, :].rearrange("p (t c) -> p t c", t=2), ACT.Copy,
                            tp, *a_war())
                    tk1[name][0] = tk1[name][0] + [t]
                    return [t]
                return f

            def evac_small(ps, tp):
                g0, g1, g2 = TG[:, 0, 0:256], TG[:, 1, 0:256], TG[:, 2, 0:256]
                t = act(g0, ps[:, 0:256], ACT.Copy, tp, *free["TG0"])
                tw = act(TK[:, :, :], ps[:, 256:320].rearrange("p (t c) -> p t c", t=2)[:, :, 0:22], ACT.Copy, tp)

                def rest():
                    pm = cst[:, C_P64:C_P64 + 128]
                    tq = op("pe", lambda e: e.matmul(pM[:, 0:256], pm, g0, start=True, stop=True), t, *free["M"])
                    t1_ = tt("dve", g1, g0, cst[:, C_COS64:C_COS64 + 256], ALU.mult, t, *free["TG1"])
                    t2_ = tt("dve", g2, pM[:, 0:256], cst[:, C_SIN64:C_SIN64 + 256], ALU.mult, tq, *free["TG2"])
                    free["TG0"] = [tq, t1_]
                    t3 = tt("dve", IK[:, :], g1, g2, ALU.add, t1_, t2_)
                    free["TG1"] = free["TG2"] = [t3]
                    s_["ik"] = t3
                    s_["w"] = ts("dve", TK[:, :, 0:16], TK[:, :, 0:16], 0.25, ALU.mult, None, None, tw)
                    c6 = lambda i: SMALL[:, i, 0:12]
                    z = c6(0).rearrange("p (t h) -> p t h", t=2)
                    bf = v(V_BF + 6 * l, 6)
                    ta = tt("dve", z, TK[:, :, 16:22], over(bf, 2), ALU.add, tw, t_vec)
                    tb = ts("dve", LF[:, :, :], z, 0.0, ALU.min, None, None, ta)
                    ta = stt(c6(0), c6(0), -1.0, c6(0), ALU.mult, ALU.max, tb)
                    p_, ta = log1p_exp(lambda i: c6(1 + i), c6(0), 12, ta)
                    lf = LF[:, :, :].rearrange("p t h -> p (t h)")
                    ta = stt(lf, p_, -2.0, lf, ALU.mult, ALU.add, ta)
                    s_["lf"] = ta
                    quiet("pe", lambda e: e.matmul(pM[:, 0:6], U[:, 0:128], LF[:, 0, :], start=True, stop=True,
                                                   skip_group_check=True), ta, t2_)
                    quiet("pe", lambda e: e.matmul(pM[:, 6:12], ones, LF[:, 0, :], start=True, stop=False,
                                                   skip_group_check=True))
                    tq = op("pe", lambda e: e.matmul(pM[:, 6:12], U[:, 0:128], LF[:, 1, :], start=False, stop=True,
                                                     skip_group_check=True))
                    tc = op("dve", lambda e: e.tensor_copy(CQ[:, :, :], pM[:, 0:12].rearrange("p (t h) -> p t h", t=2)), tq)
                    free["M"] = [tc]
                    s_["cq"] = tc
                defer(1, rest)
                return [tw]

            sc_t = [SC[:, 0:128], SC[:, 128:384]]
            sctok = [[], []]

            def idx_steps(t, b):
                nk = 128 * (t + 1)
                n = jn[0]
                jn[0] += 1
                L = LP[:, n % 3, :, 0:nk]
                lp = f"LP{n % 3}"
                x_ = {}

                def s0():
                    for i in range(2):
                        r = slice(64 * i, 64 * i + 64)
                        tp = op("pe", lambda e, i=i, r=r: e.matmul(
                            pS2[:, i, 0:nk], IQ[r, b, t * 128:(t + 1) * 128], IK[r, 0:nk], start=True,
                            stop=True, skip_group_check=True), *tk["IQ"][b], s_["ik"], *free["S"])
                    sv = pS2[:, :, 0:nk]
                    ta = act(L, sv, ACT.Relu, tp, *free[lp], scale=0.125)
                    free["S"] = [ta]
                    x_["a"] = ta

                def s1():
                    ta = x_["a"]
                    for i in range(2):
                        w = TK[:, t, 2 * b + i:2 * b + i + 1]
                        if b == 0 and i == 0:
                            ta = ts("dve", sc_t[t], L[:, 0, :], w, ALU.mult, None, None, ta, s_["w"],
                                    *st.get("sc_read", []))
                        else:
                            ta = stt(sc_t[t], L[:, i, :], w, sc_t[t], ALU.mult, ALU.add, ta, x_["a"], *sctok[t])
                        sctok[t] = [ta]
                    free[lp] = [ta]
                return [s0, s1]

            def causal(ap, t, nk, reps, tok):
                pat = [[-1, nk]] if reps == 1 else [[0, reps], [-1, nk]]
                return op("pool", lambda e: e.affine_select(out=ap, in_=ap, pattern=pat, compare_op=ALU.is_ge, fill=NEG,
                                                            base=128 * t, channel_multiplier=1), *tok)

            def top_steps(t):
                nk = 128 * (t + 1)
                a = sc_t[t]

                def start():
                    sctok[t] = [causal(a, t, nk, 1, sctok[t])]

                def rnd():
                    t_ = op("dve", lambda e: e.max(MX8[:, :], a), *sctok[t])
                    sctok[t] = [op("dve", lambda e: e.match_replace(a, MX8[:, :], a, TAKEN), t_)]

                def end():
                    t_ = ts("dve", a, a, -2e38, ALU.is_ge, NEG, ALU.mult, *sctok[t])
                    sctok[t] = [causal(a, t, nk, 1, [t_])]
                return [[start, rnd], [rnd], [rnd], [rnd], [rnd], [rnd], [rnd], [rnd, end]]

            def big_attn(Q, K, V_, n, y0, pairs, qn, kn, vn, bias_of, nk_of, scale=SC2):
                for pr in range(pairs):
                    for t in (0, 1):
                        nk = nk_of(t)

                        def heads(pr=pr, t=t, nk=nk):
                            out = []
                            for i in range(2):
                                h = 2 * pr + i
                                tks = [*kn(h), *vn(), *qn(h)]
                                out.append((Q[:, h, t * 128:(t + 1) * 128], K[:, h, 0:nk],
                                            [V_[:, k, h * 128:(h + 1) * 128] for k in range(nk // 128)], tks))
                            return out

                        def done(tok, pr=pr):
                            for i in range(2):
                                ytok[y0 + 2 * pr + i] = ytok[y0 + 2 * pr + i] + [tok]
                        pre, bi, fb = bias_of(pr, t, nk)
                        js, sd = attn_steps(heads, nk, scale, bi, Y[:, y0 + 2 * pr:y0 + 2 * pr + 2, t * 128:(t + 1) * 128],
                                            pre=fb, outtok=done)
                        sd["war"] = [st["a_end"]]
                        jobs.append(([pre] if pre else []) + js)

            def fox_bias(pr, t, nk):
                x_ = {}
                kk = [0]

                def pre():
                    k = fx[0] % 2
                    fx[0] += 1
                    kk[0] = k
                    for i in range(2):
                        h = 2 * pr + i
                        o = pM[:, i * 256:i * 256 + 256]
                        w0, w1 = spread(LF[:, 0, h:h + 1], 128), spread(LF[:, 1, h:h + 1], 128)
                        tp = op("pe", lambda e, o=o, w0=w0, i=i: e.matmul(o[:, 0:nk], w0, U[:, 0:nk], start=(i == 0), stop=(t == 0),
                                                                     skip_group_check=True), s_["lf"], *free["M"])
                        if t:
                            tp = op("pe", lambda e, o=o, w1=w1: e.matmul(o[:, 128:256], w1, U[:, 0:128], start=False,
                                                                         stop=True, skip_group_check=True))
                    for i in range(2):
                        h = 2 * pr + i
                        td = ts("dve", BT[:, k, i, 0:nk], pM[:, i * 256:i * 256 + nk], -1.0, ALU.mult,
                                CQ[:, t, h:h + 1], ALU.add, tp, s_["cq"], *free[f"BT{k}"])
                    free["M"] = [td]
                    x_["d"] = causal(BT[:, k, :, 0:nk], t, nk, 2, [td])

                def used(tok):
                    free[f"BT{kk[0]}"] = [tok]
                return pre, (lambda: (BT[:, kk[0], :, 0:nk], [x_["d"]])), used

            def dsa_bias(pr, t, nk):
                def used(tok):
                    st["sc_read"] = [tok]
                return None, (lambda: (over(sc_t[t], 2), sctok[t])), used

            def mem_bias(pr, t, nk):
                return None, None, None
            fx = [0]
            c0 = 32 * l
            for j in range(4):
                unit(w_2, c0 + j, 4, X, evac_rope(IQ, j, R64, "IQ"))
            unit(d_s2, l, 4, X, evac_small, mode="s", width=150)

            def start_idx():
                for t in (0, 1):
                    for b in range(8):
                        jobs.append(idx_steps(t, b))
                for t in (0, 1):
                    for g in top_steps(t):
                        jobs.append([(lambda g=g: [f() for f in g])])
            for j in range(3):
                unit(w_2, c0 + 4 + j, 4, X, evac_rope(DQ, j, R128, "DQ"))
                if j == 0:
                    call(start_idx)
            for j in range(3):
                unit(w_2, c0 + 7 + j, 4, X, evac_rope(DK, j, R128, "DK"))
            for j in range(2):
                unit(w_2, c0 + 10 + j, 4, X, evac_plain(MQ, j, "MQ"))
            call(lambda: big_attn(MQ, KM, VM, 4, 12, 2, lambda h: tk["MQ"][h], lambda h: kvtok["k"][h],
                                  lambda: [*kvtok["v"][0], *kvtok["v"][1]], mem_bias, lambda t: 256))
            for j in range(3):
                unit(w_2, c0 + 12 + j, 4, X, evac_v(DV, j, "DV"), mode="t")
            call(lambda: big_attn(DQ, DK, DV, 6, 6, 3, lambda h: tk["DQ"][h], lambda h: tk["DK"][h],
                                  lambda: tk1["DV"][0], dsa_bias, lambda t: 128 * (t + 1)))
            for j in range(3):
                unit(w_2, c0 + 15 + j, 4, X, evac_plain(FQ, j, "FQ"))
            for j in range(3):
                unit(w_2, c0 + 18 + j, 4, X, evac_plain(FK, j, "FK"))
            for j in range(3):
                unit(w_2, c0 + 21 + j, 4, X, evac_v(FV, j, "FV"), mode="t")
            call(lambda: big_attn(FQ, FK, FV, 6, 0, 3, lambda h: tk["FQ"][h], lambda h: tk["FK"][h],
                                  lambda: tk1["FV"][0], fox_bias, lambda t: 128 * (t + 1)))

            yact = {"hi": Yh, "lo": Yl, "toks": [[] for _ in range(NB)]}

            def evac_silu(j):
                def f(ps, tp):
                    g0, g1, g2 = TG[:, 0, :], TG[:, 1, :], TG[:, 2, :]
                    need = 2 if j >= 0 else 0
                    while any(len(ytok[b]) < need for b in (2 * j, 2 * j + 1)):
                        advance()
                    while any(len(ytok[b]) < need for b in range(6, 12)):
                        advance()
                    t = act(g0, ps[:, :], ACT.Tanh, tp, *free["TG0"], scale=0.5)
                    t = stt(g1, g0, 1.0, ps[:, :], ALU.add, ALU.mult, t, *free["TG1"])
                    free["TG0"] = [t]
                    fr = [t]
                    ys = [x for b in (2 * j, 2 * j + 1, *range(6, 12)) for x in ytok[b]]
                    t = stt(g2, g1, 0.5, pair(Y, j), ALU.mult, ALU.mult, t, *ys, *free["TG2"])
                    free["TG1"] = [t]
                    tkk = split_out(pair(Yh, j), pair(Yl, j), g2, t, "TG2", t, *ys)
                    yact["toks"][2 * j] = yact["toks"][2 * j + 1] = tkk
                    return fr
                return f
            for n, j in enumerate((3, 4, 5, 6, 7, 0, 1, 2)):
                unit(w_2, c0 + 24 + n, 4, X, evac_silu(j))
            call(lambda: (flush_later(), drain_jobs()))

            def evac_y(j):
                def f(ps, tp):
                    t = stt(pair(RES, j), pair(RES, j), ALPHA, ps[:, :], ALU.mult, ALU.add, tp, *restok[2 * j],
                            *restok[2 * j + 1])
                    restok[2 * j] = restok[2 * j + 1] = [t]
                    if j < 7:
                        defer(1, lambda: stat_mm(j, pair(RES, j), t))
                    else:
                        flush_later()
                        stat_mm(j, pair(RES, j), t)
                    return [t]
                return f
            if l == 0:
                call(lambda: st.__setitem__("m1", st["pe"]))
            for j in range(8):
                unit(w_o2, 8 * l + j, 4, lambda: yact, evac_y(j))
            call(lambda: [ytok.__setitem__(b, []) for b in range(NB)])
            if l == 0:
                mem_load(mem1, memtok1, lambda: [st["m1"]])

            def norm():
                last = st["pe"]

                def mean():
                    t = ts("dve", R2, pS[:, 0:256], 1.0 / D, ALU.mult, None, None, st["stat"], *free["BT0"],
                           *free["BT1"])
                    free["S"] = [t]
                    for j in range(8):
                        tz = tt("dve", RES[:, 2 * j:2 * j + 2, :], RES[:, 2 * j:2 * j + 2, :], over(R2, 2), ALU.subtract,
                                t, *restok[2 * j], st["stat"])
                        restok[2 * j] = restok[2 * j + 1] = [tz]
                        stat_sq(j, pair(RES, j), tz)()
                    free["BT0"] = [tz]

                def head():
                    tr = rstd(LN_EPS)
                    kind = "ln" if l == 0 else "out"
                    for q in range(5):
                        def blocks(q=q):
                            for b in range(q * 4, min(NB, q * 4 + 4)):
                                emit_h(b, kind, tr, v(V_LNG + 16 * l + b), v(V_LNB + 16 * l + b), last)
                                if l == 1 and b % 4 == 3:
                                    dma("sp", d_out[:, b - 3:b + 1, :], RES[:, b - 3:b + 1, :], s_out,
                                        *[x for z in range(b - 3, b + 1) for x in restok[z]])
                            if q == 4:
                                close_t()
                        defer(2 + q, blocks)
                mean()
                defer(2, head)
            call(norm)
            if l == 0:
                call(lambda: st.__setitem__("kv_end", st["pe"]))
                for j in range(4):
                    kv_unit(1, j, mem1, memtok1)
            call(flush_later)
            call(lambda: st.__setitem__("stat_done", st["stat"]))
        s_out = dma_sem("s_out")
        call(lambda: [ytok.__setitem__(b, []) for b in range(NB)])
        layer(0)
        layer(1)

        nw = [0]
        background = [dict(kind="ada", g=g, kt=kt) for g in range(4, 12) for kt in range(NB)]
        order = []

        def add(el):
            stream.append(el)
            return len(stream) - 1

        def add_ada(g, kt):
            add(dict(kind="ada", g=g, kt=kt, n=CH, src=d_ada[g, kt]))
        for g in range(4):
            for kt in range(NB):
                add_ada(g, kt)
        bg = 0
        chunks = 0
        for kind, s in steps:
            if kind == "unit":
                s["ids"] = []
                for c in range(s["nkc"]):
                    n = 4 * s["width"]
                    i = add(dict(kind="w", n=n, slot=nw[0] % NSP, src=s["src"][s["u"], s["kc0"] + c]))
                    nw[0] += 1
                    order.append(i)
                    s["ids"].append(i)
                    chunks += 1
                    if chunks > 8 and bg < len(background) and chunks % 2 == 0:
                        add_ada(background[bg]["g"], background[bg]["kt"])
                        bg += 1
            elif kind == "mem":
                for q in range(4):
                    add(dict(kind="mem", n=CH, q=q, src=d_mem[:, 4 * q:4 * q + 4, :].rearrange("p b s -> p (b s)"), **s))
        assert bg == len(background)
        pos = {i: n for n, i in enumerate(order)}
        for kind, s in steps:
            if kind == "unit":
                s["ahead"] = [order[min(pos[i] + AHEAD, len(order) - 1)] for i in s["ids"]]
        pump()
        while stream[st["split"]]["kind"] == "ada":
            push_split()
        for kind, s in steps:
            if kind == "unit":
                run_unit(s)
            elif kind == "call":
                s()
        flush_later()
        wait("sp", [(s_out, count[id(s_out)])])

        block = ctx.enter_context(nc.Block())

        def play(e):
            return lambda eng: [f(eng) for f in prog[e]] and None
        block.tensor(play("pe"))
        block.scalar(play("act"))
        block.vector(play("dve"))
        block.gpsimd(play("pool"))
        block.sync(play("sp"))


def _strips(w, width=256):
    k, n = w.shape
    return np.ascontiguousarray(
        w.reshape(k // 512, 4, 128, n // width, width).transpose(3, 0, 2, 1, 4)).reshape(n // width, k // 512, 128, 4 * width)


def _cols(a):
    return np.asarray(a).reshape(-1, 128).T


def _constants():
    f = np.float32
    c = np.zeros((128, C_END), f)
    c[:, C_ONE:C_ONE + 128] = 1
    i = np.arange(128)
    c[i, C_ID + i] = 1
    c[i ^ 32, C_P64 + i] = 1
    c[i ^ 64, C_P128 + i] = 1
    c[:, C_U:C_U + 256] = i[:, None] <= np.arange(256)[None, :]
    for d, cc, cs in ((128, C_COS128, C_SIN128), (64, C_COS64, C_SIN64)):
        half = d // 2
        inv = (f(10000.0) ** (-np.arange(half, dtype=f) / f(half))).astype(f)
        ang = (np.arange(S, dtype=f)[None, :] * inv[:, None]).astype(f).astype(np.float64)
        row = i % d
        c[:, cc:cc + S] = np.cos(ang)[row % half]
        c[:, cs:cs + S] = np.sin(ang)[row % half] * np.where(row < half, -1.0, 1.0)[:, None]
    hot = np.zeros((32, 384), f)
    rel = np.arange(128)
    big = 16 + (np.log(np.maximum(rel, 1).astype(f) / f(16)) / f(np.log(8.0)) * f(16)).astype(np.int32)
    bucket = np.where(rel < 16, rel, np.minimum(big, 31))
    hot[bucket, 255 - rel] = 1
    return c, hot


def kernel(**inp):
    import concourse.bacc as _bacc
    from concourse import mybir as _mybir
    from concourse.bass_utils import run_bass_kernel_spmd as _run

    a = {k: np.asarray(x) for k, x in inp.items()}
    heads = np.concatenate([[b, 8 + b] if b < 8 else [8 + b, 16 + b] for b in range(16)])
    qcols = (heads[:, None] * 64 + np.arange(64)[None]).ravel()
    xT = lambda z: np.ascontiguousarray(z[0].T.reshape(NB, 128, S).transpose(1, 0, 2))
    w_in = a["w_in"][0]
    o = {}
    o["x"] = xT(a["x"])
    o["mem"] = xT(a["mem_2"])
    rep = lambda z: np.broadcast_to(np.asarray(z).reshape(1, -1), (128, np.asarray(z).size))
    o["vec"] = np.ascontiguousarray(np.concatenate([
        _cols(a["norm1_g"]), _cols(a["conv_w"]), _cols(a["conv_b"]), _cols(a["lru_ba"]), _cols(a["lru_bx"]),
        _cols(a["lru_lambda"]), _cols(a["norm2_g"]), _cols(a["final_g"]), _cols(a["ln_gain_2"]), _cols(a["ln_bias_2"]),
        _cols(a["c"]), _cols(a["b_ada"]), rep(a["attn_sinks"][0][heads]), rep(a["b_forget_2"])], axis=1))
    o["cst"], o["hot"] = _constants()
    o["relb"] = np.ascontiguousarray(a["rel_bias"])
    o["ada"] = np.ascontiguousarray(a["w_ada"][0].reshape(NB, 128, 12, CH).transpose(2, 0, 1, 3))
    lru = np.stack([a["lru_wa"][0], a["lru_wx"][0]], axis=1)
    o["lru"] = np.ascontiguousarray(lru.reshape(4, 4, 2, 128, 128).transpose(0, 3, 1, 2, 4)).reshape(4, 128, CH)
    order = np.concatenate([np.arange(0, 2048), 4096 + qcols, np.arange(6144, 6656), np.arange(2048, 4096),
                            np.arange(6656, 10752)])
    o["w_in"] = _strips(w_in[:, order])
    o["w_lru_out"] = _strips(a["w_lru_out"][0])
    o["w_attn_out"] = _strips(a["w_attn_out"][0][qcols])
    o["w_out"] = _strips(a["w_out"][0])
    o["w_ff1"] = _strips(a["w_ff1"][0])
    o["w_ff2"] = _strips(a["w_ff2"][0])
    o["w_kv"] = np.concatenate([_strips(a["w_mem_kv_2"][l]) for l in range(2)])
    r = lambda s, n: np.arange(s, s + n)
    main = np.concatenate([r(6150, 1024), r(3078, 768), r(3846, 768), r(7254, 512), r(4614, 768), r(0, 768),
                           r(768, 768), r(1536, 768), r(5382, 768), r(7766, 512), r(2304, 768)])
    small = np.concatenate([r(7174, 64), r(7174, 64), r(7238, 16), r(3072, 6)])
    o["w_in2"] = np.concatenate([_strips(a["w_in_2"][l][:, main]) for l in range(2)])
    o["w_s2"] = np.concatenate([_strips(a["w_in_2"][l][:, small], 150) for l in range(2)])
    o["w_out2"] = np.concatenate([_strips(a["w_out_2"][l]) for l in range(2)])

    nc = _bacc.Bacc("TRN2", target_bir_lowering=False, num_devices=1)
    arrays, ap = {}, {}
    for name, z in o.items():
        arrays[f"in_{name}"] = z
        ap[name] = nc.dram_tensor(f"in_{name}", z.shape, _mybir.dt.from_np(z.dtype), kind="ExternalInput").ap()
    out = nc.dram_tensor("out_0", (128, NB, S), F32, kind="ExternalOutput").ap()
    d_w = {"in": ap["w_in"], "lru_out": ap["w_lru_out"], "attn_out": ap["w_attn_out"], "out": ap["w_out"],
           "ff1": ap["w_ff1"], "ff2": ap["w_ff2"], "kv": ap["w_kv"], "in2": ap["w_in2"], "out2": ap["w_out2"]}
    build(nc, ap["x"], ap["mem"], ap["vec"], ap["cst"], ap["hot"], ap["relb"], ap["ada"], ap["lru"], d_w, ap["w_s2"], out)
    r_ = _run(nc, [arrays], core_ids=[0])
    got = r_.results[0]["out_0"]
    return np.ascontiguousarray(got.transpose(1, 0, 2).reshape(D, S).T).reshape(1, S, D)
```

```python
from collections import deque
from contextlib import ExitStack

import numpy as np

import concourse.bass as bass
from concourse import mybir

F32 = mybir.dt.float32
F32R = mybir.dt.float32r
ALU = mybir.AluOpType
ACT = mybir.ActivationFunctionType
AX = mybir.AxisListType

D = 2048
S = 256
NB = D // 128
EPS = 1e-6
LN_EPS = 1e-5
ALPHA = 4 ** 0.25
NEG = -1e30
TAKEN = -3e38
SC1 = 64 ** -0.5
SC2 = 128 ** -0.5

V_N1, V_CW, V_CB, V_BA, V_BX, V_LAM, V_N2, V_FG = 0, 16, 80, 96, 112, 128, 144, 160
V_LNG, V_LNB, V_C, V_ADA, V_SINK, V_BF = 176, 208, 240, 256, 352, 384
V_END = 396
C_ONE, C_ID, C_DUP, C_SWAP, C_U = 0, 128, 256, 384, 512
C_COS128, C_SIN128, C_COS64, C_SIN64, C_END = 768, 1024, 1280, 1536, 1792

CH = 1024
NRAW = 5
NSP = 4
AHEAD = NSP - 1


def build(nc, d_x, d_mem, d_vec, d_cst, d_hot, d_relb, d_ada, d_lru, d_w, d_s2, d_out):
    ctx = ExitStack()
    with ctx:
        cur = [16512]

        def place(nbytes):
            at = cur[0]
            cur[0] += nbytes
            return at

        def at(name, shape, off, dt=F32):
            return nc.alloc_sbuf_tensor_at(name, shape, dt, offset=off)

        o_raw = place(NRAW * CH * 4)
        o_hi = place(NSP * CH * 4)
        o_lo = place(NSP * CH * 4)
        raw = [at(f"raw{i}", [128, CH], o_raw + i * CH * 4) for i in range(NRAW)]
        whi = at("whi", [128, NSP, CH], o_hi, F32R)
        wlo = at("wlo", [128, NSP, CH], o_lo, F32R)
        RES = at("RES", [128, NB, S], place(NB * S * 4))
        o_h = place(2 * NB * S * 4)
        Hhi = at("Hhi", [128, NB, S], o_h, F32R)
        Hlo = at("Hlo", [128, NB, S], o_h + 16384, F32R)
        o_a = place(4 * 16384)
        o_acc = place(4096)
        o_kv = place(8192)
        KM = at("KM", [128, 4, S], o_kv)
        VM = at("VM", [128, 2, 512], o_kv + 4096)
        cst = at("cst", [128, C_END], place(C_END * 4))
        vec = at("vec", [128, V_END], place(1600))
        mod = at("mod", [128, 96], place(384))
        A1v = at("A1v", [128, NB], place(64))
        A2v = at("A2v", [128, NB], place(64))
        o_lp = place(3 * 2048)
        o_pt = place(2 * 2048)
        o_bt = place(2 * 2048)
        o_tg = place(4 * 2048)
        o_sm = place(384)
        assert cur[0] <= 229344, cur[0]
        LP = at("LP", [128, 3, 2, S], o_lp)
        PT = at("PT", [128, 2, 4, 128], o_pt)
        BT = at("BT", [128, 2, 2, S], o_bt)
        TG = at("TG", [128, 4, 512], o_tg)
        SM = at("SM", [128, 4, 6, 2], o_sm)
        MX8 = at("MX8", [128, 2, 8], o_sm + 192)
        ones = cst[:, C_ONE:C_ONE + 128]
        ident = cst[:, C_ID:C_ID + 128]
        U = cst[:, C_U:C_U + 256]

        acc = [at("acc0", [128, CH], o_acc), at("acc1", [128, CH], o_a)]
        AT = at("AT", [128, NB, S], o_a)
        XC = at("XC", [128, NB, S], o_a + 16384)
        AA = at("AA", [128, NB, S], o_a + 32768)
        MM = at("MM", [128, NB, S], o_a + 49152)
        Zh = at("Zh", [128, NB, S], o_a + 16384, F32R)
        Zl = at("Zl", [128, NB, S], o_a + 32768, F32R)
        KT = at("KT", [128, 2, S], o_kv)
        VT = at("VT", [128, 2, 256], o_kv + 2048)
        Mh0 = at("Mh0", [128, NB, S], o_a + 16384, F32R)
        Ml0 = at("Ml0", [128, NB, S], o_a + 49152, F32R)
        Fh = [at(f"Fh{i}", [128, 8, S], o_a + 32768 * i, F32R) for i in range(2)]
        Fl = [at(f"Fl{i}", [128, 8, S], o_a + 32768 * i + 8192, F32R) for i in range(2)]
        DQ = at("DQ", [128, 6, S], o_a)
        DK = at("DK", [128, 6, S], o_a + 6144)
        DV = at("DV", [128, 2, 768], o_a + 12288)
        FQ = at("FQ", [128, 6, S], o_a + 18432)
        FK = at("FK", [128, 6, S], o_a + 24576)
        FV = at("FV", [128, 2, 768], o_a + 30720)
        MQ = at("MQ", [128, 4, S], o_a + 36864)
        IQ = at("IQ", [128, 8, S], o_a + 40960)
        Y = at("Y", [128, NB, S], o_a + 49152)
        Yh = at("Yh", [128, NB, S], o_a + 49152, F32R)
        Yl = at("Yl", [128, NB, S], o_a, F32R)
        Mh1 = at("Mh1", [128, NB, S], o_a + 16384, F32R)
        Ml1 = at("Ml1", [128, NB, S], o_a + 32768, F32R)
        IK = at("IK", [128, S], o_acc)
        SC = at("SC", [128, 384], o_acc + 1024)
        TK = at("TK", [128, 2, 22], o_acc + 2560)
        LF = at("LF", [128, 2, 6], o_acc + 2752)
        CQ = at("CQ", [128, 2, 6], o_acc + 2816)
        SMALL = at("SMALL", [128, 6, 16], o_acc + 2880)
        hot = at("hot", [32, 384], o_tg)
        relb = at("relb", [32, 32], o_tg + 1536)
        gsb = at("gsb", [32, 384], o_tg + 2048)
        LPS = at("LPS", [128, 8, 16], o_lp)
        CS = at("CS", [128, NB], o_sm + 256)
        SPH = at("SPH", [128, NB], o_sm + 320)

        bank = [nc.alloc_psum_tensor(f"bank{i}", [128, 512], F32) for i in range(3)]
        pS2 = nc.alloc_psum_tensor("pS2", [128, 2, 512], F32)
        pS = pS2[:, 0, :]
        pT, pO, pM = (nc.alloc_psum_tensor(f"p{i}", [128, 512], F32) for i in "TOM")
        gdram = nc.dram_tensor("gtab", (32, 384), F32, kind="Internal").ap()

        prog = {e: [] for e in ("pe", "act", "dve", "pool", "sp")}
        sems = {e: ctx.enter_context(nc.semaphore(f"s_{e}")) for e in ("pe", "act", "dve", "pool")}
        names = {id(s): e for e, s in sems.items()}
        count = {}
        reached = {}

        def dma_sem(name):
            return ctx.enter_context(nc.semaphore(name))

        def signal(sem, by):
            count[id(sem)] = count.get(id(sem), 0) + by
            return sem, count[id(sem)]

        def wait(e, toks):
            for sem, v in toks:
                if reached.get((e, id(sem)), 0) < v:
                    reached[(e, id(sem))] = v
                    prog[e].append(lambda eng, sem=sem, v=v: eng.wait_ge(sem, v))

        def op(e, fn, *toks):
            wait(e, toks)
            sem = sems[e]
            tok = signal(sem, 1)
            prog[e].append(lambda eng: fn(eng).then_inc(sem, 1))
            if e == "pe":
                st["pe"] = tok
            return tok

        def quiet(e, fn, *toks):
            wait(e, toks)
            prog[e].append(fn)

        def dma(e, out, in_, sem, *toks):
            wait(e, toks)
            tok = signal(sem, 16)
            prog[e].append(lambda eng: eng.dma_start(out, in_).then_inc(sem, 16))
            return tok

        def tt(e, out, a, b, o, *toks):
            return op(e, lambda g: g.tensor_tensor(out, a, b, o), *toks)

        def ts(e, out, a, s1, o1, s2, o2, *toks):
            if o2 is None:
                return op(e, lambda g: g.tensor_scalar(out, a, s1, None, o1), *toks)
            return op(e, lambda g: g.tensor_scalar(out, a, s1, s2, o1, o2), *toks)

        def stt(out, a, s, b, o0, o1, *toks):
            return op("dve", lambda g: g.scalar_tensor_tensor(out=out, in0=a, scalar=s, in1=b, op0=o0, op1=o1), *toks)

        def act(out, in_, f, *toks, **kw):
            return op("act", lambda g: g.activation(out, in_, f, **kw), *toks)

        def over(ap, n):
            a = list(ap.ap)
            return bass.AP(tensor=ap.tensor, offset=ap.offset, ap=[list(a[0]), [0, n]] + [list(z) for z in a[1:]])

        def spread(ap, n):
            return bass.AP(tensor=ap.tensor, offset=ap.offset, ap=[list(ap.ap[0]), [0, n]])

        def mirrored(ap):
            a = [list(z) for z in ap.ap]
            step, n = a[-1]
            return bass.AP(tensor=ap.tensor, offset=ap.offset + step * (n - 1), ap=a[:-1] + [[-step, n]])

        def v32(ap):
            return ap.bitcast(F32)

        stream = []
        s_raw = [dma_sem(f"s_raw{i}") for i in range(NRAW)]
        raw_free = [[] for _ in range(NRAW)]
        sp_free = [[] for _ in range(NSP)]
        landed = {}
        st = {"dma": 0, "split": 0, "w": 0, "main": 0, "tick": 0, "pe": None, "span": 2}
        ready = {}
        acc_free = [[], []]
        modtok = {}

        released = set()

        def pump():
            while st["dma"] < len(stream) and (st["dma"] < NRAW or st["dma"] - NRAW in released):
                i = st["dma"]
                r = i % NRAW
                n = stream[i]["n"]
                landed[i] = dma("sp", raw[r][:, 0:n], stream[i]["src"], s_raw[r], *raw_free[r])
                st["dma"] += 1

        def release(i, toks):
            raw_free[i % NRAW] = toks
            released.add(i)
            pump()

        def push_split():
            i = st["split"]
            el = stream[i]
            r = i % NRAW
            assert i in landed
            kind = el["kind"]
            if kind == "w":
                s = el["slot"]
                n = el["n"]
                th = act(whi[:, s, 0:n], raw[r][:, 0:n], ACT.Copy, landed[i], *sp_free[s])
                tl = tt("dve", wlo[:, s, 0:n], raw[r][:, 0:n], v32(whi[:, s, 0:n]), ALU.subtract, landed[i], th, *sp_free[s])
                ready[i] = [th, tl]
                release(i, [th, tl])
            elif kind == "ada":
                g, kt = el["g"], el["kt"]
                k = g % 2 if g < 4 else 0
                ac = acc[k]
                cs = CS[:, kt:kt + 1]
                if kt == 0:
                    t = ts("dve", ac[:, :], raw[r][:, :], cs, ALU.mult, None, None, landed[i], t_cs, *acc_free[k])
                else:
                    t = stt(ac[:, :], raw[r][:, :], cs, ac[:, :], ALU.mult, ALU.add, landed[i], ada_last[0])
                ada_last[0] = t
                release(i, [t])
                if kt == NB - 1:
                    def fold(g=g, t=t, k=k, ac=ac):
                        for j in range(8):
                            o, w = pM[:, j:j + 1], ac[:, j * 128:(j + 1) * 128]
                            f = lambda e, o=o, w=w: e.matmul(o, w, ones[:, 0:1], start=True, stop=True)
                            if j < 7:
                                quiet("pe", f, t, t_cst, *free["M"])
                            else:
                                tp = op("pe", f, t)
                        tm = tt("dve", mod[:, 8 * g:8 * g + 8], pM[:, 0:8], vec[:, V_ADA + 8 * g:V_ADA + 8 * g + 8],
                                ALU.add, tp, t_vec)
                        free["M"] = [tm]
                        acc_free[k] = [tp]
                        modtok[g] = tm
                    if g < 4:
                        fold()
                    else:
                        defer(2, fold)
            elif kind == "mem":
                q = el["q"]
                mh, ml = el["dst"]
                src = raw[r][:, :].rearrange("p (b s) -> p b s", b=4)
                wt = el["after"]()
                th = act(mh[:, 4 * q:4 * q + 4, :], src, ACT.Copy, landed[i], *wt)
                tl = tt("dve", ml[:, 4 * q:4 * q + 4, :], src, v32(mh[:, 4 * q:4 * q + 4, :]), ALU.subtract, landed[i], th, *wt)
                release(i, [th, tl])
                el["done"][q] = [th, tl]
            st["split"] += 1

        def ensure(i):
            while st["split"] <= i and st["split"] < len(stream):
                push_split()

        jobs = deque()
        flight = []
        later = []
        subs = []

        def rest_of(r):
            for n, fn in enumerate(f for f in r or () if f):
                subs.append((st["tick"] + 1 + n, fn))

        def run_subs(upto=None):
            while subs and (upto is None or min(x[0] for x in subs) <= upto):
                x = min(subs, key=lambda x: x[0])
                subs.remove(x)
                x[1]()

        def advance():
            run_subs()
            for j in list(flight):
                rest_of(j["steps"][j["at"]]())
                j["at"] += 1
                if j["at"] == len(j["steps"]):
                    flight.remove(j)
            if jobs:
                j = {"steps": jobs.popleft(), "at": 0}
                rest_of(j["steps"][0]())
                j["at"] = 1
                if j["at"] < len(j["steps"]):
                    flight.append(j)

        def tick():
            st["tick"] += 1
            due = [x for x in later if x[0] <= st["tick"]]
            for x in due:
                later.remove(x)
                x[1]()
            run_subs(st["tick"])
            if st["tick"] % st["span"] == 0:
                advance()

        def flush_later():
            while later:
                later.sort(key=lambda x: x[0])
                later.pop(0)[1]()

        def drain_jobs():
            while jobs or flight or subs:
                advance()

        def defer(n, fn):
            later.append((st["tick"] + n, fn))

        free = {k: [] for k in ("S", "T", "O", "M", "TG0", "TG1", "TG2", "TG3", "BT0", "BT1", "PT0", "PT1",
                                "LP0", "LP1", "LP2", "SM0", "SM1", "SM2", "SM3")}
        main_free = [[] for _ in range(3)]

        steps = []

        def unit(src, u, nkc, xact, evac, mode="f", kt0=0, width=256, kc0=0):
            steps.append(("unit", dict(src=src, u=u, nkc=nkc, x=xact, evac=evac, mode=mode, kt0=kt0, width=width, kc0=kc0)))

        def call(fn):
            steps.append(("call", fn))

        def run_unit(s):
            b = st["main"] % 3
            st["main"] += 1
            ps = bank[b]
            x = s["x"]()
            wait("pe", main_free[b])
            first = True
            width = s["width"]
            last = None
            for c in range(s["nkc"]):
                i = s["ids"][c]
                el = stream[i]
                ensure(s["ahead"][c])
                wait("pe", ready[i])
                slot = el["slot"]
                mms = []
                for k in range(4):
                    kt = s["kt0"] + 4 * c + k
                    for t in x["toks"][kt]:
                        mms.append(("w", t))
                    w0 = k * width

                    def feat(col, o, kt=kt, w0=w0):
                        h, l = whi[:, slot, w0 + col:w0 + col + 128], wlo[:, slot, w0 + col:w0 + col + 128]
                        xh, xl = x["hi"][:, kt, :], x["lo"][:, kt, :]
                        mms.extend([("m", o, h, xh), ("m", o, h, xl), ("m", o, l, xh)])

                    def toks(col, n, stride, off, kt=kt, w0=w0):
                        h, l = whi[:, slot, w0 + col:w0 + col + n], wlo[:, slot, w0 + col:w0 + col + n]
                        for t in range(2):
                            o = ps[:, off + t * stride:off + t * stride + n]
                            xh = x["hi"][:, kt, t * 128:(t + 1) * 128]
                            xl = x["lo"][:, kt, t * 128:(t + 1) * 128]
                            mms.extend([("m", o, xh, h), ("m", o, xh, l), ("m", o, xl, h)])

                    if s["mode"] == "f":
                        feat(0, ps[:, 0:256])
                        feat(128, ps[:, 256:512])
                    elif s["mode"] == "t":
                        toks(0, 256, 256, 0)
                    else:
                        h, l = whi[:, slot, w0:w0 + width], wlo[:, slot, w0:w0 + width]
                        xh, xl = x["hi"][:, kt, :], x["lo"][:, kt, :]
                        o = ps[0:width, 0:256]
                        mms.extend([("m", o, h, xh), ("m", o, h, xl), ("m", o, l, xh)])
                endm = max(j for j, m in enumerate(mms) if m[0] == "m")
                for j, m in enumerate(mms):
                    if m[0] == "w":
                        wait("pe", [m[1]])
                        continue
                    fn = lambda e, m=m, f=first, z=(c == s["nkc"] - 1 and j == endm): e.matmul(
                        m[1], m[2], m[3], start=f, stop=z, skip_group_check=True)
                    first = False
                    if j == endm:
                        last = op("pe", fn)
                    else:
                        quiet("pe", fn)
                sp_free[slot] = [last]
                if c < s["nkc"] - 1:
                    tick()
            main_free[b] = s["evac"](ps, last)
            tick()

        s_in = dma_sem("s_in")
        s_in2 = dma_sem("s_in2")
        s_hot = dma_sem("s_hot")
        s_g = dma_sem("s_g")
        t_vec = dma("pool", vec[:, :], d_vec, s_in)
        t_cst = dma("pool", cst[:, :], d_cst, s_in2)
        dma("pool", hot[:, :], d_hot, s_hot)
        t_hot = dma("pool", relb[:, :], d_relb, s_hot)
        s_x = dma_sem("s_x")
        t_x = dma("pool", RES[:, :, :], d_x, s_x)
        ada_last = [None]

        def v(c, n=1):
            return vec[:, c:c + n]

        t0 = act(LPS[:, 0, :], v(V_C, 16), ACT.Tanh, t_vec, scale=0.5)
        t0 = stt(LPS[:, 1, :], LPS[:, 0, :], 1.0, v(V_C, 16), ALU.add, ALU.mult, t0)
        t_cs = ts("dve", CS[:, :], LPS[:, 1, :], 0.5, ALU.mult, None, None, t0)

        def log1p_exp(tmp, z_abs, n, tz):
            e, d, s, q, p = (tmp(i) for i in range(5))
            t = act(e, z_abs, ACT.Exp, tz, scale=-1.0)
            t = ts("dve", d, e, 2.0, ALU.add, None, None, t)
            t = op("dve", lambda g: g.reciprocal(d, d), t)
            t = tt("dve", s, e, d, ALU.mult, t)
            t = tt("dve", q, s, s, ALU.mult, t)
            t = ts("dve", p, q, 1.0 / 17, ALU.mult, None, None, t)
            for k in (15, 13, 11, 9, 7, 5, 3):
                t = stt(p, p, 1.0 / k, q, ALU.add, ALU.mult, t)
            t = stt(p, p, 1.0, s, ALU.add, ALU.mult, t)
            return p, t

        t1 = stt(LPS[:, 2, :], v(V_LAM, 16), -1.0, v(V_LAM, 16), ALU.mult, ALU.max, t_vec)
        p, t1 = log1p_exp(lambda i: LPS[:, 3 + i, :], LPS[:, 2, :], 16, t1)
        t2 = ts("dve", LPS[:, 2, :], v(V_LAM, 16), -1.0, ALU.mult, 0.0, ALU.max, t1)
        t2 = stt(LPS[:, 3, :], p, 2.0, LPS[:, 2, :], ALU.mult, ALU.add, t2)
        t_sp = ts("dve", SPH[:, :], LPS[:, 3, :], -2.0, ALU.mult, None, None, t2)
        t_half = ts("dve", vec[:, V_BA:V_BA + 32], vec[:, V_BA:V_BA + 32], 0.5, ALU.mult, None, None, t_vec)

        tg = op("pe", lambda e: e.matmul(pT[0:32, 0:384], relb[:, :], hot[:, :], start=True, stop=True), t_hot)
        tg = op("dve", lambda e: e.tensor_copy(gsb[:, :], pT[0:32, 0:384]), tg)
        tga = op("pool", lambda e: e.memset(gsb[:, 0:128], NEG), tg)
        tgb = op("pool", lambda e: e.memset(gsb[:, 256:384], NEG), tg)
        free["T"] = [tg]
        t_g = dma("pool", gdram, gsb[:, :], s_g, tga, tgb)
        free["TG0"] = free["TG1"] = [t_g]

        def stat_sq(j, src, tok):
            k = j % 2
            tq = act(TG[:, k, :], src, ACT.Square, tok, *free[f"TG{k}"])

            def mm():
                stat_mm(j, TG[:, k, :], tq)
                free[f"TG{k}"] = [st["stat"]]
            return mm

        def stat_mm(j, src, tq):
            wt = free["S"] if j == 0 else []
            quiet("pe", lambda e: e.matmul(pS[:, 0:256], ones, src[:, 0:256], start=(j == 0), stop=False,
                                           skip_group_check=True), tq, t_cst, *wt)
            st["stat"] = op("pe", lambda e: e.matmul(pS[:, 0:256], ones, src[:, 256:512], start=False, stop=(j == 7),
                                                     skip_group_check=True), tq)

        def pair(t, j):
            return t[:, 2 * j:2 * j + 2, :].rearrange("p b s -> p (b s)")

        sumS, sumT = (LP[:, i, :, :].rearrange("p a s -> p (a s)") for i in range(2))

        def total(bk, key, acc_, src, t_src, mark):
            for n, (x, t) in enumerate(((acc_, st[key]), (src, t_src))):
                for h in range(2):
                    tp = op("pe", lambda e, x=x, h=h, n=n: e.matmul(
                        bk[:, 0:256], ones, x[:, h * 256:(h + 1) * 256], start=(n == 0 and h == 0), stop=(n == 1 and h == 1),
                        skip_group_check=True), t, t_cst, *free["S" if bk is pS else "T"])
            st[mark] = tp

        def square_up(j, tok):
            src = pair(RES, j)
            if j == 0:
                st["sqs"] = act(sumS, src, ACT.Square, tok, *free["LP0"], *free["LP1"])
                return
            k = j % 2
            tq = act(TG[:, k, :], src, ACT.Square, tok, *free[f"TG{k}"])
            if j < 7:
                st["sqs"] = tt("pool", sumS, sumS, TG[:, k, :], ALU.add, tq, st["sqs"])
                free[f"TG{k}"] = [st["sqs"]]
            else:
                total(pS, "sqs", sumS, TG[:, k, :], tq, "stat")
                free[f"TG{k}"] = [st["stat"]]
                free["LP0"] = [st["stat"]]

        Rv, R2, R3, R4 = (BT[:, 0, 0, :], BT[:, 0, 1, :], BT[:, 1, 0, :], BT[:, 1, 1, :])

        def rstd(eps, dm2=None, zm=()):
            w = free["BT0"] + free["BT1"]
            t = ts("dve", R2, pS[:, 0:256], 1.0 / D, ALU.mult, eps, ALU.add, st["stat"], *w)
            free["S"] = [t]
            if dm2:
                t = tt("dve", R2, R2, R3, ALU.subtract, t, dm2)
            t = op("dve", lambda g: g.reciprocal(R3, R2), t)
            t = act(R4, R3, ACT.Sqrt, t, *zm)
            t = tt("dve", R3, R4, R4, ALU.mult, t)
            t = tt("dve", R3, R3, R2, ALU.mult, t)
            t = ts("dve", R3, R3, -0.5, ALU.mult, 1.5, ALU.add, t)
            t = tt("dve", Rv, R4, R3, ALU.mult, t)
            free["BT0"] = free["BT1"] = []
            return t

        hact = {"hi": Hhi, "lo": Hlo, "toks": [[] for _ in range(NB)]}
        restok = [[] for _ in range(NB)]

        def tslot(b):
            k = 2 + (b // 2) % 2
            return TG[:, k, (b % 2) * 256:(b % 2) * 256 + 256], f"TG{k}{b % 2}"

        tfree = {}

        def close_t():
            for k in (2, 3):
                free[f"TG{k}"] = tfree.pop(f"TG{k}0", []) + tfree.pop(f"TG{k}1", [])
        def emit_h(b, kind, tr, g, sh, last_read, tmod=()):
            wh = [last_read] if last_read else []
            hi, lo, r = Hhi[:, b, :], Hlo[:, b, :], RES[:, b, :]
            if kind == "rms":
                t = stt(r, r, g, Rv, ALU.mult, ALU.mult, tr, t_vec, *restok[b])
                restok[b] = [t]
                th = act(hi, r, ACT.Copy, t, *wh)
                tl = tt("dve", lo, r, v32(hi), ALU.subtract, th, t, *wh)
                hact["toks"][b] = [th, tl]
                restok[b] = [t]
                return [t, th, tl]
            sl, key = tslot(b)
            w = tfree.get(key, free["TG2"] + free["TG3"])
            t = stt(sl, r, g, Rv, ALU.mult, ALU.mult, tr, t_vec, *tmod, *w, *restok[b])
            out = []
            if kind in ("ln", "out"):
                tx = act(r, sl, ACT.Identity, t, bias=sh)
                restok[b] = [tx]
                out.append(tx)
            if kind == "out":
                tfree[key] = [tx]
                return out
            th = act(hi, sl, ACT.Identity, t, *wh, bias=sh)
            tl = stt(lo, sl, sh, v32(hi), ALU.add, ALU.subtract, t, th, *wh)
            tfree[key] = [th, tl]
            hact["toks"][b] = [th, tl]
            return out + [t, th, tl]

        PERM = []
        for b in range(16):
            PERM.append((b, 8 + b) if b < 8 else (8 + b, 16 + b))

        w_in, w_lo, w_ao, w_o, w_f1, w_f2 = (d_w[k] for k in ("in", "lru_out", "attn_out", "out", "ff1", "ff2"))

        XR = at("XR", [128, NB, S], o_a + 32768)
        xrtok = []

        def x_first():
            for j in range(8):
                stat_sq(j, pair(RES, j), t_x)()
            tr = rstd(EPS)
            for j in range(8):
                xrtok.append(tt("dve", XR[:, 2 * j:2 * j + 2, :], RES[:, 2 * j:2 * j + 2, :], over(Rv, 2), ALU.mult, tr, t_x))

        def norm1():
            tm = stt(A1v[:, :], mod[:, 16:32], 1.0, v(V_N1, 16), ALU.add, ALU.mult, modtok[2], modtok[3], t_vec)
            for b in range(NB):
                restok[b] = [t_x]
                sl, key = tslot(b)
                w = tfree.get(key, free["TG2"] + free["TG3"])
                g, sh, hi, lo = A1v[:, b:b + 1], mod[:, b:b + 1], Hhi[:, b, :], Hlo[:, b, :]
                th = act(hi, XR[:, b, :], ACT.Identity, xrtok[b // 2], tm, modtok[b // 8], scale=g, bias=sh)
                t = ts("dve", sl, XR[:, b, :], g, ALU.mult, sh, ALU.add, xrtok[b // 2], tm, modtok[b // 8], *w)
                tl = tt("dve", lo, sl, v32(hi), ALU.subtract, t, th)
                tfree[key] = [tl]
                hact["toks"][b] = [th, tl]
            close_t()
            st["norm_done"] = hact["toks"][NB - 1]
        call(norm1)

        xctok = [[] for _ in range(NB)]

        def evac_lrux(j):
            def f(ps, tp):
                out = []
                for i in range(2):
                    b = 2 * j + i
                    o = XC[:, b, :]
                    p_ = ps[:, i * 256:(i + 1) * 256]
                    t = ts("dve", o, p_, v(V_CW + 48 + b), ALU.mult, v(V_CB + b), ALU.add, tp, t_vec)
                    for k in (2, 1, 0):
                        s = 3 - k
                        t = stt(o[:, s:S], p_[:, 0:S - s], v(V_CW + 16 * k + b), o[:, s:S], ALU.mult, ALU.add, t)
                    xctok[b] = [t]
                    out.append(t)
                return [out[-1]]
            return f

        def X():
            return hact
        for j in range(8):
            unit(w_in, j, 4, X, evac_lrux(j))

        qtok = [[] for _ in range(NB)]

        def evac_q(j):
            def f(ps, tp):
                src = mirrored(ps[:, :].rearrange("p (a q) -> p a q", q=128))
                t = act(pair(AT, j).rearrange("p (a q) -> p a q", q=128), src, ACT.Copy, tp)
                qtok[2 * j] = qtok[2 * j + 1] = [t]
                return [t]
            return f

        def evac_copy(dst, tokl, j, e="act"):
            def f(ps, tp):
                t = act(pair(dst, j), ps[:, :], ACT.Copy, tp)
                tokl[2 * j] = [t]
                tokl[2 * j + 1] = [t]
                return [t]
            return f
        LW = [at(f"LW{c}", [128, CH], o_lp + 4096 * c if c < 3 else o_kv + 4096) for c in range(4)]
        s_lw = dma_sem("s_lw")
        lwtok = []

        def lru_weights():
            for c in range(4):
                t = dma("pool", LW[c][:, :], d_lru[c], s_lw, *st["norm_done"])
            lwtok.append(t)
        call(lru_weights)
        mmtok = [[] for _ in range(NB)]
        aatok = [[] for _ in range(NB)]

        def lru_gates(j):
            def f():
                w = LW[j // 2][:, :].rearrange("p (b g m) -> p b g m", b=4, g=2)
                tps = []
                for g, bk, key in ((0, pS, "S"), (1, pT, "T")):
                    for h in range(2):
                        b = 2 * j + h
                        fn = lambda e, g=g, h=h, b=b, bk=bk: e.matmul(
                            bk[:, h * 256:(h + 1) * 256], w[:, b % 4, g, :], XC[:, b, :], start=(h == 0), stop=True,
                            skip_group_check=True)
                        if h == 0:
                            quiet("pe", fn, lwtok[0], *free[key], *xctok[b])
                        else:
                            tps.append(op("pe", fn, *xctok[b]))
                if j == 7:
                    for k in ("LP0", "LP1", "LP2", "PT0", "PT1", "BT0", "BT1"):
                        free[k] = [tps[1]]

                def gates():
                    tg_ = []
                    for g, bk in ((0, pS), (1, pT)):
                        for h in range(2):
                            b = 2 * j + h
                            t = act(TG[:, g, h * 256:(h + 1) * 256], bk[:, h * 256:(h + 1) * 256], ACT.Tanh, tps[g], t_half,
                                    *free[f"TG{g}"], bias=v(V_BA + 16 * g + b), scale=0.5)
                        tg_.append(t)
                    free["S"], free["T"] = [tg_[0]], [tg_[1]]
                    h_, rc = pair(MM, j), TG[:, 2 + j % 2, :]
                    key = f"TG{2 + j % 2}"
                    for h in range(2):
                        b = 2 * j + h
                        tt_ = act(MM[:, b, :], TG[:, 0, h * 256:(h + 1) * 256], ACT.Tanh, tg_[0], t_sp,
                                  scale=SPH[:, b:b + 1], bias=SPH[:, b:b + 1])
                    free["TG0"] = [tt_]
                    tu = stt(pair(XC, j), TG[:, 1, :], 1.0, pair(XC, j), ALU.add, ALU.mult, tg_[1], tps[1])
                    free["TG1"] = [tu]
                    defer(1, lambda: roots(h_, rc, key, tt_, tu))

                def roots(h_, rc, key, tt_, tu):
                    td = ts("dve", rc, h_, -1.0, ALU.mult, 1.0, ALU.add, tt_, *free[key])
                    td = op("dve", lambda e: e.reciprocal(rc, rc), td)
                    ta = ts("dve", pair(AA, j), rc, 2.0, ALU.mult, -1.0, ALU.add, td)
                    td = op("dve", lambda e: e.memset(rc.rearrange("p (b s) -> p b s", b=2)[:, :, 0:1], 1.0), ta)
                    tu = tt("dve", pair(XC, j), pair(XC, j), rc, ALU.mult, td, tu)
                    free[key] = [tu]
                    for h in range(2):
                        xctok[2 * j + h] = [tu]
                        aatok[2 * j + h] = [ta]
                        mmtok[2 * j + h] = [td]
                defer(1, gates)
            return f

        def lru_scan():
            def part(q):
                sl = MM[:, 4 * q:4 * q + 4, :]
                t = act(sl, sl, ACT.Sqrt, *mmtok[4 * q + 3], scale=-1.0)
                t2_ = op("dve", lambda e, q=q: e.memset(MM[:, 4 * q:4 * q + 4, 0:1], 0.5), t)
                t3 = tt("dve", XC[:, 4 * q:4 * q + 4, :], XC[:, 4 * q:4 * q + 4, :], sl, ALU.mult, t2_, t,
                        *xctok[4 * q + 3])
                for b in range(4 * q, 4 * q + 4):
                    mmtok[b] = [op("dve", lambda e, b=b: e.tensor_tensor_scan(
                        MM[:, b, :], AA[:, b, :], XC[:, b, :], 0.0, ALU.mult, ALU.add), t3, *aatok[b])]
            for q in range(4):
                defer(2 * q, lambda q=q: part(q))

        ktok = [[], []]
        for j in range(8):
            unit(w_in, 8 + j, 4, X, evac_q(j))
            if j < 7:
                call(lambda j=j: defer(1, lru_gates(j)))
            if j == 6:
                call(lambda: defer(3, lru_gates(7)))
        unit(w_in, 16, 4, X, evac_copy(KT, ktok, 0))
        call(lambda: defer(1, lru_scan))
        vtok = [[]]

        def evac_tok(dst, c0, tokl, n=256):
            def f(ps, tp):
                t = act(dst[:, :, c0:c0 + n], ps[:, :].rearrange("p (t c) -> p t c", t=2), ACT.Copy, tp)
                tokl[0] = [t]
                return [t]
            return f
        unit(w_in, 17, 4, X, evac_tok(VT, 0, vtok), mode="t")

        s_bt = [dma_sem("s_bt0"), dma_sem("s_bt1")]
        jn = [0]

        def attn_steps(heads, nk, scale, bias, out, sink=None, pre=None, outtok=None, d64=False):
            n = jn[0]
            jn[0] += 1
            nkt = nk // 128
            L = LP[:, n % 3, :, 0:nk]
            lp, pt, sm = f"LP{n % 3}", f"PT{n % 2}", f"SM{n % 4}"
            mx, nm, rs, es, rd = (SM[:, n % 4, i, :] for i in range(5))
            Tv = pT[:, 0:2 * nkt * 128].rearrange("p (a q) -> p a q", q=128)
            Pv = PT[:, n % 2, 0:2 * nkt, :]
            s = {}

            def s0():
                bi, bt = (None, []) if bias is None else bias()
                for i, (q, k, _, tk) in enumerate(heads()):
                    fn = lambda e, q=q, k=k, i=i: e.matmul(pS2[:, i, 0:nk], q, k, start=True, stop=True,
                                                           skip_group_check=True)
                    tp = op("pe", fn, *tk, *free["S"])

                def logits():
                    sv = pS2[:, :, 0:nk]
                    if bi is None:
                        t = ts("dve", L, sv, scale, ALU.mult, None, None, tp, *free[lp])
                    else:
                        t = stt(L, sv, scale, bi, ALU.mult, ALU.add, tp, *bt, *free[lp])
                    s["bias_read"] = t
                    free["S"] = [t]
                    if pre:
                        pre(t)
                    if sink is None:
                        t = op("dve", lambda e: e.tensor_reduce(nm, L, AX.X, ALU.max, negate=True), t, *free[sm])
                    else:
                        t = op("dve", lambda e: e.tensor_reduce(mx, L, AX.X, ALU.max), t, *free[sm])
                        t = tt("dve", mx, mx, sink, ALU.max, t, t_vec)
                        t = ts("dve", nm, mx, -1.0, ALU.mult, None, None, t)
                        s["es"] = tt("dve", es, sink, nm, ALU.add, t)
                    s["nm"] = t

                def exps():
                    t = s["nm"]
                    for i in range(2):
                        te = op("act", lambda e, i=i: e.activation(L[:, i, :], L[:, i, :], ACT.Exp, bias=nm[:, i:i + 1],
                                                                   accum_out=rs[:, i:i + 1]), t)
                    if sink is not None:
                        te = act(es, es, ACT.Exp, s["es"])
                    s["e"] = te
                return [logits, exps] if st["span"] > 2 else [lambda: (logits(), exps())]

            def s1():
                t = s["e"]
                if sink is not None:
                    t = tt("dve", rs, rs, es, ALU.add, t)
                t = op("dve", lambda e: e.reciprocal(rd, rs), t)
                for i in range(2):
                    t2_ = act(L[:, i, :], L[:, i, :], ACT.Copy, t, scale=rd[:, i:i + 1])
                free[sm] = [t2_]
                s["p"] = t2_

            def s2():
                for i in range(2):
                    for k in range(nkt):
                        a = i * nkt + k
                        fn = lambda e, i=i, k=k, a=a: e.transpose(Tv[:, a, :], L[:, i, k * 128:(k + 1) * 128], ident)
                        tp = op("pe", fn, s["p"], t_cst, *free["T"])
                free[lp] = [tp]

                def copy():
                    t = act(Pv, Tv, ACT.Copy, tp, *free[pt])
                    free["T"] = [t]
                    s["pt"] = t
                return [copy]

            def s3():
                hs = heads()
                for i in range(2):
                    o = pO[i * 64:(i + 1) * 64, 0:128] if d64 else pO[:, i * 128:(i + 1) * 128]
                    for k in range(nkt):
                        fn = lambda e, i=i, k=k, o=o, w=hs[i][2][k]: e.matmul(
                            o, w, Pv[:, i * nkt + k, :], start=(k == 0), stop=(k == nkt - 1), skip_group_check=True)
                        tp = op("pe", fn, s["pt"], *hs[i][3], *free["O"])
                free[pt] = [tp]
                src = mirrored(pO[:, 0:128]) if d64 else pO[:, 0:256].rearrange("p (a q) -> p a q", a=2)
                t = act(out, src, ACT.Copy, tp, *(s.get("war", [])))
                free["O"] = [t]
                outtok(t)
            return [s0, s1, s2, s3], s

        bt_at = {}
        ytok = [[] for _ in range(NB)]
        qk_done = {}

        def load_bt(b):
            def f():
                k = b % 2
                for i, h in enumerate(PERM[b]):
                    src = bass.AP(tensor=gdram.tensor, offset=h * 384, ap=[[1, 128], [1, 256]])
                    t = dma("pool", BT[:, k, i, :], src, s_bt[k], t_g, *free[f"BT{k}"])
                bt_at[b] = t
            return f

        def att_jobs():
            st["span"] = 3
            load_bt(0)()
            load_bt(1)()
            for b in range(NB):
                grp = b // 8
                for t in (0, 1):
                    nk = 128 * (t + 1)

                    def heads(b=b, t=t, nk=nk, grp=grp):
                        out = []
                        for i in range(2):
                            r = slice(64 * i, 64 * i + 64)
                            g = 2 * grp + i
                            out.append((AT[r, b, t * 128:(t + 1) * 128], KT[r, grp, 0:nk],
                                        [VT[:, k, g * 64:(g + 1) * 64] for k in range(t + 1)],
                                        [*qtok[b], *ktok[0], *vtok[0]]))
                        return out

                    def bias(b=b, t=t, nk=nk):
                        return BT[:, b % 2, :, 256 - nk:256], [bt_at[b]]

                    def pre(tok, b=b, t=t):
                        if t == 1:
                            free[f"BT{b % 2}"] = [tok]
                            if b + 2 < NB:
                                load_bt(b + 2)()

                    def done(tok, b=b):
                        ytok[b] = ytok[b] + [tok]
                    js, _ = attn_steps(heads, nk, SC1, bias, AT[:, b, t * 128:(t + 1) * 128],
                                       sink=v(V_SINK + 2 * b, 2), pre=pre, outtok=done, d64=True)
                    jobs.append(js)
        call(att_jobs)

        G0, G1 = 2 * 0.7978845608028654, 2 * 0.7978845608028654 * 0.044715
        ztok = [[] for _ in range(NB)]
        zact = {"hi": Zh, "lo": Zl, "toks": ztok}

        def split_out(hi, lo, src, t, key, *w):
            th = act(hi, src, ACT.Copy, t, *w)
            tl = tt("dve", lo, src, v32(hi), ALU.subtract, t, th, *w)
            free[key] = [th, tl]
            return [th, tl]

        def evac_gate(j):
            def f(ps, tp):
                g0, g1, g2 = TG[:, 0, :], TG[:, 1, :], TG[:, 2, :]
                t = act(g0, ps[:, :], ACT.Square, tp, *free["TG0"])
                t = ts("dve", g0, g0, 0.5 * G1, ALU.mult, 0.5 * G0, ALU.add, t)
                t = tt("dve", g0, g0, ps[:, :], ALU.mult, t)
                t = act(g1, g0, ACT.Tanh, t, *free["TG1"])
                free["TG0"] = [t]
                t = stt(g1, g1, 1.0, ps[:, :], ALU.add, ALU.mult, t)
                fr = [t]
                t = stt(g2, g1, 0.5, pair(MM, j), ALU.mult, ALU.mult, t, *mmtok[2 * j + 1], *free["TG2"])
                free["TG1"] = [t]
                tk = split_out(pair(Zh, j), pair(Zl, j), g2, t, "TG2", *mmtok[15])
                ztok[2 * j] = ztok[2 * j + 1] = tk
                mmtok[2 * j] = mmtok[2 * j + 1] = [t]
                return fr
            return f
        gtok = [[] for _ in range(NB)]

        def evac_sig(dst, j, war):
            def f(ps, tp):
                t = act(pair(dst, j), ps[:, :], ACT.Tanh, tp, *war(j), scale=0.5)
                gtok[2 * j] = gtok[2 * j + 1] = [t]
                return [t]
            return f

        def evac_ya(j):
            def f(ps, tp):
                t = stt(pair(MM, j), pair(MM, j), 1.0, ps[:, :], ALU.add, ALU.mult, tp, *gtok[2 * j])
                mmtok[2 * j] = mmtok[2 * j + 1] = [t]
                return [t]
            return f
        for j in range(8):
            unit(w_in, 18 + j, 4, X, evac_gate(j))
            unit(w_in, 26 + j, 4, X, evac_sig(MM, j, lambda j: mmtok[2 * j]))
        for j in range(8):
            unit(w_lo, j, 4, lambda: zact, evac_ya(j))
        TB = at("TB", [128, NB, S], o_a + 16384)
        for j in range(8):
            unit(w_in, 34 + j, 4, X, evac_sig(TB, j, lambda j: [st["ya_end"]]))
            if j == 0:
                steps.insert(len(steps) - 1, ("call", lambda: st.__setitem__("ya_end", st["pe"])))

        def att_split():
            st["span"] = 2
            flush_later()
            drain_jobs()
            for q in range(4):
                src = AT[:, 4 * q:4 * q + 4, :]
                w = [x for b in range(4 * q, 4 * q + 4) for x in ytok[b]]
                th = act(Hhi[:, 4 * q:4 * q + 4, :], src, ACT.Copy, st["pe"], *w)
                tl = tt("dve", Hlo[:, 4 * q:4 * q + 4, :], src, v32(Hhi[:, 4 * q:4 * q + 4, :]), ALU.subtract, th, st["pe"], *w)
                for b in range(4 * q, 4 * q + 4):
                    hact["toks"][b] = [th, tl]
                st["att_read"] = [th, tl]
        call(att_split)
        Gh = at("Gh", [128, NB, S], o_a, F32R)
        Gl = at("Gl", [128, NB, S], o_a + 32768, F32R)
        mgtok = [[] for _ in range(NB)]
        mact = {"hi": Gh, "lo": Gl, "toks": mgtok}

        def evac_yb(j):
            def f(ps, tp):
                g0, g1 = TG[:, 0, :], TG[:, 1, :]
                t = stt(g0, pair(TB, j), 1.0, ps[:, :], ALU.add, ALU.mult, tp, *gtok[2 * j], *free["TG0"])
                fr = [t]
                t = tt("dve", g1, g0, pair(MM, j), ALU.add, t, *mmtok[2 * j], *free["TG1"])
                free["TG0"] = [t]
                th = act(pair(Gh, j), g1, ACT.Copy, t, *st["att_read"], scale=0.5)
                tl = stt(pair(Gl, j), g1, 0.5, v32(pair(Gh, j)), ALU.mult, ALU.subtract, t, th, st["ya_end"])
                free["TG1"] = [th, tl]
                mgtok[2 * j] = mgtok[2 * j + 1] = [th, tl]
                st["mm_read"] = t
                return fr
            return f
        for j in range(8):
            unit(w_ao, j, 4, X, evac_yb(j))

        def evac_res(j, gcol, stat, gg):
            def f(ps, tp):
                for i in range(2):
                    b = 2 * j + i
                    t = stt(RES[:, b, :], ps[:, i * 256:(i + 1) * 256], mod[:, gcol + b:gcol + b + 1], RES[:, b, :],
                            ALU.mult, ALU.add, tp, modtok[gg[0]], modtok[gg[1]], *restok[b])
                    restok[b] = [t]
                if stat:
                    square_up(j, t)
                return [t]
            return f
        for j in range(8):
            unit(w_o, j, 4, lambda: mact, evac_res(j, 32, True, (4, 5)))

        memtok0 = [None] * 4
        mem0 = {"hi": Mh0, "lo": Ml0}

        def mem_act(m, tk):
            return lambda: {**m, "toks": [tk[k // 4] for k in range(NB)]}
        w_kv, w_2, w_o2 = d_w["kv"], d_w["in2"], d_w["out2"]

        def mem_load(m, tk, after):
            steps.append(("mem", dict(dst=(m["hi"], m["lo"]), done=tk, after=after)))
        mem_load(mem0, memtok0, lambda: [st["mm_read"]])
        kvtok = {"k": [[] for _ in range(4)], "v": [[], []]}
        
        def kv_war():
            return [st["kv_end"]]

        def evac_km(j):
            def f(ps, tp):
                t = act(pair(KM, j), ps[:, :], ACT.Copy, tp, *kv_war())
                kvtok["k"][2 * j] = kvtok["k"][2 * j + 1] = [t]
                return [t]
            return f

        def evac_vm(j):
            def f(ps, tp):
                t = act(VM[:, :, j * 256:(j + 1) * 256], ps[:, :].rearrange("p (t c) -> p t c", t=2), ACT.Copy, tp,
                        *kv_war())
                kvtok["v"][j] = [t]
                return [t]
            return f

        def kv_unit(layer, j, m, tk):
            unit(w_kv, 4 * layer + j, 4, mem_act(m, tk), evac_km(j) if j < 2 else evac_vm(j - 2), mode="f" if j < 2 else "t")

        def norm2():
            last = st["pe"]

            def head():
                tr = rstd(EPS)
                t = stt(A2v[:, :], mod[:, 64:80], 1.0, v(V_N2, 16), ALU.add, ALU.mult, modtok[8], modtok[9], t_vec)
                for q in range(5):
                    def blocks(q=q):
                        for b in range(q * 4, min(NB, q * 4 + 4)):
                            emit_h(b, "mod", tr, A2v[:, b:b + 1], mod[:, 48 + b:49 + b], last,
                                   tmod=[t, modtok[6], modtok[7]])
                        if q == 4:
                            close_t()
                    defer(1 + q, blocks)
            defer(1, head)
        call(norm2)

        call(lambda: st.__setitem__("kv_end", st["pe"]))
        kv_unit(0, 0, mem0, memtok0)
        kv_unit(0, 1, mem0, memtok0)
        call(flush_later)

        ftok = [[[] for _ in range(8)] for _ in range(2)]
        fread = [[], []]

        def evac_ff1(f_, j):
            def f(ps, tp):
                k = f_ % 2
                a, b_ = TG[:, 2 * (j % 2), :], TG[:, 2 * (j % 2) + 1, :]
                ka, kb = f"TG{2 * (j % 2)}", f"TG{2 * (j % 2) + 1}"
                t = act(a, ps[:, :], ACT.Relu, tp, *free[ka])
                fr = [t]
                t = act(b_, a, ACT.Square, t, *free[kb])
                free[ka] = [t]
                tk = split_out(pair(Fh[k], j), pair(Fl[k], j), b_, t, kb, *fread[k])
                ftok[k][2 * j] = ftok[k][2 * j + 1] = tk
                return fr
            return f

        def ff1(f_):
            if f_ < 2:
                call(lambda: fread.__setitem__(f_, [st["ffw"]]))
            for j in range(4):
                unit(w_f1, 4 * f_ + j, 4, X, evac_ff1(f_, j))

        def ff2(f_):
            k = f_ % 2
            for j in range(8):
                unit(w_f2, j, 2, lambda k=k: {"hi": Fh[k], "lo": Fl[k], "toks": ftok[k]},
                     evac_res(j, 80, f_ == 7, (10, 11)), kc0=2 * f_)
            call(lambda k=k: fread.__setitem__(k, [st["pe"]]))
        call(lambda: st.__setitem__("ffw", st["pe"]))
        ff1(0)
        for f_ in range(1, 8):
            ff1(f_)
            ff2(f_ - 1)
        ff2(7)

        def norm3():
            last = st["pe"]

            def head():
                tr = rstd(EPS)
                for q in range(4):
                    def blocks(q=q):
                        for b in range(q * 4, q * 4 + 4):
                            emit_h(b, "rms", tr, v(V_FG + b), None, last)
                    defer(1 + q, blocks)
            defer(1, head)
        call(norm3)
        kv_unit(0, 2, mem0, memtok0)
        kv_unit(0, 3, mem0, memtok0)
        call(flush_later)

        memtok1 = [None] * 4
        mem1 = {"hi": Mh1, "lo": Ml1}

        s_rot = dma_sem("s_rot")

        def layer(l):
            tk = {n: [[] for _ in range(8)] for n in ("DQ", "DK", "FQ", "FK", "MQ", "IQ")}
            tk1 = {n: [[]] for n in ("DV", "FV")}
            s_ = {}
            a_war = lambda: [st["a_end"]]
            call(lambda: st.__setitem__("a_end", st["pe"]))

            def evac_rope(dst, j, cc, name):
                def f(ps, tp):
                    g0, g1, g2 = TG[:, 0, :], TG[:, 1, :], TG[:, 2, :]
                    t = act(g0, ps[:, :], ACT.Copy, tp, *free["TG0"])
                    half = cc[0]
                    for r in range(0, 128, 2 * half):
                        dma("pool", g2[r:r + half, :], g0[r + half:r + 2 * half, :], s_rot, t, *free["TG2"])
                        tr = dma("pool", g2[r + half:r + 2 * half, :], g0[r:r + half, :], s_rot)

                    def rest():
                        v3 = lambda a: a.rearrange("p (b s) -> p b s", b=2)
                        t1_ = tt("dve", v3(g1), v3(g0), over(cst[:, cc[1]:cc[1] + 256], 2), ALU.mult, t, *free["TG1"])
                        t2_ = tt("dve", v3(g2), v3(g2), over(cst[:, cc[2]:cc[2] + 256], 2), ALU.mult, tr)
                        free["TG0"] = [tr, t1_]
                        t3 = tt("dve", pair(dst, j), g1, g2, ALU.add, t1_, t2_, *a_war())
                        free["TG1"] = free["TG2"] = [t3]
                        tk[name][2 * j] = tk[name][2 * j + 1] = [t3]
                    defer(3, rest)
                    return [t]
                return f
            R64 = (32, C_COS64, C_SIN64)
            R128 = (64, C_COS128, C_SIN128)

            def evac_plain(dst, j, name):
                def f(ps, tp):
                    t = act(pair(dst, j), ps[:, :], ACT.Copy, tp, *a_war())
                    tk[name][2 * j] = tk[name][2 * j + 1] = [t]
                    return [t]
                return f

            def evac_v(dst, j, name):
                def f(ps, tp):
                    t = act(dst[:, :, j * 256:(j + 1) * 256], ps[:, :].rearrange("p (t c) -> p t c", t=2), ACT.Copy,
                            tp, *a_war())
                    tk1[name][0] = tk1[name][0] + [t]
                    return [t]
                return f

            def evac_small(ps, tp):
                g0, g1, g2 = TG[0:86, 0, 0:256], TG[:, 1, 0:256], TG[:, 2, 0:256]
                t = act(g0, ps[0:86, 0:256], ACT.Copy, tp, *free["TG0"])

                def rest():
                    k0 = TG[0:64, 0, 0:256]
                    same, swap = cst[0:64, C_DUP:C_DUP + 128], cst[0:64, C_SWAP:C_SWAP + 128]
                    quiet("pe", lambda e: e.matmul(pM[:, 0:256], same, k0, start=True, stop=True, skip_group_check=True),
                          t, t_cst, *free["M"])
                    tq = op("pe", lambda e: e.matmul(pM[:, 256:512], swap, k0, start=False, stop=True,
                                                     skip_group_check=True))
                    t1_ = tt("dve", g1, pM[:, 0:256], cst[:, C_COS64:C_COS64 + 256], ALU.mult, tq, *free["TG1"])
                    t2_ = tt("dve", g2, pM[:, 256:512], cst[:, C_SIN64:C_SIN64 + 256], ALU.mult, tq, *free["TG2"])
                    free["M"] = [t2_]
                    t3 = tt("dve", IK[:, :], g1, g2, ALU.add, t1_, t2_)
                    free["TG1"] = free["TG2"] = [t3]
                    s_["ik"] = t3

                def turn():
                    for n in range(2):
                        tq = op("pe", lambda e, n=n: e.transpose(pM[:, n * 86:n * 86 + 86], TG[0:86, 0, n * 128:n * 128 + 128],
                                                                 cst[0:86, C_ID:C_ID + 86]), t, *free["M"])
                    free["TG0"] = [tq]
                    tw = act(TK[:, :, :], pM[:, 0:172].rearrange("p (t c) -> p t c", t=2)[:, :, 64:86], ACT.Copy, tq)
                    free["M"] = [tw]
                    defer(1, lambda: logs(tw))

                def logs(tw):
                    s_["w"] = ts("dve", TK[:, :, 0:16], TK[:, :, 0:16], 0.25, ALU.mult, None, None, tw)
                    c6 = lambda i: SMALL[:, i, 0:12]
                    z = c6(0).rearrange("p (t h) -> p t h", t=2)
                    bf = v(V_BF + 6 * l, 6)
                    ta = tt("dve", z, TK[:, :, 16:22], over(bf, 2), ALU.add, tw, t_vec)
                    tb = ts("dve", LF[:, :, :], z, 0.0, ALU.min, None, None, ta)
                    ta = stt(c6(0), c6(0), -1.0, c6(0), ALU.mult, ALU.max, tb)
                    p_, ta = log1p_exp(lambda i: c6(1 + i), c6(0), 12, ta)
                    lf = LF[:, :, :].rearrange("p t h -> p (t h)")
                    ta = stt(lf, p_, -2.0, lf, ALU.mult, ALU.add, ta)
                    s_["lf"] = ta
                    defer(2, sums)

                def sums():
                    ta = s_["lf"]
                    quiet("pe", lambda e: e.matmul(pM[:, 0:6], U[:, 0:128], LF[:, 0, :], start=True, stop=True,
                                                   skip_group_check=True), ta, *free["M"])
                    quiet("pe", lambda e: e.matmul(pM[:, 6:12], ones, LF[:, 0, :], start=True, stop=False,
                                                   skip_group_check=True))
                    tq = op("pe", lambda e: e.matmul(pM[:, 6:12], U[:, 0:128], LF[:, 1, :], start=False, stop=True,
                                                     skip_group_check=True))
                    tc = op("dve", lambda e: e.tensor_copy(CQ[:, :, :], pM[:, 0:12].rearrange("p (t h) -> p t h", t=2)), tq)
                    free["M"] = [tc]
                    s_["cq"] = tc
                defer(2, rest)
                defer(3, turn)
                return [t]

            sc_t = [SC[:, 0:128], SC[:, 128:384]]
            sctok = [[], []]

            def idx_steps(t, b):
                nk = 128 * (t + 1)
                n = jn[0]
                jn[0] += 1
                L = LP[:, n % 3, :, 0:nk]
                lp = f"LP{n % 3}"
                x_ = {}

                def s0():
                    for i in range(2):
                        r = slice(64 * i, 64 * i + 64)
                        tp = op("pe", lambda e, i=i, r=r: e.matmul(
                            pS2[:, i, 0:nk], IQ[r, b, t * 128:(t + 1) * 128], IK[r, 0:nk], start=True,
                            stop=True, skip_group_check=True), *tk["IQ"][b], s_["ik"], *free["S"])
                    sv = pS2[:, :, 0:nk]
                    ta = act(L, sv, ACT.Relu, tp, *free[lp], scale=0.125)
                    free["S"] = [ta]
                    x_["a"] = ta

                def s1():
                    ta = x_["a"]
                    for i in range(2):
                        w = TK[:, t, 2 * b + i:2 * b + i + 1]
                        if b == 0 and i == 0:
                            ta = ts("dve", sc_t[t], L[:, 0, :], w, ALU.mult, None, None, ta, s_["w"],
                                    *st.get("sc_read", []))
                        else:
                            ta = stt(sc_t[t], L[:, i, :], w, sc_t[t], ALU.mult, ALU.add, ta, x_["a"], *sctok[t])
                        sctok[t] = [ta]
                    free[lp] = [ta]
                return [s0, s1]

            def causal(ap, t, nk, reps, tok):
                pat = [[-1, nk]] if reps == 1 else [[0, reps], [-1, nk]]
                return op("pool", lambda e: e.affine_select(out=ap, in_=ap, pattern=pat, compare_op=ALU.is_ge, fill=NEG,
                                                            base=128 * t, channel_multiplier=1), *tok)

            def top_steps(t):
                nk = 128 * (t + 1)
                a = sc_t[t]

                def start():
                    sctok[t] = [causal(a, t, nk, 1, sctok[t])]

                def rnd():
                    t_ = op("dve", lambda e: e.max(MX8[:, t, :], a), *sctok[t])
                    sctok[t] = [op("dve", lambda e: e.match_replace(a, MX8[:, t, :], a, TAKEN), t_)]

                def end():
                    t_ = ts("dve", a, a, -2e38, ALU.is_ge, NEG, ALU.mult, *sctok[t])
                    sctok[t] = [causal(a, t, nk, 1, [t_])]
                return [[start, rnd], [rnd], [rnd], [rnd], [rnd], [rnd], [rnd], [rnd, end]]

            def big_attn(Q, K, V_, n, y0, pairs, qn, kn, vn, bias_of, nk_of, scale=SC2):
                for pr in range(pairs):
                    for t in (0, 1):
                        nk = nk_of(t)

                        def heads(pr=pr, t=t, nk=nk):
                            out = []
                            for i in range(2):
                                h = 2 * pr + i
                                tks = [*kn(h), *vn(), *qn(h)]
                                out.append((Q[:, h, t * 128:(t + 1) * 128], K[:, h, 0:nk],
                                            [V_[:, k, h * 128:(h + 1) * 128] for k in range(nk // 128)], tks))
                            return out

                        def done(tok, pr=pr):
                            for i in range(2):
                                ytok[y0 + 2 * pr + i] = ytok[y0 + 2 * pr + i] + [tok]
                        pre, bi, fb = bias_of(pr, t, nk)
                        js, sd = attn_steps(heads, nk, scale, bi, Y[:, y0 + 2 * pr:y0 + 2 * pr + 2, t * 128:(t + 1) * 128],
                                            pre=fb, outtok=done)
                        sd["war"] = [st["a_end"]]
                        jobs.append(([pre] if pre else []) + js)

            def fox_bias(pr, t, nk):
                x_ = {}
                kk = [0]

                def pre():
                    k = fx[0] % 2
                    fx[0] += 1
                    kk[0] = k
                    for i in range(2):
                        h = 2 * pr + i
                        o = pM[:, i * 256:i * 256 + 256]
                        w0, w1 = spread(LF[:, 0, h:h + 1], 128), spread(LF[:, 1, h:h + 1], 128)
                        tp = op("pe", lambda e, o=o, w0=w0, i=i: e.matmul(o[:, 0:nk], w0, U[:, 0:nk], start=(i == 0), stop=(t == 0),
                                                                     skip_group_check=True), s_["lf"], *free["M"])
                        if t:
                            tp = op("pe", lambda e, o=o, w1=w1: e.matmul(o[:, 128:256], w1, U[:, 0:128], start=False,
                                                                         stop=True, skip_group_check=True))
                    for i in range(2):
                        h = 2 * pr + i
                        td = ts("dve", BT[:, k, i, 0:nk], pM[:, i * 256:i * 256 + nk], -1.0, ALU.mult,
                                CQ[:, t, h:h + 1], ALU.add, tp, s_["cq"], *free[f"BT{k}"])
                    free["M"] = [td]
                    x_["d"] = causal(BT[:, k, :, 0:nk], t, nk, 2, [td])

                def used(tok):
                    free[f"BT{kk[0]}"] = [tok]
                return pre, (lambda: (BT[:, kk[0], :, 0:nk], [x_["d"]])), used

            def dsa_bias(pr, t, nk):
                def used(tok):
                    st["sc_read"] = [tok]
                return None, (lambda: (over(sc_t[t], 2), sctok[t])), used

            def mem_bias(pr, t, nk):
                return None, None, None
            fx = [0]
            c0 = 32 * l
            for j in range(4):
                unit(w_2, c0 + j, 4, X, evac_rope(IQ, j, R64, "IQ"))
            unit(d_s2, l, 4, X, evac_small, mode="s", width=86)

            def start_idx():
                for t in (0, 1):
                    for b in range(8):
                        jobs.append(idx_steps(t, b))
                for g in zip(top_steps(0), top_steps(1)):
                    jobs.append([(lambda g=g: [f() for x in g for f in x] and None)])
            for j in range(3):
                unit(w_2, c0 + 4 + j, 4, X, evac_rope(DQ, j, R128, "DQ"))
                if j == 0:
                    call(start_idx)
            for j in range(3):
                unit(w_2, c0 + 7 + j, 4, X, evac_rope(DK, j, R128, "DK"))
            for j in range(2):
                unit(w_2, c0 + 10 + j, 4, X, evac_plain(MQ, j, "MQ"))
            call(lambda: big_attn(MQ, KM, VM, 4, 12, 2, lambda h: tk["MQ"][h], lambda h: kvtok["k"][h],
                                  lambda: [*kvtok["v"][0], *kvtok["v"][1]], mem_bias, lambda t: 256))
            for j in range(3):
                unit(w_2, c0 + 12 + j, 4, X, evac_v(DV, j, "DV"), mode="t")
            call(lambda: big_attn(DQ, DK, DV, 6, 6, 3, lambda h: tk["DQ"][h], lambda h: tk["DK"][h],
                                  lambda: tk1["DV"][0], dsa_bias, lambda t: 128 * (t + 1)))
            for j in range(3):
                unit(w_2, c0 + 15 + j, 4, X, evac_plain(FQ, j, "FQ"))
            for j in range(3):
                unit(w_2, c0 + 18 + j, 4, X, evac_plain(FK, j, "FK"))
            for j in range(3):
                unit(w_2, c0 + 21 + j, 4, X, evac_v(FV, j, "FV"), mode="t")
            call(lambda: big_attn(FQ, FK, FV, 6, 0, 3, lambda h: tk["FQ"][h], lambda h: tk["FK"][h],
                                  lambda: tk1["FV"][0], fox_bias, lambda t: 128 * (t + 1)))

            yact = {"hi": Yh, "lo": Yl, "toks": [[] for _ in range(NB)]}

            def evac_silu(j):
                def f(ps, tp):
                    g0, g1, g2 = TG[:, 0, :], TG[:, 1, :], TG[:, 2, :]
                    need = 2 if j >= 0 else 0
                    while any(len(ytok[b]) < need for b in (2 * j, 2 * j + 1)):
                        advance()
                    while any(len(ytok[b]) < need for b in range(6, 12)):
                        advance()
                    t = act(g0, ps[:, :], ACT.Tanh, tp, *free["TG0"], scale=0.5)
                    t = stt(g1, g0, 1.0, ps[:, :], ALU.add, ALU.mult, t, *free["TG1"])
                    free["TG0"] = [t]
                    fr = [t]
                    ys = [x for b in (2 * j, 2 * j + 1, *range(6, 12)) for x in ytok[b]]
                    t = stt(g2, g1, 0.5, pair(Y, j), ALU.mult, ALU.mult, t, *ys, *free["TG2"])
                    free["TG1"] = [t]
                    tkk = split_out(pair(Yh, j), pair(Yl, j), g2, t, "TG2", t, *ys)
                    yact["toks"][2 * j] = yact["toks"][2 * j + 1] = tkk
                    return fr
                return f
            for n, j in enumerate((3, 4, 5, 6, 7, 0, 1, 2)):
                unit(w_2, c0 + 24 + n, 4, X, evac_silu(j))
            call(lambda: (flush_later(), drain_jobs()))

            def shift_pair(j):
                t = tt("dve", RES[:, 2 * j:2 * j + 2, :], RES[:, 2 * j:2 * j + 2, :], over(R2, 2), ALU.subtract,
                       st["mu"], *restok[2 * j])
                restok[2 * j] = restok[2 * j + 1] = [t]
                if j == 0:
                    st["zs"] = act(sumT, pair(RES, 0), ACT.Copy, t, *free["LP1"])
                elif j < 7:
                    st["zs"] = tt("pool", sumT, sumT, pair(RES, j), ALU.add, t, st["zs"])
                square_up(j, t)
                if j == 7:
                    total(pT, "zs", sumT, pair(RES, 7), t, "statz")
                    free["LP1"] = [st["statz"]]

            def evac_y(j):
                def f(ps, tp):
                    t = stt(pair(RES, j), pair(RES, j), ALPHA, ps[:, :], ALU.mult, ALU.add, tp, *restok[2 * j],
                            *restok[2 * j + 1])
                    restok[2 * j] = restok[2 * j + 1] = [t]
                    if j == 1:
                        def mean():
                            for n in range(4):
                                q = op("pe", lambda e, n=n: e.matmul(pS[:, 0:256], ones, RES[:, n, :], start=(n == 0),
                                                                     stop=(n == 3), skip_group_check=True),
                                       *restok[n], *free["S"])
                            st["mu"] = ts("dve", R2, pS[:, 0:256], 1.0 / 512, ALU.mult, None, None, q, *free["BT0"],
                                          *free["BT1"])
                            free["S"] = [st["mu"]]
                        defer(2, mean)
                        defer(2, lambda: shift_pair(0))
                        defer(3, lambda: shift_pair(1))
                    if j > 1:
                        shift_pair(j)
                    return [t]
                return f
            if l == 0:
                call(lambda: st.__setitem__("m1", st["pe"]))
            for j in range(8):
                unit(w_o2, 8 * l + j, 4, lambda: yact, evac_y(j))
            call(lambda: [ytok.__setitem__(b, []) for b in range(NB)])
            if l == 0:
                mem_load(mem1, memtok1, lambda: [st["m1"]])

            def norm():
                last = st["pe"]

                def tail():
                    w = free["BT0"] + free["BT1"]
                    td = ts("dve", R4, pT[:, 0:256], 1.0 / D, ALU.mult, None, None, st["statz"], *w)
                    free["T"] = [td]
                    t = tt("dve", R3, R4, R4, ALU.mult, td)
                    st["dm2"] = t
                    for j in range(8):
                        o = RES[:, 2 * j:2 * j + 2, :]
                        tz = tt("pool" if j > 4 else "dve", o, o, over(R4, 2), ALU.subtract, td, *restok[2 * j],
                                st["stat"], st["statz"])
                        restok[2 * j] = restok[2 * j + 1] = [tz]
                    st["zm"] = [x for z in range(NB) for x in restok[z]]

                def head():
                    tail()
                    tr = rstd(LN_EPS, st["dm2"], st["zm"])
                    kind = "ln" if l == 0 else "out"
                    for q in range(5):
                        def blocks(q=q):
                            for b in range(q * 4, min(NB, q * 4 + 4)):
                                emit_h(b, kind, tr, v(V_LNG + 16 * l + b), v(V_LNB + 16 * l + b), last)
                                if l == 1 and b % 4 == 3:
                                    dma("sp", d_out[:, b - 3:b + 1, :], RES[:, b - 3:b + 1, :], s_out,
                                        *[x for z in range(b - 3, b + 1) for x in restok[z]])
                            if q == 4:
                                close_t()
                        defer(2 + q, blocks)
                defer(1, head)
            call(norm)
            if l == 0:
                call(lambda: st.__setitem__("kv_end", st["pe"]))
                for j in range(4):
                    kv_unit(1, j, mem1, memtok1)
            call(flush_later)
            call(lambda: st.__setitem__("stat_done", st["stat"]))
        s_out = dma_sem("s_out")
        call(lambda: [ytok.__setitem__(b, []) for b in range(NB)])
        layer(0)
        layer(1)

        nw = [0]
        background = [dict(kind="ada", g=g, kt=kt) for g in range(4, 12) for kt in range(NB)]
        order = []

        def add(el):
            stream.append(el)
            return len(stream) - 1

        def add_ada(g, kt):
            add(dict(kind="ada", g=g, kt=kt, n=CH, src=d_ada[g, kt]))
        for g in (2, 3, 0, 1):
            for kt in range(NB):
                add_ada(g, kt)
        bg = 0
        chunks = 0
        pause = 0
        due = 0
        for kind, s in steps:
            if kind == "unit":
                s["ids"] = []
                for c in range(s["nkc"]):
                    n = 4 * s["width"]
                    i = add(dict(kind="w", n=n, slot=nw[0] % NSP, src=s["src"][s["u"], s["kc0"] + c]))
                    nw[0] += 1
                    order.append(i)
                    s["ids"].append(i)
                    chunks += 1
                    due += 0 if chunks < 32 else 0.34 if chunks < 72 else 0.45 if chunks < 136 else 0.6
                    if bg < len(background) and due >= 1 and chunks >= pause:
                        due -= 1
                        add_ada(background[bg]["g"], background[bg]["kt"])
                        bg += 1
                        if bg % NB == 0:
                            pause = chunks + 5
            elif kind == "mem":
                for q in range(4):
                    add(dict(kind="mem", n=CH, q=q, src=d_mem[:, 4 * q:4 * q + 4, :].rearrange("p b s -> p (b s)"), **s))
        assert bg == len(background)
        pos = {i: n for n, i in enumerate(order)}
        for kind, s in steps:
            if kind == "unit":
                s["ahead"] = [order[min(pos[i] + AHEAD, len(order) - 1)] for i in s["ids"]]
        pump()
        while stream[st["split"]]["kind"] == "ada":
            push_split()
            if st["split"] == NB:
                x_first()
        for kind, s in steps:
            if kind == "unit":
                run_unit(s)
            elif kind == "call":
                s()
        flush_later()
        wait("sp", [(s_out, count[id(s_out)])])

        block = ctx.enter_context(nc.Block())

        def play(e):
            return lambda eng: [f(eng) for f in prog[e]] and None
        block.tensor(play("pe"))
        block.scalar(play("act"))
        block.vector(play("dve"))
        block.gpsimd(play("pool"))
        block.sync(play("sp"))


def _strips(w, width=256):
    k, n = w.shape
    return np.ascontiguousarray(
        w.reshape(k // 512, 4, 128, n // width, width).transpose(3, 0, 2, 1, 4)).reshape(n // width, k // 512, 128, 4 * width)


def _cols(a):
    return np.asarray(a).reshape(-1, 128).T


def _constants():
    f = np.float32
    c = np.zeros((128, C_END), f)
    c[:, C_ONE:C_ONE + 128] = 1
    i = np.arange(128)
    c[i, C_ID + i] = 1
    c[i % 64, C_DUP + i] = 1
    c[(i % 64) ^ 32, C_SWAP + i] = 1
    c[:, C_U:C_U + 256] = i[:, None] <= np.arange(256)[None, :]
    for d, cc, cs in ((128, C_COS128, C_SIN128), (64, C_COS64, C_SIN64)):
        half = d // 2
        inv = (f(10000.0) ** (-np.arange(half, dtype=f) / f(half))).astype(f)
        ang = (np.arange(S, dtype=f)[None, :] * inv[:, None]).astype(f).astype(np.float64)
        row = i % d
        c[:, cc:cc + S] = np.cos(ang)[row % half]
        c[:, cs:cs + S] = np.sin(ang)[row % half] * np.where(row < half, -1.0, 1.0)[:, None]
    hot = np.zeros((32, 384), f)
    rel = np.arange(128)
    big = 16 + (np.log(np.maximum(rel, 1).astype(f) / f(16)) / f(np.log(8.0)) * f(16)).astype(np.int32)
    bucket = np.where(rel < 16, rel, np.minimum(big, 31))
    hot[bucket, 255 - rel] = 1
    return c, hot


def kernel(**inp):
    import concourse.bacc as _bacc
    from concourse import mybir as _mybir
    from concourse.bass_utils import run_bass_kernel_spmd as _run

    a = {k: np.asarray(x) for k, x in inp.items()}
    heads = np.concatenate([[b, 8 + b] if b < 8 else [8 + b, 16 + b] for b in range(16)])
    qcols = (heads[:, None] * 64 + np.arange(64)[None]).ravel()
    xT = lambda z: np.ascontiguousarray(z[0].T.reshape(NB, 128, S).transpose(1, 0, 2))
    w_in = a["w_in"][0]
    o = {}
    o["x"] = xT(a["x"])
    o["mem"] = xT(a["mem_2"])
    rep = lambda z: np.broadcast_to(np.asarray(z).reshape(1, -1), (128, np.asarray(z).size))
    o["vec"] = np.ascontiguousarray(np.concatenate([
        _cols(a["norm1_g"]), _cols(a["conv_w"]), _cols(a["conv_b"]), _cols(a["lru_ba"]), _cols(a["lru_bx"]),
        _cols(a["lru_lambda"]), _cols(a["norm2_g"]), _cols(a["final_g"]), _cols(a["ln_gain_2"]), _cols(a["ln_bias_2"]),
        _cols(a["c"]), _cols(a["b_ada"]), rep(a["attn_sinks"][0][heads]), rep(a["b_forget_2"])], axis=1))
    o["cst"], o["hot"] = _constants()
    o["relb"] = np.ascontiguousarray(a["rel_bias"])
    o["ada"] = np.ascontiguousarray(a["w_ada"][0].reshape(NB, 128, 12, CH).transpose(2, 0, 1, 3))
    lru = np.stack([a["lru_wa"][0], a["lru_wx"][0]], axis=1)
    o["lru"] = np.ascontiguousarray(lru.reshape(4, 4, 2, 128, 128).transpose(0, 3, 1, 2, 4)).reshape(4, 128, CH)
    order = np.concatenate([np.arange(0, 2048), 4096 + qcols, np.arange(6144, 6656), np.arange(2048, 4096),
                            np.arange(6656, 10752)])
    o["w_in"] = _strips(w_in[:, order])
    o["w_lru_out"] = _strips(a["w_lru_out"][0])
    o["w_attn_out"] = _strips(a["w_attn_out"][0][qcols])
    o["w_out"] = _strips(a["w_out"][0])
    o["w_ff1"] = _strips(a["w_ff1"][0])
    o["w_ff2"] = _strips(a["w_ff2"][0])
    o["w_kv"] = np.concatenate([_strips(a["w_mem_kv_2"][l]) for l in range(2)])
    r = lambda s, n: np.arange(s, s + n)
    main = np.concatenate([r(6150, 1024), r(3078, 768), r(3846, 768), r(7254, 512), r(4614, 768), r(0, 768),
                           r(768, 768), r(1536, 768), r(5382, 768), r(7766, 512), r(2304, 768)])
    small = np.concatenate([r(7174, 64), r(7238, 16), r(3072, 6)])
    o["w_in2"] = np.concatenate([_strips(a["w_in_2"][l][:, main]) for l in range(2)])
    o["w_s2"] = np.concatenate([_strips(a["w_in_2"][l][:, small], 86) for l in range(2)])
    o["w_out2"] = np.concatenate([_strips(a["w_out_2"][l]) for l in range(2)])

    nc = _bacc.Bacc("TRN2", target_bir_lowering=False, num_devices=1)
    arrays, ap = {}, {}
    for name, z in o.items():
        arrays[f"in_{name}"] = z
        ap[name] = nc.dram_tensor(f"in_{name}", z.shape, _mybir.dt.from_np(z.dtype), kind="ExternalInput").ap()
    out = nc.dram_tensor("out_0", (128, NB, S), F32, kind="ExternalOutput").ap()
    d_w = {"in": ap["w_in"], "lru_out": ap["w_lru_out"], "attn_out": ap["w_attn_out"], "out": ap["w_out"],
           "ff1": ap["w_ff1"], "ff2": ap["w_ff2"], "kv": ap["w_kv"], "in2": ap["w_in2"], "out2": ap["w_out2"]}
    build(nc, ap["x"], ap["mem"], ap["vec"], ap["cst"], ap["hot"], ap["relb"], ap["ada"], ap["lru"], d_w, ap["w_s2"], out)
    r_ = _run(nc, [arrays], core_ids=[0])
    got = r_.results[0]["out_0"]
    return np.ascontiguousarray(got.transpose(1, 0, 2).reshape(D, S).T).reshape(1, S, D)
```

```python
from collections import deque
from contextlib import ExitStack

import numpy as np

import concourse.bass as bass
from concourse import mybir

F32 = mybir.dt.float32
F32R = mybir.dt.float32r
ALU = mybir.AluOpType
ACT = mybir.ActivationFunctionType
AX = mybir.AxisListType

D = 2048
S = 256
NB = D // 128
EPS = 1e-6
LN_EPS = 1e-5
ALPHA = 4 ** 0.25
NEG = -1e30
TAKEN = -3e38
SC1 = 64 ** -0.5
SC2 = 128 ** -0.5

V_N1, V_CW, V_CB, V_BA, V_BX, V_LAM, V_N2, V_FG = 0, 16, 80, 96, 112, 128, 144, 160
V_LNG, V_LNB, V_C, V_ADA, V_SINK, V_BF = 176, 208, 240, 256, 352, 384
V_END = 396
C_ONE, C_ID, C_DUP, C_SWAP, C_U = 0, 128, 256, 384, 512
C_COS128, C_SIN128, C_COS64, C_SIN64, C_END = 768, 1024, 1280, 1536, 1792

CH = 1024
NRAW = 5
NSP = 4
AHEAD = NSP - 1


def build(nc, d_x, d_mem, d_vec, d_cst, d_hot, d_relb, d_ada, d_lru, d_w, d_s2, d_out):
    ctx = ExitStack()
    with ctx:
        cur = [16512]

        def place(nbytes):
            at = cur[0]
            cur[0] += nbytes
            return at

        def at(name, shape, off, dt=F32):
            return nc.alloc_sbuf_tensor_at(name, shape, dt, offset=off)

        o_raw = place(NRAW * CH * 4)
        o_hi = place(NSP * CH * 4)
        o_lo = place(NSP * CH * 4)
        raw = [at(f"raw{i}", [128, CH], o_raw + i * CH * 4) for i in range(NRAW)]
        whi = at("whi", [128, NSP, CH], o_hi, F32R)
        wlo = at("wlo", [128, NSP, CH], o_lo, F32R)
        RES = at("RES", [128, NB, S], place(NB * S * 4))
        o_h = place(2 * NB * S * 4)
        Hhi = at("Hhi", [128, NB, S], o_h, F32R)
        Hlo = at("Hlo", [128, NB, S], o_h + 16384, F32R)
        o_a = place(4 * 16384)
        o_acc = place(4096)
        o_kv = place(8192)
        KM = at("KM", [128, 4, S], o_kv)
        VM = at("VM", [128, 2, 512], o_kv + 4096)
        o_cst = place(C_END * 4)
        cst = at("cst", [128, C_END], o_cst)
        raw.append(at("raw5", [128, CH], o_cst + C_DUP * 4))
        raw.extend(at(f"raw{6 + i}", [128, CH], o_a + 49152 + i * 4096) for i in range(4))
        vec = at("vec", [128, V_END], place(1600))
        mod = at("mod", [128, 96], place(384))
        A1v = at("A1v", [128, NB], place(64))
        A2v = at("A2v", [128, NB], place(64))
        o_lp = place(3 * 2048)
        o_pt = place(2 * 2048)
        o_bt = place(2 * 2048)
        o_tg = place(4 * 2048)
        o_sm = place(384)
        assert cur[0] <= 229344, cur[0]
        LP = at("LP", [128, 3, 2, S], o_lp)
        PT = at("PT", [128, 2, 4, 128], o_pt)
        BT = at("BT", [128, 2, 2, S], o_bt)
        TG = at("TG", [128, 4, 512], o_tg)
        SM = at("SM", [128, 4, 6, 2], o_sm)
        MX8 = at("MX8", [128, 2, 8], o_sm + 192)
        ones = cst[:, C_ONE:C_ONE + 128]
        ident = cst[:, C_ID:C_ID + 128]
        U = cst[:, C_U:C_U + 256]

        acc = [at("acc0", [128, CH], o_acc), at("acc1", [128, CH], o_a)]
        AT = at("AT", [128, NB, S], o_a)
        XC = at("XC", [128, NB, S], o_a + 16384)
        AA = at("AA", [128, NB, S], o_a + 32768)
        MM = at("MM", [128, NB, S], o_a + 49152)
        Zh = at("Zh", [128, NB, S], o_a + 16384, F32R)
        Zl = at("Zl", [128, NB, S], o_a + 32768, F32R)
        KT = at("KT", [128, 2, S], o_kv)
        VT = at("VT", [128, 2, 256], o_kv + 2048)
        Mh0 = at("Mh0", [128, NB, S], o_a + 16384, F32R)
        Ml0 = at("Ml0", [128, NB, S], o_a + 49152, F32R)
        Fh = [at(f"Fh{i}", [128, 8, S], o_a + 32768 * i, F32R) for i in range(2)]
        Fl = [at(f"Fl{i}", [128, 8, S], o_a + 32768 * i + 8192, F32R) for i in range(2)]
        DQ = at("DQ", [128, 6, S], o_a)
        DK = at("DK", [128, 6, S], o_a + 6144)
        DV = at("DV", [128, 2, 768], o_a + 12288)
        FQ = at("FQ", [128, 6, S], o_a + 18432)
        FK = at("FK", [128, 6, S], o_a + 24576)
        FV = at("FV", [128, 2, 768], o_a + 30720)
        MQ = at("MQ", [128, 4, S], o_a + 36864)
        IQ = at("IQ", [128, 8, S], o_a + 40960)
        Y = at("Y", [128, NB, S], o_a + 49152)
        Yh = at("Yh", [128, NB, S], o_a + 49152, F32R)
        Yl = at("Yl", [128, NB, S], o_a, F32R)
        Mh1 = at("Mh1", [128, NB, S], o_a + 16384, F32R)
        Ml1 = at("Ml1", [128, NB, S], o_a + 32768, F32R)
        IK = at("IK", [128, S], o_acc)
        SC = at("SC", [128, 384], o_acc + 1024)
        TK = at("TK", [128, 2, 22], o_acc + 2560)
        LF = at("LF", [128, 2, 6], o_acc + 2752)
        CQ = at("CQ", [128, 2, 6], o_acc + 2816)
        SMALL = at("SMALL", [128, 6, 16], o_acc + 2880)
        hot = at("hot", [32, 384], o_kv)
        relb = at("relb", [32, 32], o_kv + 1536)
        gsb = at("gsb", [32, 384], o_kv + 2048)
        LPS = at("LPS", [128, 8, 16], o_lp)
        CS = at("CS", [128, NB], o_sm + 256)
        SPH = at("SPH", [128, NB], o_sm + 320)

        bank = [nc.alloc_psum_tensor(f"bank{i}", [128, 512], F32) for i in range(3)]
        pS2 = nc.alloc_psum_tensor("pS2", [128, 2, 512], F32)
        pS = pS2[:, 0, :]
        pT, pO, pM = (nc.alloc_psum_tensor(f"p{i}", [128, 512], F32) for i in "TOM")
        gdram = nc.dram_tensor("gtab", (32, 384), F32, kind="Internal").ap()

        prog = {e: [] for e in ("pe", "act", "dve", "pool", "sp")}
        sems = {e: ctx.enter_context(nc.semaphore(f"s_{e}")) for e in ("pe", "act", "dve", "pool")}
        names = {id(s): e for e, s in sems.items()}
        count = {}
        reached = {}

        def dma_sem(name):
            return ctx.enter_context(nc.semaphore(name))

        def signal(sem, by):
            count[id(sem)] = count.get(id(sem), 0) + by
            return sem, count[id(sem)]

        def wait(e, toks):
            for sem, v in toks:
                if reached.get((e, id(sem)), 0) < v:
                    reached[(e, id(sem))] = v
                    prog[e].append(lambda eng, sem=sem, v=v: eng.wait_ge(sem, v))

        def op(e, fn, *toks):
            wait(e, toks)
            sem = sems[e]
            tok = signal(sem, 1)
            prog[e].append(lambda eng: fn(eng).then_inc(sem, 1))
            if e == "pe":
                st["pe"] = tok
            return tok

        def quiet(e, fn, *toks):
            wait(e, toks)
            prog[e].append(fn)

        def dma(e, out, in_, sem, *toks):
            wait(e, toks)
            tok = signal(sem, 16)
            prog[e].append(lambda eng: eng.dma_start(out, in_).then_inc(sem, 16))
            return tok

        def tt(e, out, a, b, o, *toks):
            return op(e, lambda g: g.tensor_tensor(out, a, b, o), *toks)

        def ts(e, out, a, s1, o1, s2, o2, *toks):
            if o2 is None:
                return op(e, lambda g: g.tensor_scalar(out, a, s1, None, o1), *toks)
            return op(e, lambda g: g.tensor_scalar(out, a, s1, s2, o1, o2), *toks)

        def stt(out, a, s, b, o0, o1, *toks):
            return op("dve", lambda g: g.scalar_tensor_tensor(out=out, in0=a, scalar=s, in1=b, op0=o0, op1=o1), *toks)

        def act(out, in_, f, *toks, **kw):
            return op("act", lambda g: g.activation(out, in_, f, **kw), *toks)

        def over(ap, n):
            a = list(ap.ap)
            return bass.AP(tensor=ap.tensor, offset=ap.offset, ap=[list(a[0]), [0, n]] + [list(z) for z in a[1:]])

        def spread(ap, n):
            return bass.AP(tensor=ap.tensor, offset=ap.offset, ap=[list(ap.ap[0]), [0, n]])

        def mirrored(ap):
            a = [list(z) for z in ap.ap]
            step, n = a[-1]
            return bass.AP(tensor=ap.tensor, offset=ap.offset + step * (n - 1), ap=a[:-1] + [[-step, n]])

        def v32(ap):
            return ap.bitcast(F32)

        stream = []
        s_raw = [dma_sem(f"s_raw{i}") for i in range(10)]
        raw_free = [[] for _ in range(10)]
        slot_of = []
        before = []
        sp_free = [[] for _ in range(NSP)]
        landed = {}
        st = {"dma": 0, "split": 0, "w": 0, "main": 0, "tick": 0, "pe": None, "span": 2, "open": 0, "lag": False}
        ready = {}
        acc_free = [[], []]
        modtok = {}

        released = set()

        def pump():
            while st["dma"] < len(stream) and (before[st["dma"]] is None or before[st["dma"]] in released):
                i = st["dma"]
                r = slot_of[i]
                n = stream[i]["n"]
                landed[i] = dma("sp", raw[r][:, 0:n], stream[i]["src"], s_raw[r], *raw_free[r])
                st["dma"] += 1

        def release(i, toks):
            raw_free[slot_of[i]] = toks
            released.add(i)
            pump()

        lagging = []

        def low_half():
            while lagging:
                lagging.pop(0)()

        def push_split():
            i = st["split"]
            el = stream[i]
            r = slot_of[i]
            while i not in landed:
                low_half()
            kind = el["kind"]
            if kind == "w":
                s = el["slot"]
                n = el["n"]
                th = act(whi[:, s, 0:n], raw[r][:, 0:n], ACT.Copy, landed[i], *sp_free[s])
                low_half()
                wt = list(sp_free[s])

                def low(i=i, s=s, n=n, r=r, th=th, wt=wt):
                    tl = tt("dve", wlo[:, s, 0:n], raw[r][:, 0:n], v32(whi[:, s, 0:n]), ALU.subtract, landed[i], th, *wt)
                    ready[i] = [th, tl]
                    release(i, [th, tl])
                lagging.append(low)
                if not st["lag"]:
                    low_half()
            elif kind == "ada":
                g, kt = el["g"], el["kt"]
                k = g // 2 if g in (0, 2) else (g - 1) // 2 if g < 4 else 0
                ac = acc[k]
                cs = CS[:, kt:kt + 1]
                if kt == 0:
                    assert g < 4 or g == 4 or g - 1 in modtok
                    t = ts("dve", ac[:, :], raw[r][:, :], cs, ALU.mult, None, None, landed[i], t_cs, *acc_free[k])
                elif g >= 4 and kt % 2:
                    t = act(raw[r][:, :], raw[r][:, :], ACT.Copy, landed[i], t_cs, scale=cs)
                    t = tt("pool", ac[:, :], ac[:, :], raw[r][:, :], ALU.add, t, ada_last[0])
                else:
                    t = stt(ac[:, :], raw[r][:, :], cs, ac[:, :], ALU.mult, ALU.add, landed[i], ada_last[0])
                ada_last[0] = t
                release(i, [t])
                if kt == NB - 1:
                    def fold(g=g, t=t, k=k, ac=ac):
                        for j in range(8):
                            o, w = pM[:, j:j + 1], ac[:, j * 128:(j + 1) * 128]
                            f = lambda e, o=o, w=w: e.matmul(o, w, ones[:, 0:1], start=True, stop=True)
                            if j < 7:
                                quiet("pe", f, t, t_cst, *free["M"])
                            else:
                                tp = op("pe", f, t)
                        tm = tt("dve", mod[:, 8 * g:8 * g + 8], pM[:, 0:8], vec[:, V_ADA + 8 * g:V_ADA + 8 * g + 8],
                                ALU.add, tp, t_vec)
                        free["M"] = [tm]
                        acc_free[k] = [tp]
                        modtok[g] = tm
                    if g in (2, 0):
                        fold()
                    elif g < 4:
                        folds.append(fold)
                    else:
                        defer(4, fold)
            elif kind == "mem":
                low_half()
                q = el["q"]
                mh, ml = el["dst"]
                src = raw[r][:, :].rearrange("p (b s) -> p b s", b=4)
                wt = el["after"]()
                th = act(mh[:, 4 * q:4 * q + 4, :], src, ACT.Copy, landed[i], *wt)
                tl = tt("dve", ml[:, 4 * q:4 * q + 4, :], src, v32(mh[:, 4 * q:4 * q + 4, :]), ALU.subtract, landed[i], th, *wt)
                release(i, [th, tl])
                el["done"][q] = [th, tl]
            st["split"] += 1

        def ensure(i):
            while st["split"] <= i and st["split"] < len(stream):
                push_split()

        jobs = deque()
        flight = []
        later = []
        subs = []

        def rest_of(r):
            for n, fn in enumerate(f for f in r or () if f):
                subs.append((st["tick"] + 1 + n, fn))

        def run_subs(upto=None):
            while subs and (upto is None or min(x[0] for x in subs) <= upto):
                x = min(subs, key=lambda x: x[0])
                subs.remove(x)
                x[1]()

        def advance():
            run_subs()
            for j in list(flight):
                rest_of(j["steps"][j["at"]]())
                j["at"] += 1
                if j["at"] == len(j["steps"]):
                    flight.remove(j)
            if jobs:
                j = {"steps": jobs.popleft(), "at": 0}
                rest_of(j["steps"][0]())
                j["at"] = 1
                if j["at"] < len(j["steps"]):
                    flight.append(j)

        def tick():
            st["tick"] += 1
            due = [x for x in later if x[0] <= st["tick"]]
            for x in due:
                later.remove(x)
                x[1]()
            run_subs(st["tick"])
            if st["tick"] % st["span"] == 0:
                advance()

        def flush_later():
            while later:
                later.sort(key=lambda x: x[0])
                later.pop(0)[1]()

        def drain_jobs():
            while jobs or flight or subs:
                advance()

        def defer(n, fn):
            later.append((st["tick"] + n, fn))

        free = {k: [] for k in ("S", "T", "O", "M", "TG0", "TG1", "TG2", "TG3", "BT0", "BT1", "PT0", "PT1",
                                "LP0", "LP1", "LP2", "SM0", "SM1", "SM2", "SM3")}
        main_free = [[] for _ in range(3)]

        steps = []

        def unit(src, u, nkc, xact, evac, mode="f", kt0=0, width=256, kc0=0, corder=(0, 1, 2, 3), part=None, hold=None):
            steps.append(("unit", dict(src=src, u=u, nkc=nkc, x=xact, evac=evac, mode=mode, kt0=kt0, width=width, kc0=kc0,
                                   corder=corder, part=part, hold=hold)))

        def call(fn):
            steps.append(("call", fn))

        def run_unit(s):
            x = s["x"]()
            if s["part"] == "close":
                ps, b = s["hold"]["ps"], s["hold"]["bank"]
            elif s["part"] == "open" and st["main"] > 2:
                b = "SSOT"[st["open"]]
                ps = (pS, pS2[:, 1, :], pO, pT)[st["open"]]
                wait("pe", free[b])
                st["open"] += 1
            else:
                b = st["main"] % 3
                st["main"] += 1
                ps = bank[b]
                wait("pe", main_free[b])
            if s["part"] == "open":
                s["hold"]["ps"], s["hold"]["bank"] = ps, b
            first = s["part"] != "close"
            width = s["width"]
            last = None
            for c in range(s["nkc"]):
                i = s["ids"][c]
                el = stream[i]
                ensure(s["ahead"][c])
                if i not in ready:
                    low_half()
                wait("pe", ready[i])
                slot = el["slot"]
                mms = []
                for k in range(4):
                    kt = s["kt0"] + 4 * s["corder"][c] + k
                    for t in x["toks"][kt]:
                        mms.append(("w", t))
                    w0 = k * width

                    def feat(col, o, kt=kt, w0=w0):
                        h, l = whi[:, slot, w0 + col:w0 + col + 128], wlo[:, slot, w0 + col:w0 + col + 128]
                        xh, xl = x["hi"][:, kt, :], x["lo"][:, kt, :]
                        mms.extend([("m", o, h, xh), ("m", o, h, xl), ("m", o, l, xh)])

                    def toks(col, n, stride, off, kt=kt, w0=w0):
                        h, l = whi[:, slot, w0 + col:w0 + col + n], wlo[:, slot, w0 + col:w0 + col + n]
                        for t in range(2):
                            o = ps[:, off + t * stride:off + t * stride + n]
                            xh = x["hi"][:, kt, t * 128:(t + 1) * 128]
                            xl = x["lo"][:, kt, t * 128:(t + 1) * 128]
                            mms.extend([("m", o, xh, h), ("m", o, xh, l), ("m", o, xl, h)])

                    if s["mode"] == "f":
                        feat(0, ps[:, 0:256])
                        feat(128, ps[:, 256:512])
                    elif s["mode"] == "t":
                        toks(0, 256, 256, 0)
                    else:
                        h, l = whi[:, slot, w0:w0 + width], wlo[:, slot, w0:w0 + width]
                        xh, xl = x["hi"][:, kt, :], x["lo"][:, kt, :]
                        o = ps[0:width, 0:256]
                        mms.extend([("m", o, h, xh), ("m", o, h, xl), ("m", o, l, xh)])
                endm = max(j for j, m in enumerate(mms) if m[0] == "m")
                for j, m in enumerate(mms):
                    if m[0] == "w":
                        wait("pe", [m[1]])
                        continue
                    fn = lambda e, m=m, f=first, z=(c == s["nkc"] - 1 and j == endm and s["part"] != "open"): e.matmul(
                        m[1], m[2], m[3], start=f, stop=z, skip_group_check=True)
                    first = False
                    if j == endm:
                        last = op("pe", fn)
                    else:
                        quiet("pe", fn)
                sp_free[slot] = [last]
                if c < s["nkc"] - 1:
                    tick()
            if s["part"] == "open":
                return
            done = s["evac"](ps, last)
            if b in ("S", "O", "T"):
                free[b] = free[b] + done
            else:
                main_free[b] = done
            tick()

        s_in = dma_sem("s_in")
        s_in2 = dma_sem("s_in2")
        s_hot = dma_sem("s_hot")
        s_g = dma_sem("s_g")
        t_vec = dma("sp", vec[:, :], d_vec, s_in)
        t_cst = dma("act", cst[:, 0:C_DUP], d_cst[:, 0:C_DUP], s_in2)
        dma("pool", hot[:, :], d_hot, s_hot)
        t_hot = dma("pool", relb[:, :], d_relb, s_hot)
        s_x = dma_sem("s_x")
        t_x = dma("act", RES[:, :, :], d_x, s_x)
        ada_last = [None]

        def v(c, n=1):
            return vec[:, c:c + n]

        t0 = act(LPS[:, 0, :], v(V_C, 16), ACT.Tanh, t_vec, scale=0.5)
        t0 = stt(LPS[:, 1, :], LPS[:, 0, :], 1.0, v(V_C, 16), ALU.add, ALU.mult, t0)
        t_cs = ts("dve", CS[:, :], LPS[:, 1, :], 0.5, ALU.mult, None, None, t0)

        def log1p_exp(tmp, z_abs, n, tz):
            e, d, s, q, p = (tmp(i) for i in range(5))
            t = act(e, z_abs, ACT.Exp, tz, scale=-1.0)
            t = ts("dve", d, e, 2.0, ALU.add, None, None, t)
            t = op("dve", lambda g: g.reciprocal(d, d), t)
            t = tt("dve", s, e, d, ALU.mult, t)
            t = tt("dve", q, s, s, ALU.mult, t)
            t = ts("dve", p, q, 1.0 / 17, ALU.mult, None, None, t)
            for k in (15, 13, 11, 9, 7, 5, 3):
                t = stt(p, p, 1.0 / k, q, ALU.add, ALU.mult, t)
            t = stt(p, p, 1.0, s, ALU.add, ALU.mult, t)
            return p, t

        def decay():
            nonlocal t_sp, t_half
            t1 = stt(LPS[:, 2, :], v(V_LAM, 16), -1.0, v(V_LAM, 16), ALU.mult, ALU.max, t_vec)
            p, t1 = log1p_exp(lambda i: LPS[:, 3 + i, :], LPS[:, 2, :], 16, t1)
            t2 = ts("dve", LPS[:, 2, :], v(V_LAM, 16), -1.0, ALU.mult, 0.0, ALU.max, t1)
            t2 = stt(LPS[:, 3, :], p, 2.0, LPS[:, 2, :], ALU.mult, ALU.add, t2)
            t_sp = ts("dve", SPH[:, :], LPS[:, 3, :], -2.0, ALU.mult, None, None, t2)
            t_half = ts("dve", vec[:, V_BA:V_BA + 32], vec[:, V_BA:V_BA + 32], 0.5, ALU.mult, None, None, t_vec)

        def bias_table():
            nonlocal t_g
            tg = op("pe", lambda e: e.matmul(pM[0:32, 0:384], relb[:, :], hot[:, :], start=True, stop=True), t_hot, *free["M"])
            tg = op("dve", lambda e: e.tensor_copy(gsb[:, :], pM[0:32, 0:384]), tg)
            tga = op("pool", lambda e: e.memset(gsb[:, 0:128], NEG), tg)
            tgb = op("pool", lambda e: e.memset(gsb[:, 256:384], NEG), tg)
            free["M"] = [tg]
            t_g = dma("pool", gdram, gsb[:, :], s_g, tga, tgb)

        t_sp = t_half = t_g = None

        def stat_sq(j, src, tok):
            k = j % 2
            tq = act(TG[:, k, :], src, ACT.Square, tok, *free[f"TG{k}"])

            def mm():
                stat_mm(j, TG[:, k, :], tq)
                free[f"TG{k}"] = [st["stat"]]
            return mm

        def stat_mm(j, src, tq):
            wt = free["S"] if j == 0 else []
            quiet("pe", lambda e: e.matmul(pS[:, 0:256], ones, src[:, 0:256], start=(j == 0), stop=False,
                                           skip_group_check=True), tq, t_cst, *wt)
            st["stat"] = op("pe", lambda e: e.matmul(pS[:, 0:256], ones, src[:, 256:512], start=False, stop=(j == 7),
                                                     skip_group_check=True), tq)

        def pair(t, j):
            return t[:, 2 * j:2 * j + 2, :].rearrange("p b s -> p (b s)")

        sumS, sumT = (LP[:, i, :, :].rearrange("p a s -> p (a s)") for i in range(2))

        def total(bk, key, acc_, src, t_src, mark):
            for n, (x, t) in enumerate(((acc_, st[key]), (src, t_src))):
                for h in range(2):
                    tp = op("pe", lambda e, x=x, h=h, n=n: e.matmul(
                        bk[:, 0:256], ones, x[:, h * 256:(h + 1) * 256], start=(n == 0 and h == 0), stop=(n == 1 and h == 1),
                        skip_group_check=True), t, t_cst, *free["S" if bk is pS else "T"])
            st[mark] = tp

        def square_up(j, tok):
            src = pair(RES, j)
            if j == 0:
                st["sqs"] = act(sumS, src, ACT.Square, tok, *free["LP0"], *free["LP1"])
                return
            k = j % 2
            tq = act(TG[:, k, :], src, ACT.Square, tok, *free[f"TG{k}"])
            if j < 7:
                st["sqs"] = tt("pool", sumS, sumS, TG[:, k, :], ALU.add, tq, st["sqs"])
                free[f"TG{k}"] = [st["sqs"]]
            else:
                def tot():
                    total(pS, "sqs", sumS, TG[:, k, :], tq, "stat")
                    free[f"TG{k}"] = [st["stat"]]
                    free["LP0"] = [st["stat"]]
                defer(2, tot)

        Rv, R2, R3, R4 = (BT[:, 0, 0, :], BT[:, 0, 1, :], BT[:, 1, 0, :], BT[:, 1, 1, :])

        def root(eps, dm2=None, zm=(), R4=R4):
            w = free["BT0"] + free["BT1"]
            t = ts("dve", R2, pS[:, 0:256], 1.0 / D, ALU.mult, eps, ALU.add, st["stat"], *w)
            free["S"] = [t]
            if dm2:
                t = tt("dve", R2, R2, R3, ALU.subtract, t, dm2)
            t = op("dve", lambda g: g.reciprocal(R3, R2), t)
            return act(R4, R3, ACT.Sqrt, t, *zm)

        def newton(t, R4=R4):
            t = tt("dve", R3, R4, R4, ALU.mult, t)
            t = tt("dve", R3, R3, R2, ALU.mult, t)
            t = ts("dve", R3, R3, -0.5, ALU.mult, 1.5, ALU.add, t)
            t = tt("dve", Rv, R4, R3, ALU.mult, t)
            free["BT0"] = free["BT1"] = []
            return t

        def rstd(eps, dm2=None, zm=()):
            return newton(root(eps, dm2, zm))

        hact = {"hi": Hhi, "lo": Hlo, "toks": [[] for _ in range(NB)]}
        restok = [[] for _ in range(NB)]

        def tslot(b):
            k = 2 + (b // 2) % 2
            return TG[:, k, (b % 2) * 256:(b % 2) * 256 + 256], f"TG{k}{b % 2}"

        tfree = {}

        low = []

        def low_parts():
            while low:
                low.pop(0)()

        def close_t():
            for k in (2, 3):
                free[f"TG{k}"] = tfree.pop(f"TG{k}0", []) + tfree.pop(f"TG{k}1", [])
        def emit_h(b, kind, tr, g, sh, last_read, tmod=()):
            wh = [last_read] if last_read else []
            hi, lo, r = Hhi[:, b, :], Hlo[:, b, :], RES[:, b, :]
            if kind == "rms":
                t = stt(r, r, g, Rv, ALU.mult, ALU.mult, tr, t_vec, *restok[b])
                restok[b] = [t]
                th = act(hi, r, ACT.Copy, t, *wh)

                def part():
                    tl = tt("dve", lo, r, v32(hi), ALU.subtract, th, t, *wh)
                    hact["toks"][b] = [th, tl]
                low.append(part)
                return
            sl, key = tslot(b)
            w = tfree.get(key, free["TG2"] + free["TG3"])
            t = stt(sl, r, g, Rv, ALU.mult, ALU.mult, tr, t_vec, *tmod, *w, *restok[b])
            tx = []
            if kind == "out":
                restok[b] = tfree[key] = [act(r, sl, ACT.Identity, t, bias=sh)]
                return
            if kind == "ln":
                tx = [ts("pool", r, sl, ones[:, 0:1], ALU.mult, sh, ALU.add, t)]
                restok[b] = tx
            th = act(hi, sl, ACT.Identity, t, *wh, bias=sh)

            def part():
                tl = stt(lo, sl, sh, v32(hi), ALU.add, ALU.subtract, t, th, *wh)
                tfree[key] = [th, tl, *tx]
                hact["toks"][b] = [th, tl]
            low.append(part)

        PERM = []
        for b in range(16):
            PERM.append((b, 8 + b) if b < 8 else (8 + b, 16 + b))

        w_in, w_lo, w_ao, w_o, w_f1, w_f2 = (d_w[k] for k in ("in", "lru_out", "attn_out", "out", "ff1", "ff2"))

        XR = at("XR", [128, NB, S], o_a + 32768)
        xrtok = []

        def x_first():
            out = [None] * 6
            for j in range(8):
                out.append(lambda j=j: stat_sq(j, pair(RES, j), t_x)())
            out += [None, lambda: st.__setitem__("root", root(EPS)), None,
                    lambda: st.__setitem__("rx", newton(st["root"]))]
            for j in range(8):
                out.append(lambda j=j: xrtok.append(
                    tt("pool", XR[:, 2 * j:2 * j + 2, :], RES[:, 2 * j:2 * j + 2, :], over(Rv, 2), ALU.mult, st["rx"], t_x)))
            return out

        def norm1(half):
            c0 = 8 * half
            tm = stt(A1v[:, c0:c0 + 8], mod[:, 16 + c0:24 + c0], 1.0, v(V_N1 + c0, 8), ALU.add, ALU.mult, modtok[2 + half],
                     t_vec)
            for b in range(c0, c0 + 8):
                restok[b] = [t_x]
                sl, key = tslot(b)
                w = tfree.get(key, free["TG2"] + free["TG3"])
                g, sh, hi, lo = A1v[:, b:b + 1], mod[:, b:b + 1], Hhi[:, b, :], Hlo[:, b, :]
                th = act(hi, XR[:, b, :], ACT.Identity, xrtok[b // 2], tm, modtok[half], scale=g, bias=sh)
                t = ts("pool", sl, XR[:, b, :], g, ALU.mult, sh, ALU.add, xrtok[b // 2], tm, modtok[half], *w)
                tl = tt("dve", lo, sl, v32(hi), ALU.subtract, t, th)
                tfree[key] = [tl]
                hact["toks"][b] = [th, tl]
            close_t()
            st["norm_done"] = hact["toks"][b]
        folds = []
        call(lambda: norm1(0))

        xctok = [[] for _ in range(NB)]

        def evac_lrux(j):
            def f(ps, tp):
                out = []
                for i in range(2):
                    b = 2 * j + i
                    ta = act(XC[:, b, :], ps[:, i * 256:(i + 1) * 256], ACT.Identity, tp, t_vec, scale=v(V_CW + 48 + b),
                             bias=v(V_CB + b))
                for i in range(2):
                    b = 2 * j + i
                    o = XC[:, b, :]
                    p_ = ps[:, i * 256:(i + 1) * 256]
                    t = ta
                    for k in (2, 1, 0):
                        s = 3 - k
                        t = stt(o[:, s:S], p_[:, 0:S - s], v(V_CW + 16 * k + b), o[:, s:S], ALU.mult, ALU.add, t)
                    xctok[b] = [t]
                    out.append(t)
                return [out[-1]]
            return f

        def X():
            return hact
        held = [{} for _ in range(7)]
        for j in range(7):
            unit(w_in, j, 2, X, None, corder=(0, 1), part="open", hold=held[j])
        call(lambda: ([f() for f in folds], norm1(1)))
        for j in range(7):
            unit(w_in, j, 2, X, evac_lrux(j), corder=(2, 3), part="close", hold=held[j])
            if j == 0:
                steps.append(("ring", 6))
            if j == 3:
                call(decay)
            if j == 4:
                call(bias_table)
        unit(w_in, 7, 4, X, evac_lrux(7))

        qtok = [[] for _ in range(NB)]

        def evac_q(j):
            def f(ps, tp):
                src = mirrored(ps[:, :].rearrange("p (a q) -> p a q", q=128))
                t = act(pair(AT, j).rearrange("p (a q) -> p a q", q=128), src, ACT.Copy, tp)
                qtok[2 * j] = qtok[2 * j + 1] = [t]
                return [t]
            return f

        def evac_copy(dst, tokl, j, e="act"):
            def f(ps, tp):
                t = act(pair(dst, j), ps[:, :], ACT.Copy, tp)
                tokl[2 * j] = [t]
                tokl[2 * j + 1] = [t]
                return [t]
            return f
        LW = [at(f"LW{c}", [128, CH], o_lp + 4096 * c if c < 3 else o_kv + 4096) for c in range(4)]
        s_lw = dma_sem("s_lw")
        lwtok = []
        s_cst2 = dma_sem("s_cst2")
        t_cst2 = None

        def lru_weights():
            wait("act", [t_g, *(t for r in range(6, 10) for t in raw_free[r])])
            wait("pool", [t_g, t_sp])
            for c in range(4):
                t = dma("pool", LW[c][:, :], d_lru[c], s_lw, *st["norm_done"])
            lwtok.append(t)
        call(lru_weights)
        mmtok = [[] for _ in range(NB)]
        aatok = [[] for _ in range(NB)]

        def lru_gates(j):
            def f():
                w = LW[j // 2][:, :].rearrange("p (b g m) -> p b g m", b=4, g=2)
                tps = []
                for g, bk, key in ((0, pS, "S"), (1, pT, "T")):
                    for h in range(2):
                        b = 2 * j + h
                        fn = lambda e, g=g, h=h, b=b, bk=bk: e.matmul(
                            bk[:, h * 256:(h + 1) * 256], w[:, b % 4, g, :], XC[:, b, :], start=(h == 0), stop=True,
                            skip_group_check=True)
                        if h == 0:
                            quiet("pe", fn, lwtok[0], *free[key], *xctok[b])
                        else:
                            tps.append(op("pe", fn, *xctok[b]))
                if j == 7:
                    for k in ("LP0", "LP1", "LP2", "PT0", "PT1", "BT0", "BT1"):
                        free[k] = [tps[1]]

                def gates():
                    tg_ = []
                    for g, bk in ((0, pS), (1, pT)):
                        for h in range(2):
                            b = 2 * j + h
                            t = act(TG[:, g, h * 256:(h + 1) * 256], bk[:, h * 256:(h + 1) * 256], ACT.Tanh, tps[g], t_half,
                                    *free[f"TG{g}"], bias=v(V_BA + 16 * g + b), scale=0.5)
                        tg_.append(t)
                    free["S"], free["T"] = [tg_[0]], [tg_[1]]
                    h_, rc = pair(MM, j), TG[:, 2 + j % 2, :]
                    key = f"TG{2 + j % 2}"
                    for h in range(2):
                        b = 2 * j + h
                        tt_ = act(MM[:, b, :], TG[:, 0, h * 256:(h + 1) * 256], ACT.Tanh, tg_[0], t_sp,
                                  scale=SPH[:, b:b + 1], bias=SPH[:, b:b + 1])
                    free["TG0"] = [tt_]
                    tu = stt(pair(XC, j), TG[:, 1, :], 1.0, pair(XC, j), ALU.add, ALU.mult, tg_[1], tps[1])
                    free["TG1"] = [tu]
                    defer(1, lambda: roots(h_, rc, key, tt_, tu))

                def roots(h_, rc, key, tt_, tu):
                    td = ts("dve", rc, h_, -1.0, ALU.mult, 1.0, ALU.add, tt_, *free[key])
                    td = op("dve", lambda e: e.reciprocal(rc, rc), td)
                    ta = ts("dve", pair(AA, j), rc, 2.0, ALU.mult, -1.0, ALU.add, td)
                    td = op("dve", lambda e: e.memset(rc.rearrange("p (b s) -> p b s", b=2)[:, :, 0:1], 1.0), ta)
                    tu = tt("dve", pair(XC, j), pair(XC, j), rc, ALU.mult, td, tu)
                    free[key] = [tu]
                    for h in range(2):
                        xctok[2 * j + h] = [tu]
                        aatok[2 * j + h] = [ta]
                        mmtok[2 * j + h] = [td]
                defer(1, gates)
            return f

        def lru_scan():
            def part(q):
                sl = MM[:, 4 * q:4 * q + 4, :]
                t = act(sl, sl, ACT.Sqrt, *mmtok[4 * q + 3], scale=-1.0)
                t2_ = op("dve", lambda e, q=q: e.memset(MM[:, 4 * q:4 * q + 4, 0:1], 0.5), t)
                t3 = tt("dve", XC[:, 4 * q:4 * q + 4, :], XC[:, 4 * q:4 * q + 4, :], sl, ALU.mult, t2_, t,
                        *xctok[4 * q + 3])
                for b in range(4 * q, 4 * q + 4):
                    mmtok[b] = [op("dve", lambda e, b=b: e.tensor_tensor_scan(
                        MM[:, b, :], AA[:, b, :], XC[:, b, :], 0.0, ALU.mult, ALU.add), t3, *aatok[b])]
            for q in range(4):
                defer(2 * q, lambda q=q: part(q))

        ktok = [[], []]
        for j in range(8):
            unit(w_in, 8 + j, 4, X, evac_q(j))
            if j < 7:
                call(lambda j=j: defer(1, lru_gates(j)))
            if j == 6:
                call(lambda: defer(3, lru_gates(7)))
        unit(w_in, 16, 4, X, evac_copy(KT, ktok, 0))
        call(lambda: defer(1, lru_scan))
        vtok = [[]]

        def evac_tok(dst, c0, tokl, n=256):
            def f(ps, tp):
                t = act(dst[:, :, c0:c0 + n], ps[:, :].rearrange("p (t c) -> p t c", t=2), ACT.Copy, tp)
                tokl[0] = [t]
                return [t]
            return f
        unit(w_in, 17, 4, X, evac_tok(VT, 0, vtok), mode="t")

        s_bt = [dma_sem("s_bt0"), dma_sem("s_bt1")]
        jn = [0]

        def attn_steps(heads, nk, scale, bias, out, sink=None, pre=None, outtok=None, d64=False):
            n = jn[0]
            jn[0] += 1
            nkt = nk // 128
            L = LP[:, n % 3, :, 0:nk]
            lp, pt, sm = f"LP{n % 3}", f"PT{n % 2}", f"SM{n % 4}"
            mx, nm, rs, es, rd = (SM[:, n % 4, i, :] for i in range(5))
            Tv = pT[:, 0:2 * nkt * 128].rearrange("p (a q) -> p a q", q=128)
            Pv = PT[:, n % 2, 0:2 * nkt, :]
            s = {}

            def s0():
                bi, bt = (None, []) if bias is None else bias()
                for i, (q, k, _, tk) in enumerate(heads()):
                    fn = lambda e, q=q, k=k, i=i: e.matmul(pS2[:, i, 0:nk], q, k, start=True, stop=True,
                                                           skip_group_check=True)
                    tp = op("pe", fn, *tk, *free["S"])

                def logits():
                    sv = pS2[:, :, 0:nk]
                    if bi is None:
                        t = ts("dve", L, sv, scale, ALU.mult, None, None, tp, *free[lp])
                    else:
                        t = stt(L, sv, scale, bi, ALU.mult, ALU.add, tp, *bt, *free[lp])
                    s["bias_read"] = t
                    free["S"] = [t]
                    if pre:
                        pre(t)
                    if sink is None:
                        t = op("dve", lambda e: e.tensor_reduce(nm, L, AX.X, ALU.max, negate=True), t, *free[sm])
                    else:
                        t = op("dve", lambda e: e.tensor_reduce(mx, L, AX.X, ALU.max), t, *free[sm])
                        t = tt("dve", mx, mx, sink, ALU.max, t, t_vec)
                        t = ts("dve", nm, mx, -1.0, ALU.mult, None, None, t)
                        s["es"] = tt("dve", es, sink, nm, ALU.add, t)
                    s["nm"] = t

                def exps():
                    t = s["nm"]
                    for i in range(2):
                        te = op("act", lambda e, i=i: e.activation(L[:, i, :], L[:, i, :], ACT.Exp, bias=nm[:, i:i + 1],
                                                                   accum_out=rs[:, i:i + 1]), t)
                    if sink is not None:
                        te = act(es, es, ACT.Exp, s["es"])
                    s["e"] = te
                return [logits, exps] if st["span"] > 2 else [lambda: (logits(), exps())]

            def s1():
                t = s["e"]
                if sink is not None:
                    t = tt("dve", rs, rs, es, ALU.add, t)
                t = op("dve", lambda e: e.reciprocal(rd, rs), t)

                def weigh():
                    for i in range(2):
                        t2_ = act(L[:, i, :], L[:, i, :], ACT.Copy, t, scale=rd[:, i:i + 1])
                    free[sm] = [t2_]
                    s["p"] = t2_
                return [weigh]

            def s2():
                for i in range(2):
                    for k in range(nkt):
                        a = i * nkt + k
                        fn = lambda e, i=i, k=k, a=a: e.transpose(Tv[:, a, :], L[:, i, k * 128:(k + 1) * 128], ident)
                        tp = op("pe", fn, s["p"], t_cst, *free["T"])
                free[lp] = [tp]

                def copy():
                    t = act(Pv, Tv, ACT.Copy, tp, *free[pt])
                    free["T"] = [t]
                    s["pt"] = t
                if st["span"] > 2:
                    return [copy]
                copy()

            def s3():
                hs = heads()
                for i in range(2):
                    o = pO[i * 64:(i + 1) * 64, 0:128] if d64 else pO[:, i * 128:(i + 1) * 128]
                    for k in range(nkt):
                        fn = lambda e, i=i, k=k, o=o, w=hs[i][2][k]: e.matmul(
                            o, w, Pv[:, i * nkt + k, :], start=(k == 0), stop=(k == nkt - 1), skip_group_check=True)
                        tp = op("pe", fn, s["pt"], *hs[i][3], *free["O"])
                free[pt] = [tp]
                src = mirrored(pO[:, 0:128]) if d64 else pO[:, 0:256].rearrange("p (a q) -> p a q", a=2)
                t = act(out, src, ACT.Copy, tp, *(s.get("war", [])))
                free["O"] = [t]
                outtok(t)
            return [s0, s1, s2, s3], s

        bt_at = {}
        ytok = [[] for _ in range(NB)]
        qk_done = {}

        def load_bt(b):
            def f():
                k = b % 2
                for i, h in enumerate(PERM[b]):
                    src = bass.AP(tensor=gdram.tensor, offset=h * 384, ap=[[1, 128], [1, 256]])
                    t = dma("pool", BT[:, k, i, :], src, s_bt[k], t_g, *free[f"BT{k}"])
                bt_at[b] = t
            return f

        def att_jobs():
            st["span"] = 3
            load_bt(0)()
            load_bt(1)()
            for b in range(NB):
                grp = b // 8
                for t in (0, 1):
                    nk = 128 * (t + 1)

                    def heads(b=b, t=t, nk=nk, grp=grp):
                        out = []
                        for i in range(2):
                            r = slice(64 * i, 64 * i + 64)
                            g = 2 * grp + i
                            out.append((AT[r, b, t * 128:(t + 1) * 128], KT[r, grp, 0:nk],
                                        [VT[:, k, g * 64:(g + 1) * 64] for k in range(t + 1)],
                                        [*qtok[b], *ktok[0], *vtok[0]]))
                        return out

                    def bias(b=b, t=t, nk=nk):
                        return BT[:, b % 2, :, 256 - nk:256], [bt_at[b]]

                    def pre(tok, b=b, t=t):
                        if t == 1:
                            free[f"BT{b % 2}"] = [tok]
                            if b + 2 < NB:
                                load_bt(b + 2)()

                    def done(tok, b=b):
                        ytok[b] = ytok[b] + [tok]
                    js, _ = attn_steps(heads, nk, SC1, bias, AT[:, b, t * 128:(t + 1) * 128],
                                       sink=v(V_SINK + 2 * b, 2), pre=pre, outtok=done, d64=True)
                    jobs.append(js)
        call(att_jobs)

        G0, G1 = 2 * 0.7978845608028654, 2 * 0.7978845608028654 * 0.044715
        ztok = [[] for _ in range(NB)]
        zact = {"hi": Zh, "lo": Zl, "toks": ztok}

        def split_out(hi, lo, src, t, key, *w):
            th = act(hi, src, ACT.Copy, t, *w)
            tl = tt("dve", lo, src, v32(hi), ALU.subtract, t, th, *w)
            free[key] = [th, tl]
            return [th, tl]

        def evac_gate(j):
            def f(ps, tp):
                g0, g1, g2 = TG[:, 0, :], TG[:, 1, :], TG[:, 2, :]
                t = act(g0, ps[:, :], ACT.Square, tp, *free["TG0"])
                t = ts("dve", g0, g0, 0.5 * G1, ALU.mult, 0.5 * G0, ALU.add, t)
                t = tt("dve", g0, g0, ps[:, :], ALU.mult, t)
                fr = []

                def more(t=t):
                    t = act(g1, g0, ACT.Tanh, t, *free["TG1"])
                    free["TG0"] = [t]
                    t = stt(g1, g1, 1.0, ps[:, :], ALU.add, ALU.mult, t)
                    fr.append(t)
                    t = stt(g2, g1, 0.5, pair(MM, j), ALU.mult, ALU.mult, t, *mmtok[2 * j + 1], *free["TG2"])
                    free["TG1"] = [t]
                    mmtok[2 * j] = mmtok[2 * j + 1] = [t]

                    def parts():
                        tk = split_out(pair(Zh, j), pair(Zl, j), g2, t, "TG2", *mmtok[15])
                        ztok[2 * j] = ztok[2 * j + 1] = tk
                    defer(1, parts)
                defer(1, more)
                return fr
            return f

        gtok = [[] for _ in range(NB)]

        def evac_sig(dst, j, war):
            def f(ps, tp):
                t = act(pair(dst, j), ps[:, :], ACT.Tanh, tp, *war(j), scale=0.5)
                gtok[2 * j] = gtok[2 * j + 1] = [t]
                return [t]
            return f

        def evac_ya(j):
            def f(ps, tp):
                t = stt(pair(MM, j), pair(MM, j), 1.0, ps[:, :], ALU.add, ALU.mult, tp, *gtok[2 * j])
                mmtok[2 * j] = mmtok[2 * j + 1] = [t]
                return [t]
            return f
        for j in range(8):
            unit(w_in, 18 + j, 4, X, evac_gate(j))
            unit(w_in, 26 + j, 4, X, evac_sig(MM, j, lambda j: mmtok[2 * j]))
        for j in range(8):
            unit(w_lo, j, 4, lambda: zact, evac_ya(j))
        TB = at("TB", [128, NB, S], o_a + 16384)
        for j in range(8):
            unit(w_in, 34 + j, 4, X, evac_sig(TB, j, lambda j: [st["ya_end"]]))
            if j == 0:
                steps.insert(len(steps) - 1, ("call", lambda: st.__setitem__("ya_end", st["pe"])))

        def att_split():
            st["span"] = 2
            flush_later()
            drain_jobs()

            def quarter(q):
                src = AT[:, 4 * q:4 * q + 4, :]
                w = [x for b in range(4 * q, 4 * q + 4) for x in ytok[b]]
                th = act(Hhi[:, 4 * q:4 * q + 4, :], src, ACT.Copy, st["pe"], *w)
                tl = tt("dve", Hlo[:, 4 * q:4 * q + 4, :], src, v32(Hhi[:, 4 * q:4 * q + 4, :]), ALU.subtract, th, st["pe"], *w)
                for b in range(4 * q, 4 * q + 4):
                    hact["toks"][b] = [th, tl]
                st["att_read"] = [th, tl]
            for q in range(4):
                defer(1 + q, lambda q=q: quarter(q))
        steps.insert(len(steps) - 1, ("call", att_split))
        Gh = at("Gh", [128, NB, S], o_a, F32R)
        Gl = at("Gl", [128, NB, S], o_a + 32768, F32R)
        mgtok = [[] for _ in range(NB)]
        mact = {"hi": Gh, "lo": Gl, "toks": mgtok}

        def evac_yb(j):
            def f(ps, tp):
                g0, g1 = TG[:, 0, :], TG[:, 1, :]
                t = stt(g0, pair(TB, j), 1.0, ps[:, :], ALU.add, ALU.mult, tp, *gtok[2 * j], *free["TG0"])
                fr = [t]
                t = tt("dve", g1, g0, pair(MM, j), ALU.add, t, *mmtok[2 * j], *free["TG1"])
                free["TG0"] = [t]
                st["mm_read"] = t

                def parts():
                    th = act(pair(Gh, j), g1, ACT.Copy, t, *st["att_read"], scale=0.5)
                    tl = stt(pair(Gl, j), g1, 0.5, v32(pair(Gh, j)), ALU.mult, ALU.subtract, t, th, st["ya_end"])
                    free["TG1"] = [th, tl]
                    mgtok[2 * j] = mgtok[2 * j + 1] = [th, tl]
                defer(1, parts)
                return fr
            return f
        for j in range(8):
            unit(w_ao, j, 4, X, evac_yb(j))

        def evac_res(j, gcol, stat, gg):
            def f(ps, tp):
                for i in range(2):
                    b = 2 * j + i
                    t = stt(RES[:, b, :], ps[:, i * 256:(i + 1) * 256], mod[:, gcol + b:gcol + b + 1], RES[:, b, :],
                            ALU.mult, ALU.add, tp, modtok[gg[0]], modtok[gg[1]], *restok[b])
                    restok[b] = [t]
                if stat:
                    square_up(j, t)
                return [t]
            return f
        at_w_o = []
        for j in range(8):
            unit(w_o, j, 4, lambda: mact, evac_res(j, 32, True, (4, 5)))
            if 2 <= j < 6:
                at_w_o.append(len(steps))

        memtok0 = [None] * 4
        mem0 = {"hi": Mh0, "lo": Ml0}

        def mem_act(m, tk):
            return lambda: {**m, "toks": [tk[k // 4] for k in range(NB)]}
        w_kv, w_2, w_o2 = d_w["kv"], d_w["in2"], d_w["out2"]

        def mem_load(m, tk, after, q):
            return ("mem", dict(q=q, dst=(m["hi"], m["lo"]), done=tk, after=after))
        for q in (3, 2, 1, 0):
            steps.insert(at_w_o[q], mem_load(mem0, memtok0, lambda: [st["mm_read"]], q))
        kvtok = {"k": [[] for _ in range(4)], "v": [[], []]}
        
        def kv_war():
            return [st["kv_end"]]

        def evac_km(j):
            def f(ps, tp):
                t = act(pair(KM, j), ps[:, :], ACT.Copy, tp, *kv_war())
                kvtok["k"][2 * j] = kvtok["k"][2 * j + 1] = [t]
                return [t]
            return f

        def evac_vm(j):
            def f(ps, tp):
                t = act(VM[:, :, j * 256:(j + 1) * 256], ps[:, :].rearrange("p (t c) -> p t c", t=2), ACT.Copy, tp,
                        *kv_war())
                kvtok["v"][j] = [t]
                return [t]
            return f

        def kv_unit(layer, j, m, tk):
            unit(w_kv, 4 * layer + j, 4, mem_act(m, tk), evac_km(j) if j < 2 else evac_vm(j - 2), mode="f" if j < 2 else "t")

        def norm2():
            last = st["pe"]

            def head():
                tr = rstd(EPS)
                t = stt(A2v[:, :], mod[:, 64:80], 1.0, v(V_N2, 16), ALU.add, ALU.mult, modtok[8], modtok[9], t_vec)
                for q in range(9):
                    def blocks(q=q):
                        low_parts()
                        for b in range(2 * q, min(NB, 2 * q + 2)):
                            emit_h(b, "mod", tr, A2v[:, b:b + 1], mod[:, 48 + b:49 + b], last,
                                   tmod=[t, modtok[6], modtok[7]])
                        if q == 8:
                            close_t()
                    defer(1 + q, blocks)
            defer(2, head)
        call(norm2)
        call(lambda: st.__setitem__("lag", True))

        call(lambda: st.__setitem__("kv_end", st["pe"]))
        kv_unit(0, 0, mem0, memtok0)
        kv_unit(0, 1, mem0, memtok0)

        ftok = [[[] for _ in range(8)] for _ in range(2)]
        fread = [[], []]

        def evac_ff1(f_, j):
            def f(ps, tp):
                k = f_ % 2
                a, b_ = TG[:, 2 * (j % 2), :], TG[:, 2 * (j % 2) + 1, :]
                ka, kb = f"TG{2 * (j % 2)}", f"TG{2 * (j % 2) + 1}"
                t = act(a, ps[:, :], ACT.Relu, tp, *free[ka])
                fr = [t]
                t = act(b_, a, ACT.Square, t, *free[kb])
                free[ka] = [t]
                tk = split_out(pair(Fh[k], j), pair(Fl[k], j), b_, t, kb, *fread[k])
                ftok[k][2 * j] = ftok[k][2 * j + 1] = tk
                return fr
            return f

        def ff1(f_):
            if f_ < 2:
                call(lambda: fread.__setitem__(f_, [st["ffw"]]))
            for j in range(4):
                unit(w_f1, 4 * f_ + j, 4, X, evac_ff1(f_, j))

        def ff2(f_):
            k = f_ % 2
            for j in range(8):
                unit(w_f2, j, 2, lambda k=k: {"hi": Fh[k], "lo": Fl[k], "toks": ftok[k]},
                     evac_res(j, 80, f_ == 7, (10, 11)), kc0=2 * f_)
            call(lambda k=k: fread.__setitem__(k, [st["pe"]]))
        call(lambda: st.__setitem__("ffw", st["pe"]))
        ff1(0)
        for f_ in range(1, 8):
            ff1(f_)
            ff2(f_ - 1)
        steps.append(("ring", 5))
        ff2(7)

        def norm3():
            nonlocal t_cst2
            last = st["pe"]
            t_cst2 = dma("pool", cst[:, C_DUP:], d_cst[:, C_DUP:], s_cst2, *raw_free[5])

            def head():
                tr = rstd(EPS)
                for q in range(9):
                    def blocks(q=q):
                        low_parts()
                        for b in range(2 * q, min(NB, 2 * q + 2)):
                            emit_h(b, "rms", tr, v(V_FG + b), None, last)
                    defer(1 + q, blocks)
            defer(2, head)
        call(norm3)
        kv_unit(0, 2, mem0, memtok0)
        kv_unit(0, 3, mem0, memtok0)

        memtok1 = [None] * 4
        mem1 = {"hi": Mh1, "lo": Ml1}

        s_rot = dma_sem("s_rot")

        def layer(l):
            tk = {n: [[] for _ in range(8)] for n in ("DQ", "DK", "FQ", "FK", "MQ", "IQ")}
            tk1 = {n: [[]] for n in ("DV", "FV")}
            s_ = {}
            a_war = lambda: [st["a_end"]]
            call(lambda: st.__setitem__("a_end", st["pe"]))
            call(lambda: [wait(e, [t_cst2]) for e in ("pe", "dve")])

            def evac_rope(dst, j, cc, name):
                def f(ps, tp):
                    g0, g1, g2 = TG[:, 0, :], TG[:, 1, :], TG[:, 2, :]
                    t = act(g0, ps[:, :], ACT.Copy, tp, *free["TG0"])
                    half = cc[0]
                    for r in range(0, 128, 2 * half):
                        dma("pool", g2[r:r + half, :], g0[r + half:r + 2 * half, :], s_rot, t, *free["TG2"])
                        tr = dma("pool", g2[r + half:r + 2 * half, :], g0[r:r + half, :], s_rot)

                    def rest():
                        v3 = lambda a: a.rearrange("p (b s) -> p b s", b=2)
                        t1_ = tt("dve", v3(g1), v3(g0), over(cst[:, cc[1]:cc[1] + 256], 2), ALU.mult, t, *free["TG1"])
                        t2_ = tt("dve", v3(g2), v3(g2), over(cst[:, cc[2]:cc[2] + 256], 2), ALU.mult, tr)
                        free["TG0"] = [tr, t1_]
                        t3 = tt("dve", pair(dst, j), g1, g2, ALU.add, t1_, t2_, *a_war())
                        free["TG1"] = free["TG2"] = [t3]
                        tk[name][2 * j] = tk[name][2 * j + 1] = [t3]
                    defer(4, rest)
                    return [t]
                return f
            R64 = (32, C_COS64, C_SIN64)
            R128 = (64, C_COS128, C_SIN128)

            def evac_plain(dst, j, name):
                def f(ps, tp):
                    t = act(pair(dst, j), ps[:, :], ACT.Copy, tp, *a_war())
                    tk[name][2 * j] = tk[name][2 * j + 1] = [t]
                    return [t]
                return f

            def evac_v(dst, j, name):
                def f(ps, tp):
                    t = act(dst[:, :, j * 256:(j + 1) * 256], ps[:, :].rearrange("p (t c) -> p t c", t=2), ACT.Copy,
                            tp, *a_war())
                    tk1[name][0] = tk1[name][0] + [t]
                    return [t]
                return f

            def evac_small(ps, tp):
                g0, g1, g2 = TG[0:86, 0, 0:256], TG[:, 1, 0:256], TG[:, 2, 0:256]
                t = act(g0, ps[0:86, 0:256], ACT.Copy, tp, *free["TG0"])

                def rest():
                    k0 = TG[0:64, 0, 0:256]
                    same, swap = cst[0:64, C_DUP:C_DUP + 128], cst[0:64, C_SWAP:C_SWAP + 128]
                    quiet("pe", lambda e: e.matmul(pM[:, 0:256], same, k0, start=True, stop=True, skip_group_check=True),
                          t, t_cst, *free["M"])
                    tq = op("pe", lambda e: e.matmul(pM[:, 256:512], swap, k0, start=False, stop=True,
                                                     skip_group_check=True))
                    t1_ = tt("dve", g1, pM[:, 0:256], cst[:, C_COS64:C_COS64 + 256], ALU.mult, tq, *free["TG1"])
                    t2_ = tt("dve", g2, pM[:, 256:512], cst[:, C_SIN64:C_SIN64 + 256], ALU.mult, tq, *free["TG2"])
                    free["M"] = [t2_]
                    t3 = tt("dve", IK[:, :], g1, g2, ALU.add, t1_, t2_)
                    free["TG1"] = free["TG2"] = [t3]
                    s_["ik"] = t3

                def turn():
                    for n in range(2):
                        tq = op("pe", lambda e, n=n: e.transpose(pM[:, n * 86:n * 86 + 86], TG[0:86, 0, n * 128:n * 128 + 128],
                                                                 cst[0:86, C_ID:C_ID + 86]), t, *free["M"])
                    free["TG0"] = [tq]
                    tw = act(TK[:, :, :], pM[:, 0:172].rearrange("p (t c) -> p t c", t=2)[:, :, 64:86], ACT.Copy, tq)
                    free["M"] = [tw]
                    defer(1, lambda: logs(tw))

                def logs(tw):
                    s_["w"] = ts("dve", TK[:, :, 0:16], TK[:, :, 0:16], 0.25, ALU.mult, None, None, tw)
                    c6 = lambda i: SMALL[:, i, 0:12]
                    z = c6(0).rearrange("p (t h) -> p t h", t=2)
                    bf = v(V_BF + 6 * l, 6)
                    ta = tt("dve", z, TK[:, :, 16:22], over(bf, 2), ALU.add, tw, t_vec)
                    tb = ts("dve", LF[:, :, :], z, 0.0, ALU.min, None, None, ta)
                    ta = stt(c6(0), c6(0), -1.0, c6(0), ALU.mult, ALU.max, tb)
                    p_, ta = log1p_exp(lambda i: c6(1 + i), c6(0), 12, ta)
                    lf = LF[:, :, :].rearrange("p t h -> p (t h)")
                    ta = stt(lf, p_, -2.0, lf, ALU.mult, ALU.add, ta)
                    s_["lf"] = ta
                    defer(2, sums)

                def sums():
                    ta = s_["lf"]
                    quiet("pe", lambda e: e.matmul(pM[:, 0:6], U[:, 0:128], LF[:, 0, :], start=True, stop=True,
                                                   skip_group_check=True), ta, *free["M"])
                    quiet("pe", lambda e: e.matmul(pM[:, 6:12], ones, LF[:, 0, :], start=True, stop=False,
                                                   skip_group_check=True))
                    tq = op("pe", lambda e: e.matmul(pM[:, 6:12], U[:, 0:128], LF[:, 1, :], start=False, stop=True,
                                                     skip_group_check=True))
                    tc = op("dve", lambda e: e.tensor_copy(CQ[:, :, :], pM[:, 0:12].rearrange("p (t h) -> p t h", t=2)), tq)
                    free["M"] = [tc]
                    s_["cq"] = tc
                defer(3, rest)
                defer(4, turn)
                return [t]

            sc_t = [SC[:, 0:128], SC[:, 128:384]]
            sctok = [[], []]

            def idx_steps(t, b):
                nk = 128 * (t + 1)
                n = jn[0]
                jn[0] += 1
                L = LP[:, n % 3, :, 0:nk]
                lp = f"LP{n % 3}"
                x_ = {}

                def s0():
                    for i in range(2):
                        r = slice(64 * i, 64 * i + 64)
                        tp = op("pe", lambda e, i=i, r=r: e.matmul(
                            pS2[:, i, 0:nk], IQ[r, b, t * 128:(t + 1) * 128], IK[r, 0:nk], start=True,
                            stop=True, skip_group_check=True), *tk["IQ"][b], s_["ik"], *free["S"])
                    sv = pS2[:, :, 0:nk]
                    ta = act(L, sv, ACT.Relu, tp, *free[lp], scale=0.125)
                    free["S"] = [ta]
                    x_["a"] = ta

                def s1():
                    ta = x_["a"]
                    for i in range(2):
                        w = TK[:, t, 2 * b + i:2 * b + i + 1]
                        if b == 0 and i == 0:
                            ta = ts("dve", sc_t[t], L[:, 0, :], w, ALU.mult, None, None, ta, s_["w"],
                                    *st.get("sc_read", []))
                        else:
                            ta = stt(sc_t[t], L[:, i, :], w, sc_t[t], ALU.mult, ALU.add, ta, x_["a"], *sctok[t])
                        sctok[t] = [ta]
                    free[lp] = [ta]
                return [s0, s1]

            def causal(ap, t, nk, reps, tok):
                pat = [[-1, nk]] if reps == 1 else [[0, reps], [-1, nk]]
                return op("pool", lambda e: e.affine_select(out=ap, in_=ap, pattern=pat, compare_op=ALU.is_ge, fill=NEG,
                                                            base=128 * t, channel_multiplier=1), *tok)

            def top_steps(t):
                nk = 128 * (t + 1)
                a = sc_t[t]

                def start():
                    sctok[t] = [causal(a, t, nk, 1, sctok[t])]

                def rnd():
                    t_ = op("dve", lambda e: e.max(MX8[:, t, :], a), *sctok[t])
                    sctok[t] = [op("dve", lambda e: e.match_replace(a, MX8[:, t, :], a, TAKEN), t_)]

                def end():
                    t_ = ts("dve", a, a, -2e38, ALU.is_ge, NEG, ALU.mult, *sctok[t])
                    sctok[t] = [causal(a, t, nk, 1, [t_])]
                return [[start, rnd], [rnd], [rnd], [rnd], [rnd], [rnd], [rnd], [rnd, end]]

            def big_attn(Q, K, V_, n, y0, pairs, qn, kn, vn, bias_of, nk_of, scale=SC2):
                for pr in range(pairs):
                    for t in (0, 1):
                        nk = nk_of(t)

                        def heads(pr=pr, t=t, nk=nk):
                            out = []
                            for i in range(2):
                                h = 2 * pr + i
                                tks = [*kn(h), *vn(), *qn(h)]
                                out.append((Q[:, h, t * 128:(t + 1) * 128], K[:, h, 0:nk],
                                            [V_[:, k, h * 128:(h + 1) * 128] for k in range(nk // 128)], tks))
                            return out

                        def done(tok, pr=pr):
                            for i in range(2):
                                ytok[y0 + 2 * pr + i] = ytok[y0 + 2 * pr + i] + [tok]
                        pre, bi, fb = bias_of(pr, t, nk)
                        js, sd = attn_steps(heads, nk, scale, bi, Y[:, y0 + 2 * pr:y0 + 2 * pr + 2, t * 128:(t + 1) * 128],
                                            pre=fb, outtok=done)
                        sd["war"] = [st["a_end"]]
                        jobs.append(([pre] if pre else []) + js)

            def fox_bias(pr, t, nk):
                x_ = {}
                kk = [0]

                def pre():
                    k = fx[0] % 2
                    fx[0] += 1
                    kk[0] = k
                    for i in range(2):
                        h = 2 * pr + i
                        o = pM[:, i * 256:i * 256 + 256]
                        w0, w1 = spread(LF[:, 0, h:h + 1], 128), spread(LF[:, 1, h:h + 1], 128)
                        tp = op("pe", lambda e, o=o, w0=w0, i=i: e.matmul(o[:, 0:nk], w0, U[:, 0:nk], start=(i == 0), stop=(t == 0),
                                                                     skip_group_check=True), s_["lf"], *free["M"])
                        if t:
                            tp = op("pe", lambda e, o=o, w1=w1: e.matmul(o[:, 128:256], w1, U[:, 0:128], start=False,
                                                                         stop=True, skip_group_check=True))
                    for i in range(2):
                        h = 2 * pr + i
                        td = ts("dve", BT[:, k, i, 0:nk], pM[:, i * 256:i * 256 + nk], -1.0, ALU.mult,
                                CQ[:, t, h:h + 1], ALU.add, tp, s_["cq"], *free[f"BT{k}"])
                    free["M"] = [td]
                    x_["d"] = causal(BT[:, k, :, 0:nk], t, nk, 2, [td])

                def used(tok):
                    free[f"BT{kk[0]}"] = [tok]
                return pre, (lambda: (BT[:, kk[0], :, 0:nk], [x_["d"]])), used

            def dsa_bias(pr, t, nk):
                def used(tok):
                    st["sc_read"] = [tok]
                return None, (lambda: (over(sc_t[t], 2), sctok[t])), used

            def mem_bias(pr, t, nk):
                return None, None, None
            fx = [0]
            c0 = 32 * l
            for j in range(2):
                unit(w_2, c0 + 10 + j, 4, X, evac_plain(MQ, j, "MQ"))
            unit(d_s2, l, 4, X, evac_small, mode="s", width=86)
            call(lambda: big_attn(MQ, KM, VM, 4, 12, 2, lambda h: tk["MQ"][h], lambda h: kvtok["k"][h],
                                  lambda: [*kvtok["v"][0], *kvtok["v"][1]], mem_bias, lambda t: 256))
            for j in range(4):
                unit(w_2, c0 + j, 4, X, evac_rope(IQ, j, R64, "IQ"))

            def start_idx():
                for t in (0, 1):
                    for b in range(8):
                        jobs.append(idx_steps(t, b))
                for g in zip(top_steps(0), top_steps(1)):
                    jobs.append([(lambda g=g: [f() for x in g for f in x] and None)])
            for j in range(3):
                unit(w_2, c0 + 4 + j, 4, X, evac_rope(DQ, j, R128, "DQ"))
                if j == 0:
                    call(start_idx)
            for j in range(3):
                unit(w_2, c0 + 7 + j, 4, X, evac_rope(DK, j, R128, "DK"))
            for j in range(3):
                unit(w_2, c0 + 12 + j, 4, X, evac_v(DV, j, "DV"), mode="t")
            call(lambda: big_attn(DQ, DK, DV, 6, 6, 3, lambda h: tk["DQ"][h], lambda h: tk["DK"][h],
                                  lambda: tk1["DV"][0], dsa_bias, lambda t: 128 * (t + 1)))
            for j in range(3):
                unit(w_2, c0 + 15 + j, 4, X, evac_plain(FQ, j, "FQ"))
            for j in range(3):
                unit(w_2, c0 + 18 + j, 4, X, evac_plain(FK, j, "FK"))
            for j in range(3):
                unit(w_2, c0 + 21 + j, 4, X, evac_v(FV, j, "FV"), mode="t")
            call(lambda: big_attn(FQ, FK, FV, 6, 0, 3, lambda h: tk["FQ"][h], lambda h: tk["FK"][h],
                                  lambda: tk1["FV"][0], fox_bias, lambda t: 128 * (t + 1)))

            yact = {"hi": Yh, "lo": Yl, "toks": [[] for _ in range(NB)]}

            def evac_silu(j):
                def f(ps, tp):
                    g0, g1, g2 = TG[:, 0, :], TG[:, 1, :], TG[:, 2, :]
                    need = 2 if j >= 0 else 0
                    while any(len(ytok[b]) < need for b in (2 * j, 2 * j + 1)):
                        advance()
                    while any(len(ytok[b]) < need for b in range(6, 12)):
                        advance()
                    t = act(g0, ps[:, :], ACT.Tanh, tp, *free["TG0"], scale=0.5)
                    fr = []
                    ys = [x for b in (2 * j, 2 * j + 1, *range(6, 12)) for x in ytok[b]]

                    def more(t=t):
                        t = stt(g1, g0, 1.0, ps[:, :], ALU.add, ALU.mult, t, *free["TG1"])
                        free["TG0"] = [t]
                        fr.append(t)
                        t = stt(g2, g1, 0.5, pair(Y, j), ALU.mult, ALU.mult, t, *ys, *free["TG2"])
                        free["TG1"] = [t]

                        def parts():
                            tkk = split_out(pair(Yh, j), pair(Yl, j), g2, t, "TG2", t, *ys)
                            yact["toks"][2 * j] = yact["toks"][2 * j + 1] = tkk
                        defer(1, parts)
                    defer(1, more)
                    return fr
                return f
            for n, j in enumerate((3, 4, 5, 6, 7, 0, 1, 2)):
                unit(w_2, c0 + 24 + n, 4, X, evac_silu(j))
            call(drain_jobs)

            def shift_pair(j):
                t = tt("dve", RES[:, 2 * j:2 * j + 2, :], RES[:, 2 * j:2 * j + 2, :], over(R2, 2), ALU.subtract,
                       st["mu"], *restok[2 * j])
                restok[2 * j] = restok[2 * j + 1] = [t]
                if j == 0:
                    st["zs"] = act(sumT, pair(RES, 0), ACT.Copy, t, *free["LP1"])
                elif j < 7:
                    st["zs"] = tt("pool", sumT, sumT, pair(RES, j), ALU.add, t, st["zs"])
                square_up(j, t)
                if j == 7:
                    def totz():
                        total(pT, "zs", sumT, pair(RES, 7), t, "statz")
                        free["LP1"] = [st["statz"]]
                    defer(2, totz)

            def evac_y(j):
                def f(ps, tp):
                    t = stt(pair(RES, j), pair(RES, j), ALPHA, ps[:, :], ALU.mult, ALU.add, tp, *restok[2 * j],
                            *restok[2 * j + 1])
                    restok[2 * j] = restok[2 * j + 1] = [t]
                    if j == 1:
                        def mean():
                            for n in range(4):
                                q = op("pe", lambda e, n=n: e.matmul(pS[:, 0:256], ones, RES[:, n, :], start=(n == 0),
                                                                     stop=(n == 3), skip_group_check=True),
                                       *restok[n], *free["S"])
                            st["mu"] = ts("dve", R2, pS[:, 0:256], 1.0 / 512, ALU.mult, None, None, q, *free["BT0"],
                                          *free["BT1"])
                            free["S"] = [st["mu"]]
                        defer(2, mean)
                        defer(2, lambda: shift_pair(0))
                        defer(3, lambda: shift_pair(1))
                    if j > 1:
                        shift_pair(j)
                    return [t]
                return f
            if l == 0:
                call(lambda: st.__setitem__("m1", st["pe"]))
            for j in range(8):
                unit(w_o2, 8 * l + j, 4, lambda: yact, evac_y(j), corder=(2, 3, 0, 1))
                if l == 0 and 2 <= j < 6:
                    steps.append(mem_load(mem1, memtok1, lambda: [st["m1"]], j - 2))
            call(lambda: [ytok.__setitem__(b, []) for b in range(NB)])

            def norm():
                last = st["pe"]

                def tail():
                    w = free["BT0"] + free["BT1"]
                    td = ts("dve", R4, pT[:, 0:256], 1.0 / D, ALU.mult, None, None, st["statz"], *w)
                    free["T"] = [td]
                    t = tt("dve", R3, R4, R4, ALU.mult, td)
                    st["dm2"] = t
                    st["td"] = td

                def center(j):
                    o = RES[:, 2 * j:2 * j + 2, :]
                    tz = tt("pool" if l == 1 and j > 4 else "dve", o, o, over(R4, 2), ALU.subtract, st["td"],
                            *restok[2 * j], st["stat"], st["statz"])
                    restok[2 * j] = restok[2 * j + 1] = [tz]

                def head():
                    tail()
                    if l == 1:
                        Rq = LP[:, 2, 0, :]
                        for j in (5, 6, 7):
                            center(j)
                        tr = root(LN_EPS, st["dm2"], free["LP2"], Rq)
                        for j in range(5):
                            center(j)
                        tr = newton(tr, Rq)
                        for b in range(NB):
                            emit_h(b, "out", tr, v(V_LNG + 16 + b), v(V_LNB + 16 + b), last)
                            if b % 2:
                                dma("sp", d_out[:, b - 1:b + 1, :], RES[:, b - 1:b + 1, :], s_out,
                                    *restok[b - 1], *restok[b])
                        close_t()
                        return
                    for q in range(4):
                        def pairs(q=q):
                            center(2 * q)
                            center(2 * q + 1)
                            if q == 3:
                                st["zm"] = [x for z in range(NB) for x in restok[z]]
                                st["tr"] = rstd(LN_EPS, st["dm2"], st["zm"])
                        defer(1 + q, pairs)
                    for q in range(9):
                        def blocks(q=q):
                            low_parts()
                            for b in range(2 * q, min(NB, 2 * q + 2)):
                                emit_h(b, "ln", st["tr"], v(V_LNG + b), v(V_LNB + b), last)
                            if q == 8:
                                close_t()
                        defer(5 + q, blocks)
                defer(2, head)
            call(norm)
            if l == 0:
                call(lambda: st.__setitem__("kv_end", st["pe"]))
                for j in range(4):
                    kv_unit(1, j, mem1, memtok1)
            if l == 1:
                call(flush_later)
        s_out = dma_sem("s_out")
        call(lambda: [ytok.__setitem__(b, []) for b in range(NB)])
        layer(0)
        layer(1)

        nw = [0]
        background = [dict(kind="ada", g=g, kt=kt) for g in range(4, 12) for kt in range(NB)]
        order = []

        def add(el):
            stream.append(el)
            return len(stream) - 1

        def add_ada(g, kt):
            add(dict(kind="ada", g=g, kt=kt, n=CH, src=d_ada[g, kt]))
        first = [(g, kt) for g in (2, 0, 3, 1) for kt in range(NB)]

        def modulation(n):
            for _ in range(n):
                add_ada(*first.pop(0))
        modulation(26)
        bg = 0
        chunks = 0
        pause = 0
        due = 0
        sizes = [(0, 10)]

        def max_slots(i):
            return [n for k, n in sizes if k <= i][-1]

        for kind, s in steps:
            if kind == "ring":
                sizes.append((len(stream), s))
            if kind == "unit":
                s["ids"] = []
                if s["part"] == "close":
                    modulation(max(0, len(first) - 6))
                for c in range(s["nkc"]):
                    n = 4 * s["width"]
                    i = add(dict(kind="w", n=n, slot=nw[0] % NSP, src=s["src"][s["u"], s["kc0"] + s["corder"][c]]))
                    nw[0] += 1
                    order.append(i)
                    s["ids"].append(i)
                    if s["part"]:
                        modulation(3 if len(first) > 32 else 1 if s["part"] == "open" else min(3, len(first)))
                    chunks += 1
                    due += 0 if chunks < 72 else 0.5 if chunks < 136 else 0.6
                    if bg < len(background) and due >= 1 and chunks >= pause:
                        due -= 1
                        add_ada(background[bg]["g"], background[bg]["kt"])
                        bg += 1
                        if bg % NB == 0:
                            pause = chunks + 5
            elif kind == "mem":
                q = s["q"]
                add(dict(kind="mem", n=CH, src=d_mem[:, 4 * q:4 * q + 4, :].rearrange("p b s -> p (b s)"), **s))
        assert bg == len(background)
        ring = list(range(10))
        owner = {}
        for i in range(len(stream)):
            r = next(r for r in ring if r < max_slots(i))
            ring.remove(r)
            ring.append(r)
            slot_of.append(r)
            before.append(owner.get(r))
            owner[r] = i
        pos = {i: n for n, i in enumerate(order)}
        for kind, s in steps:
            if kind == "unit":
                s["ahead"] = [order[min(pos[i] + AHEAD, len(order) - 1)] for i in s["ids"]]
        pump()
        early = x_first()
        while st["split"] < 2 * NB + 2:
            push_split()
            if early:
                fn = early.pop(0)
                if fn:
                    fn()
        for kind, s in steps:
            if kind == "unit":
                run_unit(s)
            elif kind == "call":
                s()
        flush_later()
        wait("sp", [(s_out, count[id(s_out)])])

        block = ctx.enter_context(nc.Block())

        def play(e):
            return lambda eng: [f(eng) for f in prog[e]] and None
        block.tensor(play("pe"))
        block.scalar(play("act"))
        block.vector(play("dve"))
        block.gpsimd(play("pool"))
        block.sync(play("sp"))


def _strips(w, width=256):
    k, n = w.shape
    return np.ascontiguousarray(
        w.reshape(k // 512, 4, 128, n // width, width).transpose(3, 0, 2, 1, 4)).reshape(n // width, k // 512, 128, 4 * width)


def _cols(a):
    return np.asarray(a).reshape(-1, 128).T


def _constants():
    f = np.float32
    c = np.zeros((128, C_END), f)
    c[:, C_ONE:C_ONE + 128] = 1
    i = np.arange(128)
    c[i, C_ID + i] = 1
    c[i % 64, C_DUP + i] = 1
    c[(i % 64) ^ 32, C_SWAP + i] = 1
    c[:, C_U:C_U + 256] = i[:, None] <= np.arange(256)[None, :]
    for d, cc, cs in ((128, C_COS128, C_SIN128), (64, C_COS64, C_SIN64)):
        half = d // 2
        inv = (f(10000.0) ** (-np.arange(half, dtype=f) / f(half))).astype(f)
        ang = (np.arange(S, dtype=f)[None, :] * inv[:, None]).astype(f).astype(np.float64)
        row = i % d
        c[:, cc:cc + S] = np.cos(ang)[row % half]
        c[:, cs:cs + S] = np.sin(ang)[row % half] * np.where(row < half, -1.0, 1.0)[:, None]
    hot = np.zeros((32, 384), f)
    rel = np.arange(128)
    big = 16 + (np.log(np.maximum(rel, 1).astype(f) / f(16)) / f(np.log(8.0)) * f(16)).astype(np.int32)
    bucket = np.where(rel < 16, rel, np.minimum(big, 31))
    hot[bucket, 255 - rel] = 1
    return c, hot


def kernel(**inp):
    import concourse.bacc as _bacc
    from concourse import mybir as _mybir
    from concourse.bass_utils import run_bass_kernel_spmd as _run

    a = {k: np.asarray(x) for k, x in inp.items()}
    heads = np.concatenate([[b, 8 + b] if b < 8 else [8 + b, 16 + b] for b in range(16)])
    qcols = (heads[:, None] * 64 + np.arange(64)[None]).ravel()
    xT = lambda z: np.ascontiguousarray(z[0].T.reshape(NB, 128, S).transpose(1, 0, 2))
    w_in = a["w_in"][0]
    o = {}
    o["x"] = xT(a["x"])
    o["mem"] = xT(a["mem_2"])
    rep = lambda z: np.broadcast_to(np.asarray(z).reshape(1, -1), (128, np.asarray(z).size))
    o["vec"] = np.ascontiguousarray(np.concatenate([
        _cols(a["norm1_g"]), _cols(a["conv_w"]), _cols(a["conv_b"]), _cols(a["lru_ba"]), _cols(a["lru_bx"]),
        _cols(a["lru_lambda"]), _cols(a["norm2_g"]), _cols(a["final_g"]), _cols(a["ln_gain_2"]), _cols(a["ln_bias_2"]),
        _cols(a["c"]), _cols(a["b_ada"]), rep(a["attn_sinks"][0][heads]), rep(a["b_forget_2"])], axis=1))
    o["cst"], o["hot"] = _constants()
    o["relb"] = np.ascontiguousarray(a["rel_bias"])
    o["ada"] = np.ascontiguousarray(a["w_ada"][0].reshape(NB, 128, 12, CH).transpose(2, 0, 1, 3))
    lru = np.stack([a["lru_wa"][0], a["lru_wx"][0]], axis=1)
    o["lru"] = np.ascontiguousarray(lru.reshape(4, 4, 2, 128, 128).transpose(0, 3, 1, 2, 4)).reshape(4, 128, CH)
    order = np.concatenate([np.arange(0, 2048), 4096 + qcols, np.arange(6144, 6656), np.arange(2048, 4096),
                            np.arange(6656, 10752)])
    o["w_in"] = _strips(w_in[:, order])
    o["w_lru_out"] = _strips(a["w_lru_out"][0])
    o["w_attn_out"] = _strips(a["w_attn_out"][0][qcols])
    o["w_out"] = _strips(a["w_out"][0])
    o["w_ff1"] = _strips(a["w_ff1"][0])
    o["w_ff2"] = _strips(a["w_ff2"][0])
    o["w_kv"] = np.concatenate([_strips(a["w_mem_kv_2"][l]) for l in range(2)])
    r = lambda s, n: np.arange(s, s + n)
    main = np.concatenate([r(6150, 1024), r(3078, 768), r(3846, 768), r(7254, 512), r(4614, 768), r(0, 768),
                           r(768, 768), r(1536, 768), r(5382, 768), r(7766, 512), r(2304, 768)])
    small = np.concatenate([r(7174, 64), r(7238, 16), r(3072, 6)])
    o["w_in2"] = np.concatenate([_strips(a["w_in_2"][l][:, main]) for l in range(2)])
    o["w_s2"] = np.concatenate([_strips(a["w_in_2"][l][:, small], 86) for l in range(2)])
    o["w_out2"] = np.concatenate([_strips(a["w_out_2"][l]) for l in range(2)])

    nc = _bacc.Bacc("TRN2", target_bir_lowering=False, num_devices=1)
    arrays, ap = {}, {}
    for name, z in o.items():
        arrays[f"in_{name}"] = z
        ap[name] = nc.dram_tensor(f"in_{name}", z.shape, _mybir.dt.from_np(z.dtype), kind="ExternalInput").ap()
    out = nc.dram_tensor("out_0", (128, NB, S), F32, kind="ExternalOutput").ap()
    d_w = {"in": ap["w_in"], "lru_out": ap["w_lru_out"], "attn_out": ap["w_attn_out"], "out": ap["w_out"],
           "ff1": ap["w_ff1"], "ff2": ap["w_ff2"], "kv": ap["w_kv"], "in2": ap["w_in2"], "out2": ap["w_out2"]}
    build(nc, ap["x"], ap["mem"], ap["vec"], ap["cst"], ap["hot"], ap["relb"], ap["ada"], ap["lru"], d_w, ap["w_s2"], out)
    r_ = _run(nc, [arrays], core_ids=[0])
    got = r_.results[0]["out_0"]
    return np.ascontiguousarray(got.transpose(1, 0, 2).reshape(D, S).T).reshape(1, S, D)
```
